# Optimizing a Trainium2 kernel written in Bass

```python
import math
import jax, jax.numpy as jnp
from jax import lax
import numpy as np

D_MODEL = 1024
BATCH = 1
SEQ = 128
DEPTH = 2
DEC_BATCH = 1
DEC_SEQ = 512
PAST_LEN = 128

GRID_W = 64
ROPE_BASE = 10000.0
Q_BLOCK = 128
EPS = 1e-6
H_A = 6
DN_A = 64
DR_A = 32
DV_A = 64
Q_RANK = 384
KV_RANK = 256
H_B = 4
DH_B = 32
DV_B = 64
H_C = 4
DK_C = 48
DV_C = 96
GATE_RANK = 16
GATE_NORM = 16.0
CHUNK = 64
WIDTH_A = H_A * DV_A
WIDTH_B = H_B * DV_B
WIDTH_C = H_C * DV_C
MIX_WIDTH = WIDTH_A + WIDTH_B + WIDTH_C
D_FF = 2816
N_MOD = 9
PROJ_SPLITS = (Q_RANK, KV_RANK, DR_A, H_B * 2 * DH_B, H_B * 2 * DH_B, H_B * DV_B,
               H_C * DK_C, H_C * DK_C, H_C * DV_C, WIDTH_C, GATE_RANK, GATE_RANK)
PROJ_COLS = sum(PROJ_SPLITS)

kernel_name = "hybrid_diffusion_mla_diff_gla_step"

def rmsnorm(x, g):
    xf = x.astype(jnp.float32)
    y = xf * lax.rsqrt(jnp.mean(xf * xf, axis=-1, keepdims=True) + EPS)
    return (y * g.astype(jnp.float32)).astype(x.dtype)

def modulate_norm(x, g, shift, scale):
    return rmsnorm(x, g) * (1 + scale) + shift

def swiglu(u, w13, w2):
    a, b = jnp.split(u @ w13, 2, axis=-1)
    return (jax.nn.silu(a) * b) @ w2

def grid_positions(n):
    n_rows = n // GRID_W
    rows = jnp.repeat(jnp.arange(n_rows), GRID_W)
    cols = jnp.arange(n_rows * GRID_W) % GRID_W
    return rows, cols

def rope_1d(x, pos):
    d = x.shape[-1]
    inv = ROPE_BASE ** (-jnp.arange(0, d, 2, dtype=jnp.float32) / d)
    ang = pos.astype(jnp.float32)[:, None] * inv
    shape = (ang.shape[0],) + (1,) * (x.ndim - 3) + (d // 2,)
    cos = jnp.cos(ang).reshape(shape).astype(x.dtype)
    sin = jnp.sin(ang).reshape(shape).astype(x.dtype)
    x1, x2 = x[..., : d // 2], x[..., d // 2:]
    return jnp.concatenate([x1 * cos - x2 * sin, x1 * sin + x2 * cos], axis=-1)

def axial_rope(x):
    rows, cols = grid_positions(x.shape[1])
    h = x.shape[-1] // 2
    return jnp.concatenate([rope_1d(x[..., :h], rows), rope_1d(x[..., h:], cols)], axis=-1)

def query_blocks(fn, qs):
    b, nq = qs[0].shape[:2]
    nb = nq // Q_BLOCK
    qb = tuple(a.reshape((b, nb, Q_BLOCK) + a.shape[2:]).swapaxes(0, 1) for a in qs)
    out = lax.map(lambda t: fn(*t), qb)
    return out.swapaxes(0, 1).reshape((b, nq) + out.shape[3:])

def mla_attend(q_nope, q_rope, ckv, krope, lp):
    k_nope = jnp.einsum("bkr,rhd->bkhd", ckv, lp["mla_w_uk"].reshape(KV_RANK, H_A, DN_A))
    v = jnp.einsum("bkr,rhd->bkhd", ckv, lp["mla_w_uv"].reshape(KV_RANK, H_A, DV_A))
    scale = (DN_A + DR_A) ** -0.5

    def blk(qn, qr):
        s = jnp.einsum("bqhd,bkhd->bhqk", qn, k_nope) + jnp.einsum("bqhd,bkd->bhqk", qr, krope)
        p = jax.nn.softmax(s.astype(jnp.float32) * scale, axis=-1).astype(v.dtype)
        return jnp.einsum("bhqk,bkhd->bqhd", p, v)

    return query_blocks(blk, (q_nope, q_rope))

def diff_attend(q, k, v, lp, lam_init):
    lam = (jnp.exp(jnp.sum(lp["diff_lq1"].astype(jnp.float32) * lp["diff_lk1"].astype(jnp.float32)))
           - jnp.exp(jnp.sum(lp["diff_lq2"].astype(jnp.float32) * lp["diff_lk2"].astype(jnp.float32)))
           + lam_init)
    scale = DH_B ** -0.5

    def blk(qb):
        s = jnp.einsum("bqhjd,bkhjd->bhjqk", qb, k).astype(jnp.float32) * scale
        p = jax.nn.softmax(s, axis=-1)
        a = p[:, :, 0] - lam * p[:, :, 1]
        return jnp.einsum("bhqk,bkhd->bqhd", a.astype(v.dtype), v)

    return query_blocks(blk, (q,))

def gla_chunk_scan(q, k, v, g, s0):
    b_, n, h, _ = q.shape
    nc = n // CHUNK

    def chunks(a):
        return a.reshape(b_, nc, CHUNK, h, a.shape[-1]).transpose(1, 0, 3, 2, 4).astype(jnp.float32)

    qc, kc, vc, gc = chunks(q), chunks(k), chunks(v), chunks(g)
    bcum = jnp.cumsum(gc, axis=-2)
    blast = bcum[..., -1:, :]
    qe = qc * jnp.exp(bcum)
    ke = kc * jnp.exp(-bcum)
    kd = kc * jnp.exp(blast - bcum)
    mask = jnp.tril(jnp.ones((CHUNK, CHUNK), jnp.float32))
    attn = jnp.einsum("nbhtd,nbhsd->nbhts", qe, ke) * mask
    intra = jnp.einsum("nbhts,nbhsv->nbhtv", attn, vc)
    upd = jnp.einsum("nbhsd,nbhsv->nbhdv", kd, vc)
    decay = jnp.exp(blast[..., 0, :])

    def step(s, inp):
        dec, u = inp
        return dec[..., None] * s + u, s

    s_fin, s_in = lax.scan(step, s0.astype(jnp.float32), (decay, upd))
    o = intra + jnp.einsum("nbhtd,nbhdv->nbhtv", qe, s_in)
    o = o.transpose(1, 0, 3, 2, 4).reshape(b_, n, h, v.shape[-1])
    return o.astype(v.dtype), s_fin.astype(q.dtype)

def gla_bidir(q, k, v, g_f, g_b, s_f0, s_b0):
    o_f, s_f = gla_chunk_scan(q, k, v, g_f, s_f0)
    flip = lambda a: a[:, ::-1]
    o_b, s_b = gla_chunk_scan(flip(q), flip(k), flip(v), flip(g_b), s_b0)
    return o_f + flip(o_b), s_f, s_b

def project(u, lp):
    b_, n, _ = u.shape
    offs = np.cumsum(PROJ_SPLITS)[:-1].tolist()
    (cq, ckv, krope, qb, kb, vb, qc, kc, vc, rc, glf, glb) = jnp.split(u @ lp["w_in"], offs, axis=-1)
    q_a = (rmsnorm(cq, lp["mla_q_norm"]) @ lp["mla_w_uq"]).reshape(b_, n, H_A, DN_A + DR_A)
    g_f = jax.nn.log_sigmoid((glf @ lp["gla_wg_f"] + lp["gla_bg_f"]).astype(jnp.float32)) / GATE_NORM
    g_b = jax.nn.log_sigmoid((glb @ lp["gla_wg_b"] + lp["gla_bg_b"]).astype(jnp.float32)) / GATE_NORM
    return {
        "q_nope": q_a[..., :DN_A], "q_rope": q_a[..., DN_A:],
        "ckv": rmsnorm(ckv, lp["mla_kv_norm"]), "krope": krope,
        "q_b": qb.reshape(b_, n, H_B, 2, DH_B), "k_b": kb.reshape(b_, n, H_B, 2, DH_B),
        "v_b": vb.reshape(b_, n, H_B, DV_B),
        "q_c": qc.reshape(b_, n, H_C, DK_C) * (DK_C ** -0.5), "k_c": kc.reshape(b_, n, H_C, DK_C),
        "v_c": vc.reshape(b_, n, H_C, DV_C), "r_c": rc,
        "g_f": g_f.reshape(b_, n, H_C, DK_C), "g_b": g_b.reshape(b_, n, H_C, DK_C),
    }

def merge_groups(o_a, o_b, o_c, r_c, lp, lam_init):
    b_, n = o_a.shape[:2]
    o_a = rmsnorm(o_a.reshape(b_, n, WIDTH_A), lp["mla_out_norm"])
    o_b = (rmsnorm(o_b, lp["diff_norm"]) * (1.0 - lam_init)).reshape(b_, n, WIDTH_B)
    o_c = rmsnorm(o_c, lp["gla_norm"]).reshape(b_, n, WIDTH_C) * jax.nn.silu(r_c)
    return jnp.concatenate([o_a, o_b, o_c], axis=-1) @ lp["w_out"]

def context_mixer(u, lp, lam_init):
    p = project(u, lp)
    b_, n = u.shape[:2]
    o_a = mla_attend(p["q_nope"], p["q_rope"], p["ckv"], p["krope"], lp)
    o_b = diff_attend(p["q_b"], p["k_b"], p["v_b"], lp, lam_init)
    zeros = jnp.zeros((b_, H_C, DK_C, DV_C), u.dtype)
    o_c, s_f, s_b = gla_bidir(p["q_c"], p["k_c"], p["v_c"], p["g_f"], p["g_b"], zeros, zeros)
    out = merge_groups(o_a, o_b, o_c, p["r_c"], lp, lam_init)
    ctx = (p["ckv"], p["krope"], p["k_b"].reshape(b_, n, H_B, 2 * DH_B), p["v_b"], s_f, s_b)
    return out, ctx

def latent_mixer(u, lp, lam_init, ctx):
    ckv_c, krope_c, kb_c, vb_c, sf_c, sb_c = ctx
    p = project(u, lp)
    q_rope = axial_rope(p["q_rope"])
    krope = axial_rope(p["krope"][:, :, None, :])[:, :, 0]
    o_a = mla_attend(p["q_nope"], q_rope, jnp.concatenate([ckv_c, p["ckv"]], axis=1),
                     jnp.concatenate([krope_c, krope], axis=1), lp)
    k_all = jnp.concatenate([kb_c.reshape(kb_c.shape[:3] + (2, DH_B)), axial_rope(p["k_b"])], axis=1)
    v_all = jnp.concatenate([vb_c, p["v_b"]], axis=1)
    o_b = diff_attend(axial_rope(p["q_b"]), k_all, v_all, lp, lam_init)
    o_c, _, _ = gla_bidir(p["q_c"], p["k_c"], p["v_c"], p["g_f"], p["g_b"], sf_c, sb_c)
    return merge_groups(o_a, o_b, o_c, p["r_c"], lp, lam_init), None

def trunk_layer(x, mod, lp, mixer_fn):
    sh1, sc1, g1, sh2, sc2, g2, sh3, sc3, g3 = jnp.split(mod, N_MOD, axis=-1)
    x = x + 0.5 * g1 * swiglu(modulate_norm(x, lp["norm_ffn1"], sh1, sc1), lp["ffn1_w13"], lp["ffn1_w2"])
    mixed, aux = mixer_fn(modulate_norm(x, lp["norm_mix"], sh2, sc2))
    x = x + g2 * mixed
    x = x + 0.5 * g3 * swiglu(modulate_norm(x, lp["norm_ffn2"], sh3, sc3), lp["ffn2_w13"], lp["ffn2_w2"])
    return x, aux

def setup_inputs(seed: int = 0) -> dict:
    key = jax.random.key(seed)
    ks = iter(jax.random.split(key, 48))

    def nrm(shape, scale):
        return jax.random.normal(next(ks), shape, jnp.float32) * scale

    def gain(shape):
        return 1.0 + nrm(shape, 0.05)

    L, D = DEPTH, D_MODEL
    return {
        "x_prompt": nrm((BATCH, SEQ, D), 1.0),
        "x_sample": nrm((DEC_BATCH, DEC_SEQ, D), 1.0),
        "cache_mla_ckv": nrm((DEC_BATCH, L, PAST_LEN, KV_RANK), 1.0),
        "cache_mla_krope": nrm((DEC_BATCH, L, PAST_LEN, DR_A), 1.0),
        "cache_diff_k": nrm((DEC_BATCH, L, PAST_LEN, H_B, 2 * DH_B), 1.0),
        "cache_diff_v": nrm((DEC_BATCH, L, PAST_LEN, H_B, DV_B), 1.0),
        "state_gla_fwd": nrm((DEC_BATCH, L, H_C, DK_C, DV_C), 0.5),
        "state_gla_bwd": nrm((DEC_BATCH, L, H_C, DK_C, DV_C), 0.5),
        "c": nrm((DEC_BATCH, D), 1.0),
        "c_ctx": nrm((D,), 1.0),
        "w_mod": nrm((L, D, N_MOD * D), 0.5 * D ** -0.5),
        "b_mod": nrm((L, N_MOD * D), 0.02),
        "norm_ffn1": gain((L, D)),
        "ffn1_w13": nrm((L, D, 2 * D_FF), D ** -0.5),
        "ffn1_w2": nrm((L, D_FF, D), D_FF ** -0.5),
        "norm_mix": gain((L, D)),
        "w_in": nrm((L, D, PROJ_COLS), D ** -0.5),
        "mla_q_norm": gain((L, Q_RANK)),
        "mla_w_uq": nrm((L, Q_RANK, H_A * (DN_A + DR_A)), Q_RANK ** -0.5),
        "mla_kv_norm": gain((L, KV_RANK)),
        "mla_w_uk": nrm((L, KV_RANK, H_A * DN_A), KV_RANK ** -0.5),
        "mla_w_uv": nrm((L, KV_RANK, H_A * DV_A), KV_RANK ** -0.5),
        "mla_out_norm": gain((L, WIDTH_A)),
        "diff_lq1": nrm((L, DH_B), 0.1),
        "diff_lk1": nrm((L, DH_B), 0.1),
        "diff_lq2": nrm((L, DH_B), 0.1),
        "diff_lk2": nrm((L, DH_B), 0.1),
        "diff_norm": gain((L, DV_B)),
        "gla_wg_f": nrm((L, GATE_RANK, H_C * DK_C), GATE_RANK ** -0.5),
        "gla_bg_f": nrm((L, H_C * DK_C), 0.1),
        "gla_wg_b": nrm((L, GATE_RANK, H_C * DK_C), GATE_RANK ** -0.5),
        "gla_bg_b": nrm((L, H_C * DK_C), 0.1),
        "gla_norm": gain((L, DV_C)),
        "w_out": nrm((L, MIX_WIDTH, D), MIX_WIDTH ** -0.5),
        "norm_ffn2": gain((L, D)),
        "ffn2_w13": nrm((L, D, 2 * D_FF), D ** -0.5),
        "ffn2_w2": nrm((L, D_FF, D), D_FF ** -0.5),
        "final_norm": gain((D,)),
    }

def reference(x_prompt, x_sample, cache_mla_ckv, cache_mla_krope, cache_diff_k, cache_diff_v,
              state_gla_fwd, state_gla_bwd, c, c_ctx, w_mod, b_mod, norm_ffn1, ffn1_w13, ffn1_w2,
              norm_mix, w_in, mla_q_norm, mla_w_uq, mla_kv_norm, mla_w_uk, mla_w_uv, mla_out_norm,
              diff_lq1, diff_lk1, diff_lq2, diff_lk2, diff_norm, gla_wg_f, gla_bg_f, gla_wg_b, gla_bg_b,
              gla_norm, w_out, norm_ffn2, ffn2_w13, ffn2_w2, final_norm):
    xp, xs = x_prompt, x_sample
    new_ckv, new_krope, new_dk, new_dv, new_sf, new_sb = [], [], [], [], [], []
    for l in range(DEPTH):
        lp = {
            "norm_ffn1": norm_ffn1[l], "ffn1_w13": ffn1_w13[l], "ffn1_w2": ffn1_w2[l],
            "norm_mix": norm_mix[l], "w_in": w_in[l],
            "mla_q_norm": mla_q_norm[l], "mla_w_uq": mla_w_uq[l], "mla_kv_norm": mla_kv_norm[l],
            "mla_w_uk": mla_w_uk[l], "mla_w_uv": mla_w_uv[l], "mla_out_norm": mla_out_norm[l],
            "diff_lq1": diff_lq1[l], "diff_lk1": diff_lk1[l], "diff_lq2": diff_lq2[l],
            "diff_lk2": diff_lk2[l], "diff_norm": diff_norm[l],
            "gla_wg_f": gla_wg_f[l], "gla_bg_f": gla_bg_f[l], "gla_wg_b": gla_wg_b[l],
            "gla_bg_b": gla_bg_b[l], "gla_norm": gla_norm[l], "w_out": w_out[l],
            "norm_ffn2": norm_ffn2[l], "ffn2_w13": ffn2_w13[l], "ffn2_w2": ffn2_w2[l],
        }
        lam_init = 0.8 - 0.6 * math.exp(-0.3 * l)
        mod_ctx = (jax.nn.silu(c_ctx) @ w_mod[l] + b_mod[l])[None, None, :]
        mod_lat = (jax.nn.silu(c) @ w_mod[l] + b_mod[l])[:, None, :]
        xp, ctx_t = trunk_layer(xp, mod_ctx, lp, lambda u: context_mixer(u, lp, lam_init))
        new_ckv.append(ctx_t[0]); new_krope.append(ctx_t[1]); new_dk.append(ctx_t[2])
        new_dv.append(ctx_t[3]); new_sf.append(ctx_t[4]); new_sb.append(ctx_t[5])
        cached = (cache_mla_ckv[:, l], cache_mla_krope[:, l], cache_diff_k[:, l], cache_diff_v[:, l],
                  state_gla_fwd[:, l], state_gla_bwd[:, l])
        xs, _ = trunk_layer(xs, mod_lat, lp, lambda u: latent_mixer(u, lp, lam_init, cached))
    y_prompt = rmsnorm(xp, final_norm)
    y_sample = rmsnorm(xs, final_norm)
    return (y_prompt, y_sample, jnp.stack(new_ckv, axis=1), jnp.stack(new_krope, axis=1),
            jnp.stack(new_dk, axis=1), jnp.stack(new_dv, axis=1), jnp.stack(new_sf, axis=1),
            jnp.stack(new_sb, axis=1))


_drawn_inputs = setup_inputs


def setup_inputs(seed=0):
    import zlib

    import numpy as np

    out = dict(_drawn_inputs(seed))
    spreads = {}
    factors = {'cache_mla_krope': 3.463,
     'state_gla_fwd': 8.0,
     'state_gla_bwd': 8.0,
     'norm_ffn1': 5.444,
     'mla_q_norm': 8.0,
     'mla_out_norm': 13.417,
     'diff_lq1': 8.0,
     'diff_lk1': 7.248,
     'diff_lq2': 7.116,
     'diff_lk2': 8.0,
     'diff_norm': 21.479,
     'gla_norm': 18.897,
     'norm_ffn2': 5.814}
    for name, (base, spread) in spreads.items():
        noise = np.random.default_rng([zlib.crc32(name.encode()), seed]).standard_normal(out[name].shape)
        drawn = base * np.exp(spread * noise) if base else spread * noise
        out[name] = __import__('jax').numpy.asarray(drawn.astype(out[name].dtype))
    for name, factor in factors.items():
        out[name] = (out[name] * factor).astype(out[name].dtype)
    return out
```

```python
import math
from contextlib import ExitStack

import concourse.bass as bass
import numpy as np
from concourse import mybir

F32 = mybir.dt.float32
F32R = mybir.dt.float32r
ACT = mybir.ActivationFunctionType
ALU = mybir.AluOpType
AX = mybir.AxisListType

P = 128
D = 1024
KD = D // P
DEPTH = 2
TC, TL, PAST = 128, 512, 128
T = TC + TL
NT = T // P
TH = T // 2
NKEY = TC + PAST + TL
NKT = NKEY // P
GRID_W = 64
EPS = 1e-6
H_A, DN, DR, DV_A = 6, 64, 32, 64
DQ = DN + DR
Q_RANK, KV_RANK = 384, 256
H_B, DH_B, DV_B = 4, 32, 64
H_C, DK, DV_C = 4, 48, 96
GR = 16
GATE_NORM = 16.0
CH = 64
NCH = T // CH
HW = 64
WA, WB, WC = H_A * DV_A, H_B * DV_B, H_C * DV_C
F = 2816
NF = F // P
PARTS = [8, 8, 6]
NMOD = 9
NMT = NMOD * KD
CW = 256
MW = 512
NMC = NMOD * D // MW
NW2 = D // CW
O_CQ, O_QB, O_KB, O_VB = 0, 672, 928, 1184
O_QC, O_KC, O_VR, O_GL = 1440, 1632, 1824, 2592
PROJ = ["gl", "kb", "qc", "kc", "vr0", "vr1", "vr2", "vb", "c0", "c1", "c2", "qb"]
G_FFN1 = 0
N_FFN = sum(PARTS) + NW2 * len(PARTS)
G_PROJ = G_FFN1 + N_FFN
G_WOUT = G_PROJ + len(PROJ)
G_FFN2 = G_WOUT + NW2
N_CHUNK = G_FFN2 + N_FFN
R_BMOD, R_N1, R_NM, R_N2, R_FIN, R_QN, R_OG, R_BG, NPAR = 0, 72, 80, 88, 96, 104, 107, 115, 119


def chunk_dmas(g):
    if G_PROJ <= g < G_WOUT and PROJ[g - G_PROJ] in ("qc", "kc"):
        return H_C
    return 2


def raw_need(g):
    return 16 * sum(chunk_dmas(x) for x in range(g % 2, g + 1, 2))


def build(nc, A, O):
    ctx = ExitStack()
    with ctx:
        names = {}

        def sb(name, shape, offset, dtype=F32):
            return nc.alloc_sbuf_tensor_at(name, shape, dtype, offset=offset)

        def sem(name):
            return ctx.enter_context(nc.semaphore(name))

        XB = 16512
        UB = XB + KD * T * 4
        RB = UB + 2 * KD * T * 4
        DG = RB + 6 * KD * CW * 4
        CB = DG + 81920
        xT = sb("xT", [P, KD, T], XB)
        u_hi = sb("u_hi", [P, KD, T], UB, F32R)
        u_lo = sb("u_lo", [P, KD, T], UB + KD * T * 4, F32R)
        raw = sb("raw", [P, 2, KD * CW], RB)
        w_hi = sb("w_hi", [P, 2, KD * CW], RB + 2 * KD * CW * 4, F32R)
        w_lo = sb("w_lo", [P, 2, KD * CW], RB + 4 * KD * CW * 4, F32R)
        h_hi = sb("h_hi", [P, 8, T], DG, F32R)
        h_lo = sb("h_lo", [P, 8, T], DG + 20480, F32R)
        G0 = DG + 40960
        silu_a = sb("silu_a", [P, 2, T], G0)
        h32 = sb("h32", [P, 2, T], G0 + 5120)
        sq = sb("sq", [P, 2, T], G0 + 10240)
        sqsum = sb("sqsum", [P, T], G0 + 15360)
        rstd = sb("rstd", [P, T], G0 + 17920)
        xn = sb("xn", [P, 2, T], G0 + 20480)
        u32 = sb("u32", [P, 2, T], G0 + 25600)
        stdv = sb("stdv", [P, T], G0 + 30720)
        mraw = sb("mraw", [P, 3, KD, MW], DG)
        mrows = sb("mrows", [P, 2, MW], DG + 49152)
        xs = sb("xs", [P, NT, D], UB)
        yT = sb("yT", [P, KD, T], UB)
        ytm = sb("ytm", [P, 2, D], DG)
        omix = sb("omix", [P, NT, D], DG)
        qcT = sb("qcT", [P, 2, T], DG + 20480)
        kcT = sb("kcT", [P, 2, T], DG + 25600)
        glT = sb("glT", [2 * GR, T], DG + 30720)
        vcs = sb("vcs", [P, NT, WC], DG + 33280)
        rcs = sb("rcs", [P, NT, WC], DG + 40960)
        cqkv = sb("cqkv", [P, NT, 672], DG + 48640)
        qbT = sb("qbT", [P, 2, T], DG + 62080)
        kbT = sb("kbT", [P, 2, NKEY], DG + 67200)
        vbs = sb("vbs", [P, NKT, 288], DG + 73344)
        ck = sb("ck", [P, 256], DG + 80256)
        rotb = sb("rotb", [P, 2, TL], DG)
        csq = sb("csq", [P, NT, 640], DG + 4096)
        gab = sb("gab", [P, 2, T], UB)
        gb = sb("gb", [P, 2, T], UB + 5120)
        gcum = sb("gcum", [P, 2, T], UB + 10240)
        gqe = sb("gqe", [P, 2, T], UB + 15360)
        gke = sb("gke", [P, 2, T], UB + 20480)
        gkd = gab
        am = sb("am", [P, 2, 512], UB + 5120)
        kdt = sb("kdt", [P, NT, 2, P], UB + 25600)
        S = sb("S", [P, NCH, 2, DV_C], UB + 30720)
        Sfin = sb("Sfin", [P, 2, DV_C], UB + 38400)
        gtot = sb("gtot", [P, 2, NCH], UB + 39168)
        osq = sb("osq", [P, NT, WC], UB)
        qm = [[sb(f"qm{s}{j}", [P, T], UB + o) for j, o in enumerate(os)] for s, os in enumerate([(13824, 16384), (20480, 23040)])]
        p0 = [sb(f"p0_{s}", [P, T], UB + 25600 + 2560 * s) for s in range(2)]
        p1 = [sb(f"p1_{s}", [P, T], UB + 30720 + 2560 * s) for s in range(2)]
        pt = [sb(f"pt_{s}", [P, NT, P], UB + 35840 + 2560 * s) for s in range(2)]
        cqT = sb("cqT", [P, 3, T], UB)
        ckvT = sb("ckvT", [P, 2, NKEY], UB + 7680)
        kA = [sb(f"kA{s}", [P, NKEY], UB + 13824 + 3072 * s) for s in range(2)]
        qA = [sb(f"qA{s}", [P, T], UB + 20480 + 2560 * s) for s in range(2)]
        rota = sb("rota", [P, TL], UB + 30720)
        wuq = sb("wuq", [P, 3, H_A * DQ], DG + 20480)
        wuk = sb("wuk", [P, 2, H_A * DN], DG + 27392)
        wuv = sb("wuv", [P, 2, WA], DG + 30464)
        vas = sb("vas", [P, NKT, 416], DG + 33536)
        krT = sb("krT", [DR, NKEY], DG + 43520)
        cc = sb("cc", [P, KV_RANK], DG + 46592)
        cck = sb("cck", [P, DR], DG + 47616)
        asq = sb("asq", [P, NT, WA], UB)
        off = [CB]

        def small(name, shape, dtype=F32):
            n = 4
            for s in shape[1:]:
                n *= s
            t = sb(name, shape, off[0], dtype)
            off[0] += (n + 31) // 32 * 32
            return t

        cosT, sinT = small("cosT", [P, TL]), small("sinT", [P, TL])
        ident, ones = small("ident", [P, P]), small("ones", [P, P])
        mask = small("mask", [P, 2, P])
        keep = small("keep", [P, 2, T])
        csp = small("csp", [P, KD, 32])
        comb = small("comb", [P, 2])
        modT = small("modT", [P, NMT, 2])
        gains = small("gains", [P, 3, KD, 2])
        gates = small("gates", [P, 3, KD, 2])
        par = small("par", [P, P])
        parT = small("parT", [P, P])
        grp = small("grp", [P, 4])
        lqk = small("lqk", [P, 4, DH_B])
        wgp = small("wgp", [2 * GR, 2, H_C * HW])
        Sini = small("Sini", [P, 2, 2, DV_C])
        kvw = small("kvw", [P, KV_RANK])
        st = small("st", [P, 96])
        assert off[0] <= 229368, off[0]
        eps = st[:, 0:1]
        lam2, lexp, nlam = st[:, 1:3], st[:, 3:5], st[:, 5:6]
        lcon = st[:, 6:8]
        ldif = st[:, 8:9]
        css, crs = st[:, 10:30], st[:, 30:50]
        ss10, rs10 = st[:, 50:60], st[:, 60:70]
        amax, aneg, asum, arec = st[:, 70:74], st[:, 74:78], st[:, 78:82], st[:, 82:86]
        ps = ctx.enter_context(nc.psum_tensor("ps", [P, 8, 512], F32))
        psf = ps[:, :, :].rearrange("p b n -> p (b n)")

        s_const = sem("s_const")
        s_tab = sem("s_tab")
        s_xs = sem("s_xs")
        s_ctp = sem("s_ctp")
        s_csil = sem("s_csil")
        s_xtp = sem("s_xtp")
        s_xa = sem("s_xa")
        s_xv = sem("s_xv")
        s_go = sem("s_go")
        s_yt = sem("s_yt")
        s_ytp = sem("s_ytp")
        s_ytm = sem("s_ytm")
        s_yout = [sem("s_yout0"), sem("s_yout1")]
        f_sq, f_sqd, f_sum, f_ss, f_std, f_xn = (sem("f_" + n) for n in ("sq", "sqd", "sum", "ss", "std", "xn"))
        par_in = sem("par_in")
        kv_in = sem("kv_in")
        aw_in = sem("aw_in")
        out_in = sem("out_in")
        layer_sems = []

        def lsem(name):
            s = sem(name)
            layer_sems.append(s)
            return s

        l_done = lsem("l_done")
        par_tp = lsem("par_tp")
        par_ok = lsem("par_ok")
        lam_s = lsem("lam_s")
        lam_e = lsem("lam_e")
        m_raw = [lsem(f"m_raw{i}") for i in range(3)]
        m_mm, m_row, m_tp, m_ev = lsem("m_mm"), lsem("m_row"), lsem("m_tp"), lsem("m_ev")
        mod_ok = lsem("mod_ok")
        raw_in = [lsem("raw_in0"), lsem("raw_in1")]
        hi_ok, lo_ok = lsem("hi_ok"), lsem("lo_ok")
        mm_ok = lsem("mm_ok")
        ev_ok = lsem("ev_ok")
        sil_ok, h32_ok, hhi_ok, hlo_ok = lsem("sil_ok"), lsem("h32_ok"), lsem("hhi_ok"), lsem("hlo_ok")
        x_upd = lsem("x_upd")
        n_sq, n_sqd, n_sum, n_ss, n_std = (lsem("n_" + n) for n in ("sq", "sqd", "sum", "ss", "std"))
        n_xn, n_u32, n_uhi, n_ulo = (lsem("n_" + n) for n in ("xn", "u32", "uhi", "ulo"))
        dve_c = lsem("dve_c")
        act_c = lsem("act_c")
        pool_c = lsem("pool_c")
        bk_tp, bk_ev = lsem("bk_tp"), lsem("bk_ev")
        rb_ok = lsem("rb_ok")
        cq_ss, cq_sd, cq_ok = lsem("cq_ss"), lsem("cq_sd"), lsem("cq_ok")
        g_z, g_abs, g_min, g_ln, g_cum = (lsem("g_" + n) for n in ("z", "abs", "min", "ln", "cum"))
        g_e1, g_e2, g_bl, g_e3, g_qe, g_ke, g_kd = (lsem("g_" + n) for n in ("e1", "e2", "bl", "e3", "qe", "ke", "kd"))
        g_tp, g_tev, g_u, g_s = (lsem("g_" + n) for n in ("tp", "tev", "u", "s"))
        g_at, g_am, g_o, g_oev = (lsem("g_" + n) for n in ("at", "am", "o", "oev"))
        g_fin = lsem("g_fin")
        gn_v, gn_s, gn_ok = lsem("gn_v"), lsem("gn_s"), lsem("gn_ok")
        b_qm, b_sc, b_neg, b_exp, b_a, b_tp, b_pt, b_pv, b_o = (lsem("b_" + n) for n in ("qm", "sc", "neg", "exp", "a", "tp", "pt", "pv", "o"))
        ap_tp, ap_ev, ap_kr = lsem("ap_tp"), lsem("ap_ev"), lsem("ap_kr")
        x_mm, x_ev, a_qk = lsem("x_mm"), lsem("x_ev"), lsem("a_qk")
        a_sc, a_neg, a_exp, a_tp, a_pt, a_pv, a_o = (lsem("a_" + n) for n in ("sc", "neg", "exp", "tp", "pt", "pv", "o"))
        on_v, on_s, on_ok = lsem("on_v"), lsem("on_s"), lsem("on_ok")
        ot_tp, ot_hi, ot_lo = lsem("ot_tp"), lsem("ot_hi"), lsem("ot_lo")
        lo_n, hi_n = min(s.num for s in layer_sems), max(s.num for s in layer_sems)
        assert hi_n - lo_n + 1 == len(layer_sems)

        RANGES = [(0, 0, 0, 0, TC), (1, 0, TC, TC, TH - TC), (1, 1, 0, TH, TH)]
        U_ORDER = [[0, 1, 2, 3, 4, 5, 6, 7, 8], [1, 0, 9, 8, 7, 6, 5, 4, 3]]
        O_ORDER = [[0, 1, 2, 3, 4], [0, 4, 3, 2, 1]]
        N_STATE = len(U_ORDER[0])

        def state_count(d, c):
            if d == 0:
                return {0: 0, 2: 0}.get(c, c)
            return {1: 0, 9: 0, 0: 1}.get(c, 11 - c)

        def has_state(d, c):
            return c != (0, 1)[d]

        def entering(d, c):
            return Sini[:, d] if c == (2, 9)[d] else S[:, c]

        def heads_out(t):
            return omix[:, t, WA + WB:D].rearrange("p (a b v) -> p b a v", b=2, v=DV_C)

        def heads_ps():
            return ps[:, 4:6, 0:2 * DV_C].rearrange("p b (a v) -> p b a v", a=2)

        def keys_of(qi):
            return (0, 1) if qi == 0 else (1, NKT)

        cv = lambda ap: ap.bitcast(F32)

        block = ctx.enter_context(nc.Block())

        @block.sync
        def _(sp):
            sp.dma_start(cosT[:, :], A["rope_cos"]).then_inc(s_tab, 16)
            sp.dma_start(sinT[:, :], A["rope_sin"]).then_inc(s_tab, 16)
            sp.dma_start(par[0:KD, :], A["c_ctx"].rearrange("(k p) -> k p", p=P)).then_inc(s_tab, 16)
            sp.dma_start(par[KD:2 * KD, :], A["c"].rearrange("b (k p) -> (b k) p", p=P)).then_inc(s_tab, 16)
            sp.dma_start(xs[:, 0, :], A["x_prompt"][0]).then_inc(s_xs, 16)
            sp.dma_start(xs[:, 1:NT, :], A["x_sample"][0].rearrange("(t p) d -> p t d", p=P)).then_inc(s_xs, 16)
            sp.wait_ge(s_xa, KD // 2)
            sp.wait_ge(s_xv, KD // 2)

            with sp.Fori(0, DEPTH) as l:
                def slot(g):
                    return raw[:, g % 2, :].rearrange("p (k n) -> p k n", k=KD)

                def halves(dst, src, g):
                    n = dst.shape[1] // 2
                    for k in range(2):
                        sp.dma_start(dst[:, k * n:(k + 1) * n, :], src[:, k * n:(k + 1) * n, :]).then_inc(raw_in[g % 2], 16)

                def free(g, step=0):
                    if g >= 2:
                        sp.wait_ge(lo_ok, g - 1 + step)

                def load_up(w13, g, i, j, f0):
                    src = w13[l].rearrange("(k p) n -> p k n", p=P)
                    for s in range(2):
                        sp.dma_start(slot(g)[:, :, s * P:(s + 1) * P], src[:, :, bass.ds(i * 256 + (j * P + f0 + s * F), P)]).then_inc(raw_in[g % 2], 16)

                def load_down(w2, g, i, j, r0, n):
                    halves(slot(g)[:, 0:n, :], w2[l][r0:r0 + n * P, bass.ds(i * 512 + j * CW, CW)].rearrange("(k p) n -> p k n", p=P), g)

                def load_ffn(w13, w2, g, first):
                    for q, n in enumerate(PARTS):
                        f0 = sum(PARTS[:q]) * P
                        start = 0
                        if q == 0 and first:
                            load_up(w13, g, 0, 0, f0)
                            load_up(w13, g + 1, 0, 1, f0)
                            start = 1
                        with sp.Fori(start, n // 2) as i:
                            for j in range(2):
                                free(g + 2 + j, i * 2 - 2)
                                load_up(w13, g + j, i, j, f0)
                        g += n
                        with sp.Fori(0, NW2 // 2) as i:
                            for j in range(2):
                                free(g + 2 + j, i * 2 - 2)
                                load_down(w2, g + j, i, j, f0, n)
                        g += NW2

                def load_mod(i, j, wait):
                    if wait:
                        sp.wait_ge(m_mm, i * 3 + (j - 2))
                    src = A["w_mod"][l][:, bass.ds(i * (3 * MW) + j * MW, MW)].rearrange("(k p) n -> p k n", p=P)
                    sp.dma_start(mraw[:, j], src).then_inc(m_raw[j], 16)

                for j in range(3):
                    load_mod(0, j, False)
                with sp.Fori(1, NMC // 3) as i:
                    for j in range(3):
                        load_mod(i, j, True)
                load_ffn(A["ffn1_w13"], A["ffn1_w2"], G_FFN1, True)
                win = A["w_in"][l].rearrange("(k p) n -> p k n", p=P)
                COL = {"vr0": O_VR, "vr1": O_VR + CW, "vr2": O_VR + 2 * CW, "vb": O_VB, "c0": 0, "c1": CW, "c2": 2 * CW,
                       "qb": O_QB, "kb": O_KB}
                for n, name in enumerate(PROJ):
                    g = G_PROJ + n
                    free(g)
                    if name == "gl":
                        halves(slot(g)[:, :, 0:2 * GR], win[:, :, O_GL:O_GL + 2 * GR], g)
                    elif name in ("qc", "kc"):
                        for h in range(H_C):
                            c0 = {"qc": O_QC, "kc": O_KC}[name] + h * DK
                            sp.dma_start(slot(g)[:, :, h * HW:(h + 1) * HW], win[:, :, c0:c0 + HW]).then_inc(raw_in[g % 2], 16)
                    else:
                        halves(slot(g), win[:, :, COL[name]:COL[name] + CW], g)
                wo = A["w_out"][l].rearrange("(k p) n -> p k n", p=P)
                for n in range(NW2):
                    g = G_WOUT + n
                    free(g)
                    halves(slot(g), wo[:, :, n * CW:(n + 1) * CW], g)
                load_ffn(A["ffn2_w13"], A["ffn2_w2"], G_FFN2, False)
                sp.wait_ge(l_done, 4)
                sp.sem_clear(range(lo_n, hi_n + 1))
                sp.sem_inc(s_go, 1)
            for t in range(NT):
                sp.wait_ge(s_ytm, t + 1)
                dst = O["y_prompt"][0] if t == 0 else O["y_sample"][0, (t - 1) * P:t * P, :]
                sp.dma_start(dst, ytm[:, t % 2, :]).then_inc(s_yout[t % 2], 16)
            sp.wait_ge(s_yout[0], 16 * 3)
            sp.wait_ge(s_yout[1], 16 * 2)

        @block.gpsimd
        def _(pool):
            n_const = [0]

            def made(ins):
                n_const[0] += 1
                ins.then_inc(s_const, 1)
                pool.wait_ge(s_const, n_const[0])

            made(pool.memset(ident[:, :], 0.0))
            made(pool.affine_select(out=ident[:, :], in_=ident[:, :], compare_op=ALU.not_equal, fill=1.0, base=0,
                                    pattern=[[-1, P]], channel_multiplier=1))
            made(pool.memset(ones[:, :], 1.0))
            made(pool.memset(mask[:, :, :], 1.0))
            made(pool.affine_select(out=mask[:, 0, :], in_=mask[:, 0, :], compare_op=ALU.is_ge, fill=0.0, base=0,
                                    pattern=[[1, P]], channel_multiplier=-1))
            made(pool.memset(mask[0:CH, 0, CH:P], 0.0))
            made(pool.affine_select(out=mask[:, 1, :], in_=mask[:, 1, :], compare_op=ALU.is_ge, fill=0.0, base=0,
                                    pattern=[[-1, P]], channel_multiplier=1))
            made(pool.memset(mask[CH:P, 1, 0:CH], 0.0))
            made(pool.memset(keep[:, :, :], 1.0))
            kc = keep[:, :, :].rearrange("p d (c t) -> p d c t", t=CH)
            made(pool.memset(kc[:, 0, :, 0:1], 0.0))
            made(pool.memset(kc[:, 1, :, CH - 1:CH], 0.0))
            made(pool.memset(comb[:, :], 0.0))
            for j in range(4):
                made(pool.affine_select(out=comb[:, :], in_=comb[:, :], compare_op=ALU.not_equal, fill=1.0, base=-32 * j,
                                        pattern=[[-1, 2]], channel_multiplier=1))
            made(pool.memset(grp[:, :], 0.0))
            for j in range(4):
                made(pool.memset(grp[32 * j:32 * j + 32, j:j + 1], 1.0))
            made(pool.memset(csp[:, :, :], 0.0))
            made(pool.memset(wgp[:, :, :], 0.0))
            made(pool.memset(Sini[:, :, :, :], 0.0))
            made(pool.memset(st[:, :], 0.0))
            made(pool.memset(eps, EPS))
            pool.wait_ge(s_ctp, 1)
            made(pool.memset(par[:, :], 0.0))

            with pool.Fori(0, DEPTH) as l:
                n_par = [0]

                def pin(dst, src):
                    n_par[0] += 1
                    pool.dma_start(dst, src).then_inc(par_in, 16)

                pin(par[R_BMOD:R_BMOD + NMT, :], A["b_mod"][l].rearrange("(r p) -> r p", p=P))
                pin(par[R_N1:R_N1 + KD, :], A["norm_ffn1"][l].rearrange("(r p) -> r p", p=P))
                pin(par[R_NM:R_NM + KD, :], A["norm_mix"][l].rearrange("(r p) -> r p", p=P))
                pin(par[R_N2:R_N2 + KD, :], A["norm_ffn2"][l].rearrange("(r p) -> r p", p=P))
                pin(par[R_FIN:R_FIN + KD, :], A["final_norm"].rearrange("(r p) -> r p", p=P))
                pin(par[R_QN:R_QN + 3, :], A["mla_q_norm"][l].rearrange("(r p) -> r p", p=P))
                pin(par[R_OG:R_OG + 3, :], A["mla_out_norm"][l].rearrange("(r p) -> r p", p=P))
                dn = A["diff_norm"][l].rearrange("(a n) -> a n", a=1)
                for r in range(2):
                    for c in range(2):
                        pin(par[R_OG + 3 + r:R_OG + 4 + r, c * DV_B:(c + 1) * DV_B], dn)
                gn = A["gla_norm"][l].rearrange("(a n) -> a n", a=1)
                at = 0
                while at < WC:
                    src0 = at % DV_C
                    n = min(DV_C - src0, P - at % P)
                    r = R_OG + 5 + at // P
                    pin(par[r:r + 1, at % P:at % P + n], gn[:, src0:src0 + n])
                    at += n
                for d, name in enumerate(("f", "b")):
                    bg = A["gla_bg_" + name][l].rearrange("(a n) -> a n", a=1)
                    wg = A["gla_wg_" + name][l]
                    for h in range(H_C):
                        n = min(HW, H_C * DK - h * DK)
                        r = R_BG + 2 * d + h // 2
                        pin(par[r:r + 1, (h % 2) * HW:(h % 2) * HW + n], bg[:, h * DK:h * DK + n])
                        pin(wgp[GR * d:GR * d + GR, d, h * HW:h * HW + n], wg[:, h * DK:h * DK + n])
                    s0 = A["state_gla_fwd" if d == 0 else "state_gla_bwd"][0, l].rearrange("(p h) k v -> h k p v", h=2)
                    for hh in range(2):
                        pin(Sini[HW * hh:HW * hh + DK, d, :, :], s0[hh])
                for n, name in enumerate(("diff_lq1", "diff_lk1", "diff_lq2", "diff_lk2")):
                    pin(lqk[:, n, :], A[name][l].rearrange("(a n) -> a n", a=1).broadcast_to([P, DH_B]))
                pin(kvw[:, :], A["mla_kv_norm"][l].rearrange("(a n) -> a n", a=1).broadcast_to([P, KV_RANK]))
                pin(lcon, A["layer_consts"][l])
                names["n_par"] = n_par[0]
                pool.dma_start(ck[:, :], A["cache_diff_k"][0, l].rearrange("t h d -> t (h d)")).then_inc(kv_in, 16)
                pool.wait_ge(n_ulo, 2 * KD)
                pool.dma_start(vbs[:, 1, 0:WB], A["cache_diff_v"][0, l].rearrange("t h d -> t (h d)")).then_inc(kv_in, 16)
                pool.memset(vbs[:, :, WB:288], 0.0).then_inc(pool_c, 1)
                pool.wait_ge(ev_ok, PROJ.index("vb") + 1)
                pool.dma_start(O["new_diff_v"][0, l].rearrange("t h d -> t (h d)"), vbs[:, 0, 0:WB]).then_inc(out_in, 16)
                pool.wait_ge(bk_ev, 2)
                pool.dma_start(O["new_diff_k"][0, l].rearrange("t h d -> t (h d)"), ck[:, :]).then_inc(out_in, 16)
                pool.wait_ge(cq_ok, 1)
                pool.dma_start(O["new_mla_ckv"][0, l], cqkv[:, 0, Q_RANK:Q_RANK + KV_RANK]).then_inc(out_in, 16)
                pool.dma_start(O["new_mla_krope"][0, l], cqkv[:, 0, 640:672]).then_inc(out_in, 16)
                for d in range(2):
                    dst = O["new_gla_fwd" if d == 0 else "new_gla_bwd"][0, l].rearrange("(p h) k v -> h k p v", h=2)
                    pool.wait_ge(g_fin, d + 1)
                    for hh in range(2):
                        pool.dma_start(dst[hh], Sfin[HW * hh:HW * hh + DK, :, :]).then_inc(out_in, 16)
                pool.wait_ge(gn_ok, 1)
                pool.dma_start(wuq[:, :, :], A["mla_w_uq"][l].rearrange("(k p) n -> p k n", p=P)).then_inc(aw_in, 16)
                pool.dma_start(wuk[:, :, :], A["mla_w_uk"][l].rearrange("(k p) n -> p k n", p=P)).then_inc(aw_in, 16)
                pool.dma_start(wuv[:, :, :], A["mla_w_uv"][l].rearrange("(k p) n -> p k n", p=P)).then_inc(aw_in, 16)
                pool.dma_start(cc[:, :], A["cache_mla_ckv"][0, l]).then_inc(aw_in, 16)
                pool.dma_start(cck[:, :], A["cache_mla_krope"][0, l]).then_inc(aw_in, 16)
                pool.memset(vas[:, :, WA:416], 0.0).then_inc(pool_c, 1)
                pool.wait_ge(out_in, (l + 1) * (16 * 8))
                pool.wait_ge(pool_c, 2)
                pool.sem_inc(l_done, 1)
                pool.wait_ge(s_go, l + 1)

        @block.scalar
        def _(act):
            steps = [0]

            def link(ins):
                steps[0] += 1
                ins.then_inc(act_c, 1)
                act.wait_ge(act_c, steps[0])

            def hi(g, step=0):
                act.wait_ge(raw_in[g % 2], raw_need(g) + step * 16)
                if g >= 2:
                    act.wait_ge(mm_ok, g - 1 + step)
                act.activation(w_hi[:, g % 2, :], raw[:, g % 2, :], ACT.Copy).then_inc(hi_ok, 1)

            def norm(n, last_norm=False):
                for m in range(KD):
                    if n > 0:
                        act.wait_ge(x_upd, (0, 24, 32)[n] - KD + m + 1)
                    if m >= 2:
                        act.wait_ge(n_sqd, n * KD + m - 1)
                    act.activation(sq[:, m % 2, :], xT[:, m, :], ACT.Square).then_inc(n_sq, 1)
                act.wait_ge(n_ss, n + 1)
                act.activation(stdv[:, :].rearrange("p (b t) -> p b t", b=2), ps[:, 0:2, 0:TH], ACT.Sqrt,
                               bias=eps, scale=1.0 / D).then_inc(n_std, 1)
                sh = 3 * n * KD
                for m in range(KD + 1):
                    if m < KD:
                        act.wait_ge(n_xn, n * KD + m + 1)
                        if m >= 2:
                            act.wait_ge(n_ulo, n * KD + m - 1)
                        for c, t0, t1 in ((0, 0, TC), (1, TC, T)):
                            act.activation(u32[:, m % 2, t0:t1], xn[:, m % 2, t0:t1], ACT.Identity,
                                           bias=modT[:, sh + m, c:c + 1], scale=gains[:, n, m, c:c + 1]).then_inc(n_u32, 1)
                    if m >= 1:
                        act.wait_ge(n_u32, 2 * (n * KD + m))
                        act.activation(u_hi[:, m - 1, :], u32[:, (m - 1) % 2, :], ACT.Copy).then_inc(n_uhi, 1)

            def ffn(g, up0, last=False):
                for q, n in enumerate(PARTS):
                    with act.Fori(0, n // 2) as i:
                        for j in range(2):
                            k = up0 + j
                            act.wait_ge(mm_ok, g + j + 1 + i * 2)
                            if k >= 2:
                                act.wait_ge(h32_ok, k - 1 + i * 2)
                            else:
                                pass
                            act.activation(silu_a[:, j, :].rearrange("p (b t) -> p b t", b=2),
                                           ps[:, 4 * ((g + j) % 2):4 * ((g + j) % 2) + 2, 0:TH], ACT.Silu).then_inc(sil_ok, 1)
                            act.wait_ge(h32_ok, k + 1 + i * 2)
                            act.activation(h_hi[:, bass.ds(i * 2 + j, 1), :].rearrange("p a t -> p (a t)"), h32[:, j, :],
                                           ACT.Copy).then_inc(hhi_ok, 1)
                            hi(g + j + 2, i * 2)
                    g += n
                    up0 += n
                    stop = last and q == len(PARTS) - 1
                    if stop:
                        for j in range(2):
                            act.wait_ge(mm_ok, g + j + 1)
                            hi(g + j + 2)
                    else:
                        with act.Fori(0, NW2 // 2) as i:
                            for j in range(2):
                                act.wait_ge(mm_ok, g + j + 1 + i * 2)
                                hi(g + j + 2, i * 2)
                    g += NW2

            act.wait_ge(s_ctp, 1)
            act.activation(csp[:, :, 0:2].rearrange("p k c -> p c k"), ps[:, 0, 0:2 * KD].rearrange("p (c k) -> p c k", c=2),
                           ACT.Silu).then_inc(s_csil, 1)
            for m in range(KD):
                if m % 2:
                    continue
                act.wait_ge(s_xtp, m + 1)
                b = 2 * (m % 4)
                act.activation(xT[:, m, :], psf[:, b * 512:b * 512 + T], ACT.Copy).then_inc(s_xa, 1)

            with act.Fori(0, DEPTH) as l:
                steps[0] = 0
                act.wait_ge(lam_s, 1)
                act.activation(lexp, lam2, ACT.Exp).then_inc(lam_e, 1)
                def mod_rows(c, b, first, i=0):
                    act.wait_ge(m_mm, c + 1 + i * 6)
                    if not first:
                        act.wait_ge(m_tp, c - 1 + i * 6)
                    act.activation(mrows[:, b, :], ps[:, b, :], ACT.Copy).then_inc(m_row, 1)

                for c in range(6):
                    mod_rows(c, c % 2, c < 2)
                with act.Fori(1, NMC // 6) as i:
                    for c in range(6):
                        mod_rows(c, c % 2, False, i)
                hi(0)
                hi(1)
                act.wait_ge(mod_ok, 1)
                norm(0)
                ffn(G_FFN1, 0)
                norm(1)
                for n, name in enumerate(PROJ):
                    g = G_PROJ + n
                    b = 4 * (g % 2)
                    act.wait_ge(mm_ok, g + 1)
                    four = ps[:, b:b + 4, 0:TH]
                    tm = psf[:, b * 512:b * 512 + NT * CW].rearrange("p (t n) -> p t n", n=CW)
                    if name == "gl":
                        act.activation(glT[:, :].rearrange("p (b t) -> p b t", b=2), ps[0:2 * GR, b:b + 2, 0:TH], ACT.Copy).then_inc(ev_ok, 1)
                    elif name in ("qc", "kc", "qb"):
                        dst = {"qc": qcT, "kc": kcT, "qb": qbT}[name]
                        act.activation(dst[:, :, :].rearrange("p m (b t) -> p (m b) t", b=2), four, ACT.Copy).then_inc(ev_ok, 1)
                    elif name == "kb":
                        f2 = ps[:, b:b + 4, :].rearrange("p (m b) t -> p m b t", b=2)
                        act.activation(kbT[:, :, 0:TC], f2[:, :, 0, 0:TC], ACT.Copy)
                        act.activation(kbT[:, :, TC + PAST:PAST + TH], f2[:, :, 0, TC:TH], ACT.Copy)
                        act.activation(kbT[:, :, PAST + TH:NKEY], f2[:, :, 1, 0:TH], ACT.Copy).then_inc(ev_ok, 1)
                    elif name == "vr0":
                        act.activation(vcs[:, :, 0:CW], tm, ACT.Copy).then_inc(ev_ok, 1)
                    elif name == "vr1":
                        act.activation(vcs[:, :, CW:WC], tm[:, :, 0:P], ACT.Copy)
                        act.activation(rcs[:, :, 0:P], tm[:, :, P:CW], ACT.Silu).then_inc(ev_ok, 1)
                    elif name == "vr2":
                        act.activation(rcs[:, :, P:WC], tm, ACT.Silu).then_inc(ev_ok, 1)
                    elif name == "vb":
                        act.activation(vbs[:, 0, 0:WB], tm[:, 0, :], ACT.Copy)
                        act.activation(vbs[:, 2:NKT, 0:WB], tm[:, 1:NT, :], ACT.Copy).then_inc(ev_ok, 1)
                    else:
                        c0 = int(name[1]) * CW
                        w = min(CW, 672 - c0)
                        act.activation(cqkv[:, :, c0:c0 + w], tm[:, :, 0:w], ACT.Copy).then_inc(ev_ok, 1)
                    hi(g + 2)
                act.wait_ge(bk_tp, 1)
                act.activation(kbT[:, :, TC:TC + PAST], ps[:, 0, 0:256].rearrange("p (m t) -> p m t", m=2), ACT.Copy).then_inc(bk_ev, 1)
                act.wait_ge(bk_tp, 2)
                act.activation(ck[:, :], ps[:, 1, 0:256], ACT.Copy).then_inc(bk_ev, 1)
                act.wait_ge(ev_ok, len(PROJ))
                act.activation(csq[:, :, :], cqkv[:, :, 0:640], ACT.Square).then_inc(cq_ss, 1)
                act.wait_ge(cq_sd, 1)
                act.activation(rs10[:, 0:NT], ss10[:, 0:NT], ACT.Sqrt, bias=eps, scale=1.0 / Q_RANK)
                act.activation(rs10[:, NT:2 * NT], ss10[:, NT:2 * NT], ACT.Sqrt, bias=eps, scale=1.0 / KV_RANK).then_inc(cq_ss, 1)
                for d in range(2):
                    act.wait_ge(g_min, d + 1)
                    link(act.activation(gab[:, :, :], gb[:, :, :], ACT.Abs))
                    link(act.activation(gab[:, :, :], gab[:, :, :], ACT.Exp, scale=-1.0))
                    act.activation(gab[:, :, :], gab[:, :, :], ACT.Ln, bias=1.0).then_inc(g_ln, 1)
                    act.wait_ge(g_cum, d + 1)
                    act.activation(gqe[:, :, :], gcum[:, :, :], ACT.Exp, scale=1.0 / GATE_NORM).then_inc(g_e1, 1)
                    act.activation(gke[:, :, :], gcum[:, :, :], ACT.Exp, scale=-1.0 / GATE_NORM).then_inc(g_e2, 1)
                    tot = gcum[:, :, :].rearrange("p a (c t) -> p a c t", t=CH)[:, :, :, (CH - 1, 0)[d]]
                    act.activation(gtot[:, :, :], tot, ACT.Exp, scale=1.0 / GATE_NORM)
                    act.wait_ge(g_bl, d + 1)
                    act.activation(gkd[:, :, :], gb[:, :, :], ACT.Exp, scale=1.0 / GATE_NORM).then_inc(g_e3, 1)
                    for t in range(NT):
                        act.wait_ge(g_tp, d * NT + t + 1)
                        act.activation(kdt[:, t, :, :], ps[:, 4 + t % 2, 0:256].rearrange("p (a k) -> p a k", a=2), ACT.Copy).then_inc(g_tev, 1)
                    if d == 0:
                        for n, t in enumerate(O_ORDER[d]):
                            act.wait_ge(g_o, n + 1)
                            act.activation(heads_out(t), heads_ps(), ACT.Copy).then_inc(g_oev, 1)
                act.wait_ge(gn_v, 1)
                act.activation(crs, css, ACT.Sqrt, bias=eps, scale=1.0 / DV_C).then_inc(gn_s, 1)
                SB = DH_B ** -0.5
                NB = H_B * NT

                def scores_view(s, qi):
                    if qi == 0:
                        return ps[:, s, 0:P], lambda tile: tile[:, 0:P]
                    return ps[:, s:s + 2, 0:TH], lambda tile: tile[:, :].rearrange("p (b t) -> p b t", b=2)

                def turn_copy(n, s_tp, s_pv, s_pt):
                    nk = 1 if n % NT == 0 else NT
                    act.wait_ge(s_tp, n + 1)
                    if n >= 2:
                        act.wait_ge(s_pv, n - 1)
                    act.activation(pt[n % 2][:, 0:nk, :].rearrange("p a t -> p (a t)"), psf[:, 4 * 512:4 * 512 + nk * P], ACT.Copy).then_inc(s_pt, 1)

                act.wait_ge(out_in, (l + 1) * (16 * 8))
                for n in range(NB + 1):
                    if n < NB:
                        for j in range(2):
                            act.wait_ge(b_neg, 2 * n + j + 1)
                            if n >= 2 and j == 0:
                                act.wait_ge(b_tp, n - 1)
                            src, view = scores_view(2 * j, n % NT)
                            c = 2 * (n % 2) + j
                            act.activation(view((p0, p1)[j][n % 2]), src, ACT.Exp, bias=aneg[:, c:c + 1], scale=SB,
                                           accum_out=asum[:, c:c + 1]).then_inc(b_exp, 1)
                    if n >= 1:
                        turn_copy(n - 1, b_tp, b_pv, b_pt)
                for s in range(6):
                    act.wait_ge(ap_tp, s + 1)
                    b = 2 * (s % 4) * 512
                    if s < 3:
                        ins = act.activation(cqT[:, s, :], psf[:, b:b + T], ACT.Copy, scale=parT[:, R_QN + s:R_QN + s + 1])
                    elif s < 5:
                        ins = act.activation(ckvT[:, s - 3, :], psf[:, b:b + NKEY], ACT.Copy)
                    else:
                        ins = act.activation(krT[:, :], psf[0:DR, b:b + NKEY], ACT.Copy)
                    ins.then_inc(ap_ev, 1)
                for t in range(NKT):
                    act.wait_ge(ap_tp, 6 + t + 1)
                    act.activation(vas[:, t, 0:WA], ps[:, t, 0:WA], ACT.Copy).then_inc(ap_ev, 1)
                SA = DQ ** -0.5
                NA = H_A * NT

                def head_piece(r):
                    h, k = r // 4, r % 4
                    if h >= 2:
                        act.wait_ge(a_sc, (h - 1) * NT)
                    act.wait_ge(x_mm, r + 1)
                    if k < 2:
                        ins = act.activation(qA[h % 2][0:DQ, k * TH:(k + 1) * TH], ps[0:DQ, 7, 0:TH], ACT.Copy)
                    else:
                        c0 = (k - 2) * (NKEY // 2)
                        ins = act.activation(kA[h % 2][0:DN, c0:c0 + NKEY // 2], ps[0:DN, 7, 0:NKEY // 2], ACT.Copy)
                    ins.then_inc(x_ev, 1)

                for r in range(4):
                    head_piece(r)
                for n in range(NA + 1):
                    h, qi = n // NT, n % NT
                    if n < NA:
                        act.wait_ge(a_neg, n + 1)
                        if n >= 2:
                            act.wait_ge(a_tp, n - 1)
                        src, view = scores_view(2 * (n % 2), qi)
                        act.activation(view(p0[n % 2]), src, ACT.Exp, bias=aneg[:, n % 2:n % 2 + 1], scale=SA,
                                       accum_out=asum[:, n % 2:n % 2 + 1]).then_inc(a_exp, 1)
                    if n >= 1:
                        turn_copy(n - 1, a_tp, a_pv, a_pt)
                    if qi < 4 and h < H_A - 1:
                        head_piece(4 * (h + 1) + qi)
                act.wait_ge(on_v, 1)
                act.activation(rs10[:, 0:NT], ss10[:, 0:NT], ACT.Sqrt, bias=eps, scale=1.0 / WA)
                act.activation(crs, css, ACT.Sqrt, bias=eps, scale=1.0 / DV_B).then_inc(on_s, 1)
                for k in range(KD):
                    act.wait_ge(ot_tp, k + 1)
                    b = 2 * (k % 4) * 512
                    act.activation(u_hi[:, k, :], psf[:, b:b + T], ACT.Copy, scale=parT[:, R_OG + k:R_OG + k + 1]).then_inc(ot_hi, 1)
                for n in range(NW2):
                    g = G_WOUT + n
                    act.wait_ge(mm_ok, g + 1)
                    hi(g + 2)
                norm(2)
                ffn(G_FFN2, NF, last=True)
                act.drain().then_inc(l_done, 1)
                act.wait_ge(s_go, l + 1)
            for m in range(KD):
                if m >= 2:
                    act.wait_ge(f_sqd, m - 1)
                act.activation(sq[:, m % 2, :], xT[:, m, :], ACT.Square).then_inc(f_sq, 1)
            act.wait_ge(f_ss, 1)
            act.activation(stdv[:, :].rearrange("p (b t) -> p b t", b=2), ps[:, 0:2, 0:TH], ACT.Sqrt, bias=eps, scale=1.0 / D).then_inc(f_std, 1)
            for m in range(KD):
                act.wait_ge(f_xn, m + 1)
                act.activation(yT[:, m, :], xn[:, m % 2, :], ACT.Copy, scale=parT[:, R_FIN + m:R_FIN + m + 1]).then_inc(s_yt, 1)
            for t in range(NT):
                act.wait_ge(s_ytp, t + 1)
                if t >= 2:
                    act.wait_ge(s_yout[t % 2], 16 * (t // 2))
                b = 2 * (t % 4) * 512
                act.activation(ytm[:, t % 2, :], psf[:, b:b + D], ACT.Copy).then_inc(s_ytm, 1)

        @block.vector
        def _(dve):
            steps = [0]

            def link(ins):
                steps[0] += 1
                ins.then_inc(dve_c, 1)
                dve.wait_ge(dve_c, steps[0])

            def lo(g, step=0):
                dve.wait_ge(hi_ok, g + 1 + step)
                dve.tensor_tensor(w_lo[:, g % 2, :], raw[:, g % 2, :], cv(w_hi[:, g % 2, :]), ALU.subtract).then_inc(lo_ok, 1)

            def norm(n):
                for m in range(KD):
                    dve.wait_ge(n_sq, n * KD + m + 1)
                    if m == 0:
                        dve.tensor_copy(sqsum[:, :], sq[:, 0, :]).then_inc(n_sqd, 1)
                    else:
                        dve.wait_ge(n_sqd, n * KD + m)
                        dve.tensor_tensor(sqsum[:, :], sqsum[:, :], sq[:, m % 2, :], ALU.add).then_inc(n_sqd, 1)
                dve.wait_ge(n_std, n + 1)
                link(dve.reciprocal(rstd[:, :], stdv[:, :]))
                for m in range(KD + 1):
                    if m < KD:
                        if m >= 2:
                            dve.wait_ge(n_u32, 2 * (n * KD + m - 1))
                        dve.tensor_tensor(xn[:, m % 2, :], xT[:, m, :], rstd[:, :], ALU.mult).then_inc(n_xn, 1)
                    if m >= 1:
                        dve.wait_ge(n_uhi, n * KD + m)
                        dve.tensor_tensor(u_lo[:, m - 1, :], u32[:, (m - 1) % 2, :], cv(u_hi[:, m - 1, :]), ALU.subtract).then_inc(n_ulo, 1)

            def update_x(kind, bank, m, dyn):
                for n, (c, b, o, t0, w) in enumerate(RANGES):
                    xa = xT[:, bass.ds(m, 1), t0:t0 + w].rearrange("p a t -> p (a t)") if dyn else xT[:, m, t0:t0 + w]
                    ga = gates[:, kind, bass.ds(m, 1), c:c + 1].rearrange("p a c -> p (a c)") if dyn else gates[:, kind, m, c:c + 1]
                    last = dve.scalar_tensor_tensor(out=xa, in0=ps[:, bank + b, o:o + w], scalar=ga, in1=xa, op0=ALU.mult, op1=ALU.add)
                return last

            def ffn(g, up0, kind, x0, last=False):
                for q, n in enumerate(PARTS):
                    with dve.Fori(0, n // 2) as i:
                        for j in range(2):
                            b = 4 * ((g + j) % 2)
                            k = up0 + j
                            dve.wait_ge(sil_ok, k + 1 + i * 2)
                            if k >= 2:
                                dve.wait_ge(hlo_ok, k - 1 + i * 2)
                            dve.tensor_tensor(h32[:, j, :].rearrange("p (b t) -> p b t", b=2), ps[:, b + 2:b + 4, 0:TH],
                                              silu_a[:, j, :].rearrange("p (b t) -> p b t", b=2), ALU.mult).then_inc(h32_ok, 1)
                            dve.wait_ge(hhi_ok, k + 1 + i * 2)
                            dve.tensor_tensor(h_lo[:, bass.ds(i * 2 + j, 1), :].rearrange("p a t -> p (a t)"), h32[:, j, :],
                                              cv(h_hi[:, bass.ds(i * 2 + j, 1), :]).rearrange("p a t -> p (a t)"), ALU.subtract).then_inc(hlo_ok, 1)
                            lo(g + j + 2, i * 2)
                    g += n
                    up0 += n
                    if x0 > 0 or q > 0:
                        dve.wait_ge(x_upd, x0)
                    with dve.Fori(0, NW2 // 2 - (1 if last and q == len(PARTS) - 1 else 0)) as i:
                        for j in range(2):
                            dve.wait_ge(mm_ok, g + j + 1 + i * 2)
                            for m2 in range(2):
                                update_x(kind, 4 * ((g + j) % 2) + 2 * m2, i * 4 + (2 * j + m2), True).then_inc(x_upd, 1)
                            lo(g + j + 2, i * 2)
                    if last and q == len(PARTS) - 1:
                        for j in range(2):
                            dve.wait_ge(mm_ok, g + j + 3)
                            for m2 in range(2):
                                update_x(kind, 4 * ((g + j) % 2) + 2 * m2, 4 + 2 * j + m2, False).then_inc(x_upd, 1)
                    g += NW2
                    x0 += KD

            def rope(x, rot, cos, sin, lk):
                swap = [i + 8 if i % 16 < 8 else i - 8 for i in range(32)]
                lk(dve.stream_shuffle(rot, x, swap))
                dve.tensor_tensor(x, x, cos, ALU.mult)
                lk(dve.tensor_tensor(rot, rot, sin, ALU.mult))
                return dve.tensor_tensor(x, x, rot, ALU.add)

            dve.wait_ge(s_const, 1)
            for m in range(KD):
                if m % 2 == 0:
                    continue
                dve.wait_ge(s_xtp, m + 1)
                b = 2 * (m % 4)
                dve.tensor_copy(xT[:, m, :], psf[:, b * 512:b * 512 + T]).then_inc(s_xv, 1)

            with dve.Fori(0, DEPTH) as l:
                steps[0] = 0
                dve.wait_ge(par_in, (l + 1) * (16 * names["n_par"]))
                for n in range(2):
                    last = dve.tensor_tensor_reduce(out=lqk[:, 2 * n, :], in0=lqk[:, 2 * n, :], in1=lqk[:, 2 * n + 1, :], scale=1.0,
                                                    scalar=0.0, op0=ALU.mult, op1=ALU.add, accum_out=lam2[:, n:n + 1])
                last.then_inc(lam_s, 1)
                dve.wait_ge(par_tp, 1)
                dve.tensor_copy(parT[:, 0:P], ps[:, 7, 0:P]).then_inc(par_ok, 1)
                dve.wait_ge(par_ok, 1)
                dve.wait_ge(lam_e, 1)
                link(dve.tensor_tensor(ldif, lexp[:, 1:2], lexp[:, 0:1], ALU.subtract))
                dve.tensor_tensor(nlam, ldif, lcon[:, 0:1], ALU.subtract)
                link(dve.tensor_scalar(parT[:, R_OG + 3:R_OG + 5], parT[:, R_OG + 3:R_OG + 5], lcon[:, 1:2], None, ALU.mult))

                def mod_add(c, i=0):
                    dve.wait_ge(m_tp, c + 1 + i * 6)
                    n = MW // P
                    r0 = i * (6 * n) + c * n
                    dst = modT[:, bass.ds(r0, n), :]
                    bias = parT[:, bass.ds(r0, n)].unsqueeze(2).broadcast_to([P, n, 2])
                    dve.tensor_tensor(dst, ps[:, 2 + c % 2, 0:2 * n].rearrange("p (r c) -> p r c", c=2), bias, ALU.add).then_inc(m_ev, 1)

                with dve.Fori(0, NMC // 6) as i:
                    for c in range(6):
                        mod_add(c, i)
                dve.wait_ge(m_ev, NMC)
                for n, r in enumerate((R_N1, R_NM, R_N2)):
                    w = parT[:, r:r + KD].unsqueeze(2).broadcast_to([P, KD, 2])
                    dve.scalar_tensor_tensor(out=gains[:, n], in0=modT[:, (3 * n + 1) * KD:(3 * n + 2) * KD, :], scalar=1.0, in1=w,
                                             op0=ALU.add, op1=ALU.mult)
                    last = dve.tensor_scalar(gates[:, n], modT[:, (3 * n + 2) * KD:(3 * n + 3) * KD, :], (0.5, 1.0, 0.5)[n], None, ALU.mult)
                link(last)
                dve.sem_inc(mod_ok, 1)
                lo(0)
                lo(1)
                norm(0)
                ffn(G_FFN1, 0, 0, 0)
                norm(1)
                for n, name in enumerate(PROJ):
                    lo(G_PROJ + n + 2)
                cos2 = cosT[:, :].unsqueeze(1).broadcast_to([P, 2, TL])
                sin2 = sinT[:, :].unsqueeze(1).broadcast_to([P, 2, TL])
                dve.wait_ge(ev_ok, len(PROJ))
                link(rope(kbT[:, :, TC + PAST:NKEY], rotb[:, :, :], cos2, sin2, link))
                rope(qbT[:, :, TC:T], rotb[:, :, :], cos2, sin2, link).then_inc(rb_ok, 1)
                dve.wait_ge(cq_ss, 1)
                dve.tensor_reduce(ss10[:, 0:NT], csq[:, :, 0:Q_RANK], AX.X, ALU.add)
                dve.tensor_reduce(ss10[:, NT:2 * NT], csq[:, :, Q_RANK:640], AX.X, ALU.add).then_inc(cq_sd, 1)
                dve.wait_ge(cq_ss, 2)
                link(dve.reciprocal(ss10, rs10))
                for t in range(NT):
                    dve.tensor_scalar(cqkv[:, t, 0:Q_RANK], cqkv[:, t, 0:Q_RANK], ss10[:, t:t + 1], None, ALU.mult)
                    last = dve.tensor_scalar(cqkv[:, t, Q_RANK:640], cqkv[:, t, Q_RANK:640], ss10[:, NT + t:NT + t + 1], None, ALU.mult)
                link(last)
                kv = cqkv[:, :, Q_RANK:640]
                dve.tensor_tensor(kv, kv, kvw[:, :].unsqueeze(1).broadcast_to([P, NT, KV_RANK]), ALU.mult).then_inc(cq_ok, 1)
                for d in range(2):
                    rev = slice(None, None, -1) if d else slice(None)
                    dve.wait_ge(g_z, d + 1)
                    for p in range(2):
                        last = dve.tensor_scalar(gb[:, p, :].rearrange("p (b t) -> p b t", b=2), ps[:, 2 * p:2 * p + 2, 0:TH],
                                                 parT[:, R_BG + 2 * d + p:R_BG + 2 * d + p + 1], None, ALU.add)
                    last.then_inc(g_min, 1)
                    dve.wait_ge(g_ln, d + 1)
                    link(dve.scalar_tensor_tensor(out=gb[:, :, :], in0=gb[:, :, :], scalar=0.0, in1=gab[:, :, :], op0=ALU.min, op1=ALU.subtract))
                    for p in range(2):
                        last = dve.tensor_tensor_scan(gcum[:, p, rev], keep[:, d, rev], gb[:, p, rev], 0.0, ALU.mult, ALU.add)
                    last.then_inc(g_cum, 1)
                    dve.wait_ge(g_cum, d + 1)
                    c4 = gcum[:, :, :].rearrange("p a (c t) -> p (a c) t", t=CH)
                    e = (CH - 1, 0)[d]
                    dve.tensor_tensor(gb[:, :, :].rearrange("p a (c t) -> p (a c) t", t=CH),
                                      c4[:, :, e:e + 1].broadcast_to([P, 2 * NCH, CH]), c4, ALU.subtract).then_inc(g_bl, 1)
                    dve.wait_ge(g_e1, d + 1)
                    dve.scalar_tensor_tensor(out=gqe[:, :, :], in0=qcT[:, :, :], scalar=DK ** -0.5, in1=gqe[:, :, :],
                                             op0=ALU.mult, op1=ALU.mult).then_inc(g_qe, 1)
                    dve.wait_ge(g_e2, d + 1)
                    dve.tensor_tensor(gke[:, :, :], kcT[:, :, :], gke[:, :, :], ALU.mult).then_inc(g_ke, 1)
                    dve.wait_ge(g_e3, d + 1)
                    dve.tensor_tensor(gkd[:, :, :], kcT[:, :, :], gkd[:, :, :], ALU.mult).then_inc(g_kd, 1)
                    for n, c in enumerate(U_ORDER[d]):
                        dve.wait_ge(g_u, d * N_STATE + n + 1)
                        upd = ps[:, 6 + n % 2, 0:2 * DV_C].rearrange("p (a v) -> p a v", a=2)
                        nxt = c + (1, -1)[d]
                        if n == 0:
                            dve.tensor_copy(S[:, nxt], upd).then_inc(g_s, 1)
                            continue
                        if n == 1 and d == 1:
                            dve.wait_ge(out_in, l * (16 * 8) + 16 * 6)
                        dve.wait_ge(g_s, d * N_STATE + n)
                        src = entering(d, c)
                        dst = Sfin[:, :, :] if n == 1 else S[:, nxt]
                        for a in range(2):
                            last = dve.scalar_tensor_tensor(out=dst[:, a, :], in0=src[:, a, :], scalar=gtot[:, a, c:c + 1], in1=upd[:, a, :],
                                                            op0=ALU.mult, op1=ALU.add)
                        last.then_inc(g_s, 1)
                        if n == 1:
                            dve.wait_ge(g_s, d * N_STATE + 2)
                            dve.sem_inc(g_fin, 1)
                    for n, t in enumerate(O_ORDER[d]):
                        dve.wait_ge(g_at, d * NT + n + 1)
                        if n >= 2:
                            dve.wait_ge(g_o, d * NT + n - 1)
                        b = 2 * (n % 2)
                        dve.tensor_tensor(am[:, n % 2, :].rearrange("p (b a t) -> p b a t", b=2, a=2),
                                          ps[:, b:b + 2, 0:2 * P].rearrange("p b (a t) -> p b a t", a=2),
                                          mask[:, d, :].unsqueeze(1).unsqueeze(1).broadcast_to([P, 2, 2, P]), ALU.mult).then_inc(g_am, 1)
                        if d == 1 and n >= 1:
                            add_back(n - 1)
                    if d == 0:
                        def add_back(n):
                            t = O_ORDER[1][n]
                            dve.wait_ge(g_o, NT + n + 1)
                            dve.tensor_tensor(heads_out(t), heads_ps(), heads_out(t), ALU.add).then_inc(g_oev, 1)
                add_back(NT - 1)
                dve.wait_ge(g_oev, 2 * NT)
                oc = omix[:, :, WA + WB:D]
                link(dve.tensor_tensor(osq[:, :, :], oc, oc, ALU.mult))
                dve.tensor_reduce(css.rearrange("p (t h) -> p t h", h=H_C), osq[:, :, :].rearrange("p t (h v) -> p t h v", h=H_C), AX.X, ALU.add).then_inc(gn_v, 1)
                dve.wait_ge(gn_s, 1)
                link(dve.reciprocal(css, crs))
                och = oc.rearrange("p t (h v) -> p t h v", h=H_C)
                link(dve.tensor_tensor(och, och, css.rearrange("p (t h) -> p t h", h=H_C).unsqueeze(3).broadcast_to([P, NT, H_C, DV_C]), ALU.mult))
                dve.tensor_tensor(oc, oc, rcs[:, :, :], ALU.mult).then_inc(gn_ok, 1)
                NB = H_B * NT

                def scores(s, qi):
                    return ps[:, s, 0:P] if qi == 0 else ps[:, s:s + 2, 0:TH]

                def top(s, qi, c, scale):
                    link(dve.tensor_reduce(amax[:, c:c + 1], scores(s, qi), AX.X if qi == 0 else AX.XY, ALU.max))
                    return dve.tensor_scalar(aneg[:, c:c + 1], amax[:, c:c + 1], -scale, None, ALU.mult)

                dve.wait_ge(rb_ok, 1)
                for n in range(NB + 3):
                    h, qi = n // NT, n % NT
                    if n >= 3:
                        m = n - 3
                        dve.wait_ge(b_pv, m + 1)
                        c0 = WA + (m // NT) * DV_B
                        dve.tensor_copy(omix[:, m % NT, c0:c0 + DV_B], ps[:, 6, 0:DV_B]).then_inc(b_o, 1)
                    if n < NB:
                        if qi == 0:
                            if h >= 2:
                                dve.wait_ge(b_sc, 2 * NT * (h - 1))
                            for j in range(2):
                                r = 2 * h + j
                                last = dve.tensor_scalar(qm[h % 2][j][:, :], qbT[:, r // 4, :], grp[:, r % 4:r % 4 + 1], None, ALU.mult)
                            last.then_inc(b_qm, 1)
                        for j in range(2):
                            dve.wait_ge(b_sc, 2 * n + j + 1)
                            top(2 * j, qi, 2 * (n % 2) + j, DH_B ** -0.5).then_inc(b_neg, 1)
                    if 1 <= n <= NB:
                        m = n - 1
                        w = P if m % NT == 0 else T
                        c = 2 * (m % 2)
                        dve.wait_ge(b_exp, 2 * m + 2)
                        link(dve.reciprocal(arec[:, c:c + 2], asum[:, c:c + 2]))
                        dve.tensor_tensor(arec[:, c + 1:c + 2], arec[:, c + 1:c + 2], nlam, ALU.mult)
                        link(dve.tensor_scalar(p0[m % 2][:, 0:w], p0[m % 2][:, 0:w], arec[:, c:c + 1], None, ALU.mult))
                        dve.scalar_tensor_tensor(out=p0[m % 2][:, 0:w], in0=p1[m % 2][:, 0:w], scalar=arec[:, c + 1:c + 2], in1=p0[m % 2][:, 0:w],
                                                 op0=ALU.mult, op1=ALU.add).then_inc(b_a, 1)
                dve.wait_ge(ap_ev, 6)
                rope(krT[:, TC + PAST:NKEY], rota[0:DR, :], cosT[0:DR, :], sinT[0:DR, :], link).then_inc(ap_kr, 1)
                dve.wait_ge(ap_kr, 1)

                def head_ready(h):
                    dve.wait_ge(x_ev, 4 * h + 4)
                    dve.tensor_copy(kA[h % 2][DN:DQ, :], krT[:, :])
                    rope(qA[h % 2][DN:DQ, TC:T], rota[DN:DQ, :], cosT[DN:DQ, :], sinT[DN:DQ, :], link).then_inc(a_qk, 1)

                head_ready(0)
                NA = H_A * NT
                for n in range(NA + 3):
                    h, qi = n // NT, n % NT
                    if n >= 3:
                        m = n - 3
                        dve.wait_ge(a_pv, m + 1)
                        dve.tensor_scalar(omix[:, m % NT, (m // NT) * DV_A:(m // NT + 1) * DV_A], ps[:, 6, 0:DV_A],
                                          arec[:, m % 4:m % 4 + 1], None, ALU.mult).then_inc(a_o, 1)
                    if n < NA:
                        dve.wait_ge(a_sc, n + 1)
                        top(2 * (n % 2), qi, n % 2, DQ ** -0.5).then_inc(a_neg, 1)
                    if 1 <= n <= NA:
                        m = n - 1
                        dve.wait_ge(a_exp, m + 1)
                        link(dve.reciprocal(arec[:, m % 4:m % 4 + 1], asum[:, m % 2:m % 2 + 1]))
                    if qi == 4 and h < H_A - 1:
                        head_ready(h + 1)
                dve.wait_ge(a_o, NA)
                oa, ob = omix[:, :, 0:WA], omix[:, :, WA:WA + WB]
                link(dve.tensor_tensor(asq[:, :, :], oa, oa, ALU.mult))
                link(dve.tensor_reduce(ss10[:, 0:NT], asq[:, :, :], AX.X, ALU.add))
                link(dve.tensor_tensor(asq[:, :, 0:WB], ob, ob, ALU.mult))
                dve.tensor_reduce(css.rearrange("p (t h) -> p t h", h=H_B), asq[:, :, 0:WB].rearrange("p t (h v) -> p t h v", h=H_B), AX.X, ALU.add).then_inc(on_v, 1)
                dve.wait_ge(on_s, 1)
                dve.reciprocal(ss10[:, 0:NT], rs10[:, 0:NT])
                link(dve.reciprocal(css, crs))
                dve.tensor_tensor(oa, oa, ss10[:, 0:NT].unsqueeze(2).broadcast_to([P, NT, WA]), ALU.mult)
                obh = ob.rearrange("p t (h v) -> p t h v", h=H_B)
                dve.tensor_tensor(obh, obh, css.rearrange("p (t h) -> p t h", h=H_B).unsqueeze(3).broadcast_to([P, NT, H_B, DV_B]), ALU.mult).then_inc(on_ok, 1)
                for k in range(KD):
                    dve.wait_ge(ot_hi, k + 1)
                    b = 2 * (k % 4) * 512
                    dve.scalar_tensor_tensor(out=u_lo[:, k, :], in0=psf[:, b:b + T], scalar=parT[:, R_OG + k:R_OG + k + 1], in1=cv(u_hi[:, k, :]),
                                             op0=ALU.mult, op1=ALU.subtract).then_inc(ot_lo, 1)
                for n in range(NW2):
                    g = G_WOUT + n
                    dve.wait_ge(mm_ok, g + 1)
                    for m2 in range(2):
                        update_x(1, 4 * (g % 2) + 2 * m2, 2 * n + m2, False).then_inc(x_upd, 1)
                    lo(g + 2)
                norm(2)
                ffn(G_FFN2, NF, 2, (len(PARTS) + 1) * KD, last=True)
                dve.drain().then_inc(l_done, 1)
                dve.wait_ge(s_go, l + 1)
            for m in range(KD):
                dve.wait_ge(f_sq, m + 1)
                if m == 0:
                    dve.tensor_copy(sqsum[:, :], sq[:, 0, :]).then_inc(f_sqd, 1)
                else:
                    dve.wait_ge(f_sqd, m)
                    dve.tensor_tensor(sqsum[:, :], sqsum[:, :], sq[:, m % 2, :], ALU.add).then_inc(f_sqd, 1)
            dve.wait_ge(f_std, 1)
            dve.reciprocal(rstd[:, :], stdv[:, :]).then_inc(f_sum, 1)
            dve.wait_ge(f_sum, 1)
            for m in range(KD):
                if m >= 2:
                    dve.wait_ge(s_yt, m - 1)
                dve.tensor_tensor(xn[:, m % 2, :], xT[:, m, :], rstd[:, :], ALU.mult).then_inc(f_xn, 1)

        @block.tensor
        def _(pe):
            def up_banks(g):
                return 4 * (g % 2)

            def fm(g, step, src, nk, per_k, n_out=2, width=P, tail=None):
                b = up_banks(g)
                wh = w_hi[:, g % 2, :].rearrange("p (k n) -> p k n", k=KD)
                wl = w_lo[:, g % 2, :].rearrange("p (k n) -> p k n", k=KD)
                xh, xl = src
                pe.wait_ge(lo_ok, g + 1 + step)
                for o in range(n_out):
                    for k in range(nk):
                        if o == 0 and per_k is not None:
                            per_k(k)
                        for half in range(2):
                            t = slice(half * TH, (half + 1) * TH)
                            out = ps[0:width, b + 2 * o + half, 0:TH]
                            c = slice(o * P, o * P + width)
                            pe.matmul(out, wh[:, k, c], xh[:, k, t], start=k == 0, stop=False)
                            pe.matmul(out, wh[:, k, c], xl[:, k, t], start=False, stop=False)
                            last = pe.matmul(out, wl[:, k, c], xh[:, k, t], start=False, stop=k == nk - 1)
                last.then_inc(mm_ok, 1)

            def fm_pair(g, src, per_k, shapes):
                xh, xl = src
                pe.wait_ge(lo_ok, g + 2)
                last = [None, None]
                for k in range(KD):
                    per_k(k)
                    for c in range(2):
                        n_out, width = shapes[c]
                        wh = w_hi[:, (g + c) % 2, :].rearrange("p (k n) -> p k n", k=KD)
                        wl = w_lo[:, (g + c) % 2, :].rearrange("p (k n) -> p k n", k=KD)
                        for o in range(n_out):
                            for half in range(2):
                                t = slice(half * TH, (half + 1) * TH)
                                out = ps[0:width, up_banks(g + c) + 2 * o + half, 0:TH]
                                w = slice(o * P, o * P + width)
                                pe.matmul(out, wh[:, k, w], xh[:, k, t], start=k == 0, stop=False)
                                pe.matmul(out, wh[:, k, w], xl[:, k, t], start=False, stop=False)
                                last[c] = pe.matmul(out, wl[:, k, w], xh[:, k, t], start=False, stop=k == KD - 1)
                        if k == KD - 1:
                            last[c].then_inc(mm_ok, 1)

            def tmaj(g):
                b = up_banks(g)
                wh = w_hi[:, g % 2, :].rearrange("p (k n) -> p k n", k=KD)
                wl = w_lo[:, g % 2, :].rearrange("p (k n) -> p k n", k=KD)
                pe.wait_ge(lo_ok, g + 1)
                for t in range(NT):
                    out = psf[:, b * 512 + t * CW:b * 512 + (t + 1) * CW]
                    c = slice(t * P, (t + 1) * P)
                    for k in range(KD):
                        pe.matmul(out, u_hi[:, k, c], wh[:, k, :], start=k == 0, stop=False)
                        pe.matmul(out, u_lo[:, k, c], wh[:, k, :], start=False, stop=False)
                        last = pe.matmul(out, u_hi[:, k, c], wl[:, k, :], start=False, stop=k == KD - 1)
                last.then_inc(mm_ok, 1)

            def sums(s_in, v_in, s_out):
                pe.wait_ge(s_in, v_in)
                for half in range(2):
                    last = pe.matmul(ps[:, half, 0:TH], ones[:, :], sqsum[:, half * TH:(half + 1) * TH], start=True, stop=True)
                last.then_inc(s_out, 1)

            def u_tile(n):
                return lambda k: pe.wait_ge(n_ulo, n * KD + k + 1)

            def ffn(g, up0, x0, n):
                for q, cnt in enumerate(PARTS):
                    start = 0
                    if q == 0:
                        fm_pair(g, (u_hi, u_lo), u_tile(n), [(2, P), (2, P)])
                        start = 1
                    with pe.Fori(start, cnt // 2) as i:
                        for j in range(2):
                            if q > 0:
                                pe.wait_ge(x_upd, x0 + q * KD)
                            pe.wait_ge(h32_ok, up0 + j - 1 + i * 2) if up0 + j + 2 * start >= 2 and not (q > 0 and up0 + j < 2) else None
                            fm(g + j, i * 2, (u_hi, u_lo), KD, None)
                    g += cnt
                    up0 += cnt
                    pe.wait_ge(h32_ok, up0)
                    h_in = (lambda base: lambda k: pe.wait_ge(hlo_ok, base + k + 1))(up0 - cnt)
                    fm(g, 0, (h_hi, h_lo), cnt, h_in)
                    fm(g + 1, 0, (h_hi, h_lo), cnt, None)
                    with pe.Fori(1, NW2 // 2) as i:
                        for j in range(2):
                            pe.wait_ge(x_upd, i * 4 + (x0 + q * KD + 2 * j - 2))
                            fm(g + j, i * 2, (h_hi, h_lo), cnt, None)
                    g += NW2

            pe.wait_ge(s_const, 26)
            pe.wait_ge(s_tab, 64)
            pe.transpose(ps[:, 0, 0:2 * KD], par[0:2 * KD, :], ident[0:2 * KD, 0:2 * KD]).then_inc(s_ctp, 1)
            pe.wait_ge(s_csil, 1)
            pe.wait_ge(s_xs, 32)
            for m in range(KD):
                if m >= 4:
                    pe.wait_ge((s_xa, s_xv)[m % 2], (m - 4) // 2 + 1)
                b = 2 * (m % 4) * 512
                for t in range(NT):
                    last = pe.transpose(psf[:, b + t * P:b + (t + 1) * P], xs[:, t, m * P:(m + 1) * P], ident[:, :])
                last.then_inc(s_xtp, 1)
            pe.wait_ge(s_const, 27)
            pe.wait_ge(s_xa, KD // 2)
            pe.wait_ge(s_xv, KD // 2)

            with pe.Fori(0, DEPTH) as l:
                pe.wait_ge(par_in, (l + 1) * (16 * names["n_par"]))
                pe.transpose(ps[:, 7, 0:P], par[:, :], ident[:, :]).then_inc(par_tp, 1)
                def mod(c, i, first):
                    s = c % 3
                    pe.wait_ge(m_raw[s], 16 * (c // 3 + 1) + i * 32)
                    if not first:
                        pe.wait_ge(m_row, c - 1 + i * 6)
                    for kk in range(2):
                        for j in range(4):
                            k = j + 4 * kk
                            last = pe.matmul(ps[32 * j:32 * j + 32, c % 2, :], csp[:, k, :], mraw[:, s, k, :], start=kk == 0, stop=kk == 1)
                    last.then_inc(m_mm, 1)
                    pe.wait_ge(m_row, c + 1 + i * 6)
                    if not first:
                        pe.wait_ge(m_ev, c - 1 + i * 6)
                    for r in range(MW // P):
                        last = pe.matmul(ps[:, 2 + c % 2, 2 * r:2 * r + 2], mrows[:, c % 2, r * P:(r + 1) * P], comb[:, :], start=True, stop=True)
                    last.then_inc(m_tp, 1)

                for c in range(6):
                    mod(c, 0, c < 2)
                with pe.Fori(1, NMC // 6) as i:
                    for c in range(6):
                        mod(c, i, False)
                sums(n_sqd, KD, n_ss)
                ffn(G_FFN1, 0, 0, 0)
                sums(n_sqd, 2 * KD, n_ss)
                for n, name in enumerate(PROJ):
                    g = G_PROJ + n
                    if n >= 2:
                        pe.wait_ge(ev_ok, n - 1)
                    if n == 0:
                        fm_pair(g, (u_hi, u_lo), u_tile(1), [(1, 2 * GR), (2, P)])
                    elif n == 1:
                        continue
                    elif name in ("qc", "kc", "qb"):
                        fm(g, 0, (u_hi, u_lo), KD, None)
                    else:
                        tmaj(g)
                pe.wait_ge(ev_ok, len(PROJ))
                pe.wait_ge(kv_in, (l + 1) * 32)
                for m in range(2):
                    last = pe.transpose(ps[:, 0, m * P:(m + 1) * P], ck[:, m * P:(m + 1) * P], ident[:, :])
                last.then_inc(bk_tp, 1)
                for m in range(2):
                    last = pe.transpose(ps[:, 1, m * P:(m + 1) * P], kbT[:, m, 0:TC], ident[:, :])
                last.then_inc(bk_tp, 1)
                pe.wait_ge(bk_ev, 2)
                for d in range(2):
                    if d == 1:
                        pe.wait_ge(g_oev, NT)
                        pe.wait_ge(g_s, N_STATE)
                    for p in range(2):
                        for half in range(2):
                            last = pe.matmul(ps[:, 2 * p + half, 0:TH], wgp[:, d, p * P:(p + 1) * P], glT[:, half * TH:(half + 1) * TH], start=True, stop=True)
                    last.then_inc(g_z, 1)
                    pe.wait_ge(g_kd, d + 1)
                    for t in range(NT):
                        if d * NT + t >= 2:
                            pe.wait_ge(g_tev, d * NT + t - 1)
                        for a in range(2):
                            last = pe.transpose(ps[:, 4 + t % 2, a * P:(a + 1) * P], gkd[:, a, t * P:(t + 1) * P], ident[:, :])
                        last.then_inc(g_tp, 1)
                    for n, c in enumerate(U_ORDER[d]):
                        pe.wait_ge(g_tev, d * NT + c // 2 + 1)
                        if n >= 2:
                            pe.wait_ge(g_s, d * N_STATE + n - 1)
                        r = slice(CH * (c % 2), CH * (c % 2) + CH)
                        for h in range(H_C):
                            hh, a = h % 2, h // 2
                            last = pe.matmul(ps[HW * hh:HW * hh + HW, 6 + n % 2, a * DV_C:(a + 1) * DV_C],
                                             kdt[r, c // 2, a, HW * hh:HW * hh + HW], vcs[r, c // 2, h * DV_C:(h + 1) * DV_C], start=True, stop=True)
                        last.then_inc(g_u, 1)
                    pe.wait_ge(g_ke, d + 1)

                    def intra_scores(n):
                        t = O_ORDER[d][n]
                        if n >= 2:
                            pe.wait_ge(g_am, d * NT + n - 1)
                        ts = slice(t * P, (t + 1) * P)
                        for h in range(H_C):
                            rows = slice(HW * (h % 2), HW * (h % 2) + DK)
                            last = pe.matmul(ps[:, 2 * (n % 2) + h % 2, (h // 2) * P:(h // 2 + 1) * P], gke[rows, h // 2, ts], gqe[rows, h // 2, ts], start=True, stop=True)
                        last.then_inc(g_at, 1)

                    intra_scores(0)
                    for n, t in enumerate(O_ORDER[d]):
                        if n + 1 < NT:
                            intra_scores(n + 1)
                        pe.wait_ge(g_am, d * NT + n + 1)
                        if n >= 1:
                            pe.wait_ge(g_oev, d * NT + n)
                        for c in (2 * t, 2 * t + 1):
                            if state_count(d, c):
                                pe.wait_ge(g_s, d * N_STATE + state_count(d, c))
                        for h in range(H_C):
                            rows = slice(HW * (h % 2), HW * (h % 2) + DK)
                            bank, cols = 4 + h % 2, slice((h // 2) * DV_C, (h // 2 + 1) * DV_C)
                            ha = 2 * (h % 2) + h // 2
                            last = pe.matmul(ps[:, bank, cols], am[:, n % 2, ha * P:(ha + 1) * P], vcs[:, t, h * DV_C:(h + 1) * DV_C], start=True, stop=False, skip_group_check=True)
                            for c in (2 * t, 2 * t + 1):
                                if has_state(d, c):
                                    q0 = CH * (c % 2)
                                    last = pe.matmul(ps[q0:q0 + CH, bank, cols], gqe[rows, h // 2, c * CH:(c + 1) * CH],
                                                     entering(d, c)[rows, h // 2, :], start=False, stop=True, skip_group_check=True)
                        last.then_inc(g_o, 1)
                NB = H_B * NT
                pe.wait_ge(g_oev, 2 * NT)
                pe.wait_ge(g_s, 2 * N_STATE)

                def score(s, q, kt, qi, s_sc):
                    if qi == 0:
                        last = pe.matmul(ps[:, s, 0:P], q, kt[:, 0:TC], start=True, stop=True)
                    else:
                        for half in range(2):
                            k0 = TC + half * TH
                            last = pe.matmul(ps[:, s + half, 0:TH], q, kt[:, k0:k0 + TH], start=True, stop=True)
                    last.then_inc(s_sc, 1)

                def turn(m, prob, s_tp, s_pt):
                    nk = 1 if m % NT == 0 else NT
                    if m >= 1:
                        pe.wait_ge(s_pt, m)
                    for k in range(nk):
                        last = pe.transpose(psf[:, 4 * 512 + k * P:4 * 512 + (k + 1) * P], prob[:, k * P:(k + 1) * P], ident[:, :])
                    last.then_inc(s_tp, 1)

                def values(m, s_pt, s_pv, s_o, v, c0):
                    nk = 1 if m % NT == 0 else NT
                    pe.wait_ge(s_pt, m + 1)
                    if m >= 1:
                        pe.wait_ge(s_o, m)
                    v0 = keys_of(m % NT)[0]
                    for k in range(nk):
                        last = pe.matmul(ps[:, 6, 0:96], pt[m % 2][:, k, :], v[:, v0 + k, c0:c0 + 96], start=k == 0, stop=k == nk - 1)
                    last.then_inc(s_pv, 1)

                pe.wait_ge(pool_c, 1)
                for n in range(NB + 2):
                    h, qi = n // NT, n % NT
                    if n < NB:
                        if qi == 0:
                            pe.wait_ge(b_qm, h + 1)
                        for j in range(2):
                            r = 2 * h + j
                            if n >= 1:
                                pe.wait_ge(b_exp, 2 * (n - 1) + j + 1)
                            score(2 * j, qm[h % 2][j][:, qi * P:(qi + 1) * P], kbT[:, r // 4, :], qi, b_sc)
                    if n >= 2:
                        values(n - 2, b_pt, b_pv, b_o, vbs, ((n - 2) // NT) * DV_B)
                    if 1 <= n <= NB:
                        pe.wait_ge(b_a, n)
                        turn(n - 1, p0[(n - 1) % 2], b_tp, b_pt)
                pe.wait_ge(aw_in, (l + 1) * (16 * 5))
                pe.wait_ge(b_o, NB)
                pe.wait_ge(cq_ok, 1)
                for s in range(6):
                    if s >= 4:
                        pe.wait_ge(ap_ev, s - 3)
                    b = 2 * (s % 4) * 512
                    w = (DR if s == 5 else P)
                    c0 = (s * P if s < 3 else Q_RANK + (s - 3) * P if s < 5 else 640)
                    tiles = [cqkv[:, t, c0:c0 + w] for t in range(NT)]
                    if s in (3, 4):
                        tiles.insert(1, cc[:, (s - 3) * P:(s - 2) * P])
                    if s == 5:
                        tiles.insert(1, cck[:, :])
                    for t, src in enumerate(tiles):
                        last = pe.transpose(psf[0:w, b + t * P:b + (t + 1) * P], src, ident[:, :])
                    last.then_inc(ap_tp, 1)
                pe.wait_ge(ap_ev, 6)
                for t in range(NKT):
                    for k in range(2):
                        last = pe.matmul(ps[:, t, 0:WA], ckvT[:, k, t * P:(t + 1) * P], wuv[:, k, :], start=k == 0, stop=k == 1)
                    last.then_inc(ap_tp, 1)

                def head_piece(r):
                    h, k = r // 4, r % 4
                    if r >= 1:
                        pe.wait_ge(x_ev, r)
                    if k < 2:
                        for c in range(3):
                            last = pe.matmul(ps[0:DQ, 7, 0:TH], wuq[:, c, h * DQ:(h + 1) * DQ], cqT[:, c, k * TH:(k + 1) * TH], start=c == 0, stop=c == 2)
                    else:
                        c0 = (k - 2) * (NKEY // 2)
                        for c in range(2):
                            last = pe.matmul(ps[0:DN, 7, 0:NKEY // 2], wuk[:, c, h * DN:(h + 1) * DN], ckvT[:, c, c0:c0 + NKEY // 2], start=c == 0, stop=c == 1)
                    last.then_inc(x_mm, 1)

                for r in range(4):
                    head_piece(r)
                NA = H_A * NT
                pe.wait_ge(ap_ev, 6 + NKT)
                pe.wait_ge(pool_c, 2)
                for n in range(NA + 2):
                    h, qi = n // NT, n % NT
                    if n < NA:
                        if qi == 0:
                            pe.wait_ge(a_qk, h + 1)
                        if n >= 2:
                            pe.wait_ge(a_exp, n - 1)
                        score(2 * (n % 2), qA[h % 2][0:DQ, qi * P:(qi + 1) * P], kA[h % 2][0:DQ, :], qi, a_sc)
                    if n >= 2:
                        values(n - 2, a_pt, a_pv, a_o, vas, ((n - 2) // NT) * DV_A)
                    if 1 <= n <= NA:
                        pe.wait_ge(a_exp, n)
                        turn(n - 1, p0[(n - 1) % 2], a_tp, a_pt)
                    if qi < 4 and h < H_A - 1:
                        head_piece(4 * (h + 1) + qi)
                pe.wait_ge(on_ok, 1)
                for k in range(KD):
                    if k >= 4:
                        pe.wait_ge(ot_lo, k - 3)
                    b = 2 * (k % 4) * 512
                    for t in range(NT):
                        last = pe.transpose(psf[:, b + t * P:b + (t + 1) * P], omix[:, t, k * P:(k + 1) * P], ident[:, :])
                    last.then_inc(ot_tp, 1)
                pe.wait_ge(ot_lo, KD)
                for n in range(NW2):
                    g = G_WOUT + n
                    if n >= 2:
                        pe.wait_ge(x_upd, 3 * KD + 2 * (n - 1))
                    fm(g, 0, (u_hi, u_lo), KD, None)
                sums(n_sqd, 3 * KD, n_ss)
                ffn(G_FFN2, NF, 4 * KD, 2)
                pe.drain().then_inc(l_done, 1)
                pe.wait_ge(s_go, l + 1)
            sums(f_sqd, KD, f_ss)
            pe.wait_ge(s_yt, KD)
            for t in range(NT):
                if t >= 4:
                    pe.wait_ge(s_ytm, t - 3)
                b = 2 * (t % 4) * 512
                for k in range(KD):
                    last = pe.transpose(psf[:, b + k * P:b + (k + 1) * P], yT[:, k, t * P:(t + 1) * P], ident[:, :])
                last.then_inc(s_ytp, 1)


def rope_tables():
    inv = (10000.0 ** (-np.arange(0, 16, 2, dtype=np.float32) / np.float32(16))).astype(np.float32)
    tok = np.arange(TL)
    cos, sin = np.zeros((32, TL), np.float32), np.zeros((32, TL), np.float32)
    for i in range(32):
        pos = (tok // GRID_W if i < 16 else tok % GRID_W).astype(np.float32)
        ang = pos * inv[i % 8]
        cos[i] = np.cos(ang)
        sin[i] = np.sin(ang) * (-1.0 if i % 16 < 8 else 1.0)
    return np.tile(cos, (4, 1)), np.tile(sin, (4, 1))


def layer_constants():
    lam = [0.8 - 0.6 * math.exp(-0.3 * l) for l in range(DEPTH)]
    return np.ascontiguousarray(np.broadcast_to(np.array([[x, 1.0 - x] for x in lam], np.float32)[:, None, :], (DEPTH, P, 2)))


OUTS = {
    "y_prompt": (1, TC, D), "y_sample": (1, TL, D),
    "new_mla_ckv": (1, DEPTH, TC, KV_RANK), "new_mla_krope": (1, DEPTH, TC, DR),
    "new_diff_k": (1, DEPTH, TC, H_B, 2 * DH_B), "new_diff_v": (1, DEPTH, TC, H_B, DV_B),
    "new_gla_fwd": (1, DEPTH, H_C, DK, DV_C), "new_gla_bwd": (1, DEPTH, H_C, DK, DV_C),
}


def kernel(**inputs):
    import concourse.bacc as bacc
    from concourse.bass_utils import run_bass_kernel_spmd

    nc = bacc.Bacc("TRN2", target_bir_lowering=False, num_devices=1)
    arrays = {name: np.ascontiguousarray(a) for name, a in inputs.items()}
    arrays["rope_cos"], arrays["rope_sin"] = rope_tables()
    arrays["layer_consts"] = layer_constants()
    A = {n: nc.dram_tensor(f"in_{n}", a.shape, mybir.dt.from_np(a.dtype), kind="ExternalInput").ap() for n, a in arrays.items()}
    O = {n: nc.dram_tensor(f"out_{n}", s, F32, kind="ExternalOutput").ap() for n, s in OUTS.items()}
    build(nc, A, O)
    r = run_bass_kernel_spmd(nc, [{f"in_{n}": a for n, a in arrays.items()}], core_ids=[0])
    return tuple(r.results[0][f"out_{n}"] for n in OUTS)
```

```python
import math
from contextlib import ExitStack

import concourse.bass as bass
import numpy as np
from concourse import mybir

F32 = mybir.dt.float32
F32R = mybir.dt.float32r
ACT = mybir.ActivationFunctionType
ALU = mybir.AluOpType
AX = mybir.AxisListType

P = 128
D = 1024
KD = D // P
DEPTH = 2
TC, TL, PAST = 128, 512, 128
T = TC + TL
NT = T // P
TH = T // 2
NKEY = TC + PAST + TL
NKT = NKEY // P
GRID_W = 64
EPS = 1e-6
H_A, DN, DR, DV_A = 6, 64, 32, 64
DQ = DN + DR
Q_RANK, KV_RANK = 384, 256
H_B, DH_B, DV_B = 4, 32, 64
H_C, DK, DV_C = 4, 48, 96
GR = 16
GATE_NORM = 16.0
CH = 64
NCH = T // CH
HW = 64
WA, WB, WC = H_A * DV_A, H_B * DV_B, H_C * DV_C
F = 2816
NF = F // P
PARTS = [8, 8, 6]
NMOD = 9
NMT = NMOD * KD
CW = 256
MW = 512
NMC = 2 * D // MW
G_MOD = 2
N_UNDER = (NMOD - 2) * D // CW
NW2 = D // CW
O_CQ, O_QB, O_KB, O_VB = 0, 672, 928, 1184
O_QC, O_KC, O_VR, O_GL = 1440, 1632, 1824, 2592
PROJ = ["gl", "kb", "qb", "qc", "kc", "c0", "c1", "c2", "vb", "vr0", "vr1", "vr2"]
Z_AT = 2
G_FFN1 = 0
N_FFN = sum(PARTS) + NW2 * len(PARTS)
G_PROJ = G_FFN1 + N_FFN
G_WOUT = G_PROJ + len(PROJ)
G_FFN2 = G_WOUT + NW2
N_CHUNK = G_FFN2 + N_FFN
R_BMOD, R_N1, R_NM, R_N2, R_FIN, R_QN, R_OG, R_BG, NPAR = 0, 72, 80, 88, 96, 104, 107, 115, 119


def chunk_dmas(g):
    if G_PROJ <= g < G_WOUT and PROJ[g - G_PROJ] in ("qc", "kc"):
        return H_C
    return 2


def raw_need(g):
    return 16 * sum(chunk_dmas(x) for x in range(g % 2, g + 1, 2))


def build(nc, A, O):
    ctx = ExitStack()
    with ctx:
        names = {}

        def sb(name, shape, offset, dtype=F32):
            return nc.alloc_sbuf_tensor_at(name, shape, dtype, offset=offset)

        def sem(name):
            return ctx.enter_context(nc.semaphore(name))

        XB = 16512
        UB = XB + KD * T * 4
        RB = UB + 2 * KD * T * 4
        DG = RB + 6 * KD * CW * 4
        CB = DG + 81920
        xT = sb("xT", [P, KD, T], XB)
        u_hi = sb("u_hi", [P, KD, T], UB, F32R)
        u_lo = sb("u_lo", [P, KD, T], UB + KD * T * 4, F32R)
        raw = sb("raw", [P, 2, KD * CW], RB)
        w_hi = sb("w_hi", [P, 2, KD * CW], RB + 2 * KD * CW * 4, F32R)
        w_lo = sb("w_lo", [P, 2, KD * CW], RB + 4 * KD * CW * 4, F32R)
        h_hi = sb("h_hi", [P, 8, T], DG, F32R)
        h_lo = sb("h_lo", [P, 8, T], DG + 20480, F32R)
        G0 = DG + 40960
        silu_a = sb("silu_a", [P, 2, T], G0)
        h32 = sb("h32", [P, 2, T], G0 + 5120)
        sq = sb("sq", [P, 2, T], G0 + 10240)
        sqsum = sb("sqsum", [P, T], G0 + 15360)
        rstd = sb("rstd", [P, T], G0 + 17920)
        xn = sb("xn", [P, 2, T], G0 + 20480)
        u32 = sb("u32", [P, 2, T], G0 + 25600)
        stdv = sb("stdv", [P, T], G0 + 30720)
        mraw = sb("mraw", [P, NMC, KD, MW], DG)
        mrows = sb("mrows", [P, NMC, MW], DG + 65536)
        uraw = sb("uraw", [P, 2, KD, CW], G0 + 10240)
        urows = sb("urows", [P, 2, CW], G0 + 26624)
        xs = sb("xs", [P, NT, D], UB)
        yT = sb("yT", [P, KD, T], UB)
        ytm = sb("ytm", [P, 2, D], DG)
        omix = sb("omix", [P, NT, D], DG)
        qcT = sb("qcT", [P, 2, T], DG + 20480)
        kcT = sb("kcT", [P, 2, T], DG + 25600)
        glT = sb("glT", [2 * GR, T], DG + 30720)
        vcs = sb("vcs", [P, NT, WC], DG + 33280)
        rcs = sb("rcs", [P, NT, WC], DG + 40960)
        cqkv = sb("cqkv", [P, NT, 672], DG + 48640)
        qbT = sb("qbT", [P, 2, T], DG + 62080)
        kbT = sb("kbT", [P, 2, NKEY], DG + 67200)
        vbs = sb("vbs", [P, NKT, 288], DG + 73344)
        ck = sb("ck", [P, 256], DG + 80256)
        rotb = sb("rotb", [P, 2, TL], DG + 15360)
        GB = (DG, UB)
        gab = [sb(f"gab{d}", [P, 2, T], GB[d]) for d in range(2)]
        gb = [sb(f"gb{d}", [P, 2, T], GB[d] + 5120) for d in range(2)]
        gcum = [sb(f"gcum{d}", [P, 2, T], GB[d] + 10240) for d in range(2)]
        gqe = [sb(f"gqe{d}", [P, 2, T], GB[d] + 15360) for d in range(2)]
        gke, gkd = gcum, gab
        am = sb("am", [P, 2, 512], DG + 5120)
        kdt = sb("kdt", [P, NT, 2, P], UB + 20480)
        S = sb("S", [P, NCH, 2, DV_C], UB + 25600)
        S_FIN = (2, 1)
        oc = sb("oc", [P, NT, WC], UB + 33280)
        osq = sb("osq", [P, NT, WC], UB)
        qm = [[sb(f"qm{s}{j}", [P, T], UB + o) for j, o in enumerate(os)] for s, os in enumerate([(13824, 16384), (20480, 23040)])]
        p0 = [sb(f"p0_{s}", [P, T], UB + o) for s, o in enumerate((25600, 28160, 0))]
        pa = [sb(f"pa_{s}", [P, T], UB + o) for s, o in enumerate((25600, 28160, 33280))]
        p1 = [sb(f"p1_{s}", [P, T], UB + 30720 + 2560 * s) for s in range(2)]
        pt = [sb(f"pt_{s}", [P, NT, P], UB + 35840 + 2560 * s) for s in range(2)]
        cqT = sb("cqT", [P, 3, T], UB)
        ckvT = sb("ckvT", [P, 2, NKEY], UB + 7680)
        kA = [sb(f"kA{s}", [P, NKEY], UB + 13824 + 3072 * s) for s in range(2)]
        qA = [sb(f"qA{s}", [P, T], UB + 20480 + 2560 * s) for s in range(2)]
        rota = sb("rota", [P, TL], UB + 30720)
        wuq = sb("wuq", [P, 3, H_A * DQ], DG + 20480)
        wuk = sb("wuk", [P, 2, H_A * DN], DG + 27392)
        wuv = sb("wuv", [P, 2, WA], DG + 30464)
        vas = sb("vas", [P, NKT, 416], DG + 33536)
        krT = sb("krT", [DR, NKEY], DG + 43520)
        cc = sb("cc", [P, KV_RANK], DG + 46592)
        cck = sb("cck", [P, DR], DG + 47616)
        asq = sb("asq", [P, NT, WA], UB)
        off = [CB]

        def small(name, shape, dtype=F32):
            n = 4
            for s in shape[1:]:
                n *= s
            t = sb(name, shape, off[0], dtype)
            off[0] += (n + 31) // 32 * 32
            return t

        cosT, sinT = small("cosT", [P, TL]), small("sinT", [P, TL])
        ident, ones = small("ident", [P, P]), small("ones", [P, P])
        mask = small("mask", [P, 2, P])
        keep = small("keep", [P, 2, T])
        csp = small("csp", [P, KD, 32])
        comb = small("comb", [P, 2])
        modT = small("modT", [P, NMT, 2])
        gains = small("gains", [P, 3, KD, 2])
        gates = small("gates", [P, 3, KD, 2])
        par = small("par", [P, P])
        parT = small("parT", [P, P])
        grp = small("grp", [P, 4])
        lqk = small("lqk", [P, 4, DH_B])
        wgp = small("wgp", [2 * GR, 2, H_C * HW])
        Sini = small("Sini", [P, 2, 2, DV_C])
        kvw = small("kvw", [P, KV_RANK])
        st = small("st", [P, 96])
        gtot = [small(f"gtot{d}", [P, 2, NCH]) for d in range(2)]
        assert off[0] <= 229368, off[0]
        eps = st[:, 0:1]
        lam2, lexp, nlam = st[:, 1:3], st[:, 3:5], st[:, 5:6]
        lcon = st[:, 6:8]
        ldif = st[:, 8:9]
        css, crs = st[:, 10:30], st[:, 30:50]
        ss10, rs10 = st[:, 50:60], st[:, 60:70]
        ratio, aneg, asum, arec = st[:, 70:72], st[:, 74:78], st[:, 78:82], st[:, 82:90]
        ps = ctx.enter_context(nc.psum_tensor("ps", [P, 8, 512], F32))
        psf = ps[:, :, :].rearrange("p b n -> p (b n)")

        s_const = sem("s_const")
        s_tab = sem("s_tab")
        s_xs = sem("s_xs")
        s_ctp = sem("s_ctp")
        s_csil = sem("s_csil")
        s_xtp = sem("s_xtp")
        s_xa = sem("s_xa")
        s_xv = sem("s_xv")
        s_go = sem("s_go")
        s_yt = sem("s_yt")
        s_ytp = sem("s_ytp")
        s_ytm = sem("s_ytm")
        s_yout = [sem("s_yout0"), sem("s_yout1")]
        f_sq, f_sqd, f_sum, f_ss, f_std, f_xn = (sem("f_" + n) for n in ("sq", "sqd", "sum", "ss", "std", "xn"))
        par_in = sem("par_in")
        kv_in = sem("kv_in")
        aw_in = sem("aw_in")
        out_in = sem("out_in")
        layer_sems = []

        def lsem(name):
            s = sem(name)
            layer_sems.append(s)
            return s

        l_done = lsem("l_done")
        par_tp = lsem("par_tp")
        par_ok = lsem("par_ok")
        lam_s = lsem("lam_s")
        lam_e = lsem("lam_e")
        m_raw = [lsem(f"m_raw{i}") for i in range(NMC)]
        m_mm, m_row, m_tp, m_ev = lsem("m_mm"), lsem("m_row"), lsem("m_tp"), lsem("m_ev")
        mod_ok = lsem("mod_ok")
        v_in = [lsem("v_in0"), lsem("v_in1")]
        v_mm, v_row, v_ev = lsem("v_mm"), lsem("v_row"), lsem("v_ev")
        raw_in = [lsem("raw_in0"), lsem("raw_in1")]
        hi_ok, lo_ok = lsem("hi_ok"), lsem("lo_ok")
        mm_ok = lsem("mm_ok")
        ev_ok = lsem("ev_ok")
        sil_ok, h32_ok, hhi_ok, hlo_ok = lsem("sil_ok"), lsem("h32_ok"), lsem("hhi_ok"), lsem("hlo_ok")
        x_upd = lsem("x_upd")
        n_sq, n_sqd, n_sum, n_ss, n_std = (lsem("n_" + n) for n in ("sq", "sqd", "sum", "ss", "std"))
        n_xn, n_u32, n_uhi, n_ulo = (lsem("n_" + n) for n in ("xn", "u32", "uhi", "ulo"))
        dve_c = lsem("dve_c")
        act_c = lsem("act_c")
        pool_c = lsem("pool_c")
        bk_tp, bk_ev = lsem("bk_tp"), lsem("bk_ev")
        cq_ss, cq_sd, cq_ok = lsem("cq_ss"), lsem("cq_sd"), lsem("cq_ok")
        g_z, g_abs, g_min, g_ln, g_cum = (lsem("g_" + n) for n in ("z", "abs", "min", "ln", "cum"))
        g_e1, g_e2, g_bl, g_e3, g_qe, g_ke, g_kd = (lsem("g_" + n) for n in ("e1", "e2", "bl", "e3", "qe", "ke", "kd"))
        g_tp, g_tev, g_u, g_s = (lsem("g_" + n) for n in ("tp", "tev", "u", "s"))
        g_at, g_am, g_o, g_oev = (lsem("g_" + n) for n in ("at", "am", "o", "oev"))
        g_fin = lsem("g_fin")
        fin_out = lsem("fin_out")
        gn_v, gn_s, gn_ok = lsem("gn_v"), lsem("gn_s"), lsem("gn_ok")
        b_qm, b_sc, b_neg, b_exp, b_a, b_tp, b_pt, b_pv, b_o = (lsem("b_" + n) for n in ("qm", "sc", "neg", "exp", "a", "tp", "pt", "pv", "o"))
        ap_tp, ap_ev, ap_kr = lsem("ap_tp"), lsem("ap_ev"), lsem("ap_kr")
        x_mm, x_ev, a_qk = lsem("x_mm"), lsem("x_ev"), lsem("a_qk")
        a_sc, a_neg, a_exp, a_tp, a_pt, a_pv, a_o = (lsem("a_" + n) for n in ("sc", "neg", "exp", "tp", "pt", "pv", "o"))
        on_v, on_s, on_ok = lsem("on_v"), lsem("on_s"), lsem("on_ok")
        ot_tp, ot_hi, ot_lo = lsem("ot_tp"), lsem("ot_hi"), lsem("ot_lo")
        lo_n, hi_n = min(s.num for s in layer_sems), max(s.num for s in layer_sems)
        assert hi_n - lo_n + 1 == len(layer_sems)

        RANGES = [(0, 0, 0, 0, TC), (1, 0, TC, TC, TH - TC), (1, 1, 0, TH, TH)]
        U_ORDER = [[0, 1, 2, 3, 4, 5, 6, 7, 8], [1, 0, 9, 8, 7, 6, 5, 4, 3]]
        O_ORDER = [[0, 1, 2, 3, 4], [0, 4, 3, 2, 1]]
        N_STATE = len(U_ORDER[0])

        def state_count(d, c):
            if d == 0:
                return {0: 0, 2: 0}.get(c, c)
            return {1: 0, 9: 0, 0: 1}.get(c, 11 - c)

        def has_state(d, c):
            return c != (0, 1)[d]

        def entering(d, c):
            return Sini[:, d] if c == (2, 9)[d] else S[:, c]

        def heads_out(t):
            return oc[:, t, :].rearrange("p (a b v) -> p b a v", b=2, v=DV_C)

        def heads_ps():
            return ps[:, 4:6, 0:2 * DV_C].rearrange("p b (a v) -> p b a v", a=2)

        def keys_of(qi):
            return (0, 1) if qi == 0 else (1, NKT)

        cv = lambda ap: ap.bitcast(F32)

        block = ctx.enter_context(nc.Block())

        @block.sync
        def _(sp):
            sp.dma_start(cosT[:, :], A["rope_cos"]).then_inc(s_tab, 16)
            sp.dma_start(sinT[:, :], A["rope_sin"]).then_inc(s_tab, 16)
            sp.dma_start(par[0:KD, :], A["c_ctx"].rearrange("(k p) -> k p", p=P)).then_inc(s_tab, 16)
            sp.dma_start(par[KD:2 * KD, :], A["c"].rearrange("b (k p) -> (b k) p", p=P)).then_inc(s_tab, 16)
            sp.dma_start(xs[:, 0, :], A["x_prompt"][0]).then_inc(s_xs, 16)
            sp.dma_start(xs[:, 1:NT, :], A["x_sample"][0].rearrange("(t p) d -> p t d", p=P)).then_inc(s_xs, 16)
            sp.wait_ge(s_xa, KD // 2)
            sp.wait_ge(s_xv, KD // 2)

            with sp.Fori(0, DEPTH) as l:
                def slot(g):
                    return raw[:, g % 2, :].rearrange("p (k n) -> p k n", k=KD)

                def halves(dst, src, g):
                    n = dst.shape[1] // 2
                    for k in range(2):
                        sp.dma_start(dst[:, k * n:(k + 1) * n, :], src[:, k * n:(k + 1) * n, :]).then_inc(raw_in[g % 2], 16)

                def free(g, step=0):
                    if g >= 2:
                        sp.wait_ge(lo_ok, g - 1 + step)

                def load_up(w13, g, i, j, f0):
                    src = w13[l].rearrange("(k p) n -> p k n", p=P)
                    for s in range(2):
                        sp.dma_start(slot(g)[:, :, s * P:(s + 1) * P], src[:, :, bass.ds(i * 256 + (j * P + f0 + s * F), P)]).then_inc(raw_in[g % 2], 16)

                def load_down(w2, g, i, j, r0, n):
                    halves(slot(g)[:, 0:n, :], w2[l][r0:r0 + n * P, bass.ds(i * 512 + j * CW, CW)].rearrange("(k p) n -> p k n", p=P), g)

                def load_under(g, i):
                    c = g - G_MOD
                    if c >= 2:
                        sp.wait_ge(v_mm, i * 2 + (c - 1))
                    src = A["w_mod"][l][:, bass.ds(i * (2 * CW) + (2 * D + c * CW), CW)].rearrange("(k p) n -> p k n", p=P)
                    sp.dma_start(uraw[:, g % 2], src).then_inc(v_in[g % 2], 16)

                def load_ffn(w13, w2, g, first):
                    for q, n in enumerate(PARTS):
                        f0 = sum(PARTS[:q]) * P
                        start = 0
                        if q == 0:
                            for j in range(4):
                                free(g + j)
                                load_up(w13, g + j, 0, j, f0)
                            if first:
                                sp.wait_ge(n_ulo, KD)
                                for j in range(2):
                                    load_under(g + G_MOD + j, 0)
                            start = 2
                        with sp.Fori(0, n // 2 - start) as i:
                            for j in range(2):
                                free(g + 2 * start + j, i * 2)
                                load_up(w13, g + j, i, 2 * start + j, f0)
                                if first:
                                    load_under(g + 2 * start + j, i)
                        g += n
                        with sp.Fori(0, NW2 // 2) as i:
                            for j in range(2):
                                free(g + j, i * 2)
                                load_down(w2, g + j, i, j, f0, n)
                                if first and q < len(PARTS) - 1:
                                    load_under(g + j, i)
                        g += NW2

                for c in range(NMC):
                    src = A["w_mod"][l][:, c * MW:(c + 1) * MW].rearrange("(k p) n -> p k n", p=P)
                    sp.dma_start(mraw[:, c], src).then_inc(m_raw[c], 16)
                load_ffn(A["ffn1_w13"], A["ffn1_w2"], G_FFN1, True)
                win = A["w_in"][l].rearrange("(k p) n -> p k n", p=P)
                COL = {"vr0": O_VR, "vr1": O_VR + CW, "vr2": O_VR + 2 * CW, "vb": O_VB, "c0": 0, "c1": CW, "c2": 2 * CW,
                       "qb": O_QB, "kb": O_KB}
                for n, name in enumerate(PROJ):
                    g = G_PROJ + n
                    free(g)
                    if name == "gl":
                        halves(slot(g)[:, :, 0:2 * GR], win[:, :, O_GL:O_GL + 2 * GR], g)
                    elif name in ("qc", "kc"):
                        for h in range(H_C):
                            c0 = {"qc": O_QC, "kc": O_KC}[name] + h * DK
                            sp.dma_start(slot(g)[:, :, h * HW:(h + 1) * HW], win[:, :, c0:c0 + HW]).then_inc(raw_in[g % 2], 16)
                    else:
                        halves(slot(g), win[:, :, COL[name]:COL[name] + CW], g)
                wo = A["w_out"][l].rearrange("(k p) n -> p k n", p=P)
                for n in range(NW2):
                    g = G_WOUT + n
                    free(g)
                    halves(slot(g), wo[:, :, n * CW:(n + 1) * CW], g)
                load_ffn(A["ffn2_w13"], A["ffn2_w2"], G_FFN2, False)
                sp.wait_ge(l_done, 4)
                sp.sem_clear(range(lo_n, hi_n + 1))
                sp.sem_inc(s_go, 1)
            for t in range(NT):
                sp.wait_ge(s_ytm, t + 1)
                dst = O["y_prompt"][0] if t == 0 else O["y_sample"][0, (t - 1) * P:t * P, :]
                sp.dma_start(dst, ytm[:, t % 2, :]).then_inc(s_yout[t % 2], 16)
            sp.wait_ge(s_yout[0], 16 * 3)
            sp.wait_ge(s_yout[1], 16 * 2)

        @block.gpsimd
        def _(pool):
            n_const = [0]

            def made(ins):
                n_const[0] += 1
                ins.then_inc(s_const, 1)
                pool.wait_ge(s_const, n_const[0])

            made(pool.memset(ident[:, :], 0.0))
            made(pool.affine_select(out=ident[:, :], in_=ident[:, :], compare_op=ALU.not_equal, fill=1.0, base=0,
                                    pattern=[[-1, P]], channel_multiplier=1))
            made(pool.memset(ones[:, :], 1.0))
            made(pool.memset(mask[:, :, :], 1.0))
            made(pool.affine_select(out=mask[:, 0, :], in_=mask[:, 0, :], compare_op=ALU.is_ge, fill=0.0, base=0,
                                    pattern=[[1, P]], channel_multiplier=-1))
            made(pool.memset(mask[0:CH, 0, CH:P], 0.0))
            made(pool.affine_select(out=mask[:, 1, :], in_=mask[:, 1, :], compare_op=ALU.is_ge, fill=0.0, base=0,
                                    pattern=[[-1, P]], channel_multiplier=1))
            made(pool.memset(mask[CH:P, 1, 0:CH], 0.0))
            made(pool.memset(keep[:, :, :], 1.0))
            kc = keep[:, :, :].rearrange("p d (c t) -> p d c t", t=CH)
            made(pool.memset(kc[:, 0, :, 0:1], 0.0))
            made(pool.memset(kc[:, 1, :, CH - 1:CH], 0.0))
            made(pool.memset(comb[:, :], 0.0))
            for j in range(4):
                made(pool.affine_select(out=comb[:, :], in_=comb[:, :], compare_op=ALU.not_equal, fill=1.0, base=-32 * j,
                                        pattern=[[-1, 2]], channel_multiplier=1))
            made(pool.memset(grp[:, :], 0.0))
            for j in range(4):
                made(pool.memset(grp[32 * j:32 * j + 32, j:j + 1], 1.0))
            made(pool.memset(csp[:, :, :], 0.0))
            made(pool.memset(wgp[:, :, :], 0.0))
            made(pool.memset(Sini[:, :, :, :], 0.0))
            made(pool.memset(st[:, :], 0.0))
            made(pool.memset(eps, EPS))
            pool.wait_ge(s_ctp, 1)
            made(pool.memset(par[:, :], 0.0))

            with pool.Fori(0, DEPTH) as l:
                n_par = [0]

                def pin(dst, src):
                    n_par[0] += 1
                    pool.dma_start(dst, src).then_inc(par_in, 16)

                pin(par[R_BMOD:R_BMOD + NMT, :], A["b_mod"][l].rearrange("(r p) -> r p", p=P))
                pin(par[R_N1:R_N1 + KD, :], A["norm_ffn1"][l].rearrange("(r p) -> r p", p=P))
                pin(par[R_NM:R_NM + KD, :], A["norm_mix"][l].rearrange("(r p) -> r p", p=P))
                pin(par[R_N2:R_N2 + KD, :], A["norm_ffn2"][l].rearrange("(r p) -> r p", p=P))
                pin(par[R_FIN:R_FIN + KD, :], A["final_norm"].rearrange("(r p) -> r p", p=P))
                pin(par[R_QN:R_QN + 3, :], A["mla_q_norm"][l].rearrange("(r p) -> r p", p=P))
                pin(par[R_OG:R_OG + 3, :], A["mla_out_norm"][l].rearrange("(r p) -> r p", p=P))
                dn = A["diff_norm"][l].rearrange("(a n) -> a n", a=1)
                for r in range(2):
                    for c in range(2):
                        pin(par[R_OG + 3 + r:R_OG + 4 + r, c * DV_B:(c + 1) * DV_B], dn)
                gn = A["gla_norm"][l].rearrange("(a n) -> a n", a=1)
                at = 0
                while at < WC:
                    src0 = at % DV_C
                    n = min(DV_C - src0, P - at % P)
                    r = R_OG + 5 + at // P
                    pin(par[r:r + 1, at % P:at % P + n], gn[:, src0:src0 + n])
                    at += n
                for d, name in enumerate(("f", "b")):
                    bg = A["gla_bg_" + name][l].rearrange("(a n) -> a n", a=1)
                    wg = A["gla_wg_" + name][l]
                    for h in range(H_C):
                        n = min(HW, H_C * DK - h * DK)
                        r = R_BG + 2 * d + h // 2
                        pin(par[r:r + 1, (h % 2) * HW:(h % 2) * HW + n], bg[:, h * DK:h * DK + n])
                        pin(wgp[GR * d:GR * d + GR, d, h * HW:h * HW + n], wg[:, h * DK:h * DK + n])
                    s0 = A["state_gla_fwd" if d == 0 else "state_gla_bwd"][0, l].rearrange("(p h) k v -> h k p v", h=2)
                    for hh in range(2):
                        pin(Sini[HW * hh:HW * hh + DK, d, :, :], s0[hh])
                for n, name in enumerate(("diff_lq1", "diff_lk1", "diff_lq2", "diff_lk2")):
                    pin(lqk[:, n, :], A[name][l].rearrange("(a n) -> a n", a=1).broadcast_to([P, DH_B]))
                pin(kvw[:, :], A["mla_kv_norm"][l].rearrange("(a n) -> a n", a=1).broadcast_to([P, KV_RANK]))
                pin(lcon, A["layer_consts"][l])
                names["n_par"] = n_par[0]
                pool.dma_start(ck[:, :], A["cache_diff_k"][0, l].rearrange("t h d -> t (h d)")).then_inc(kv_in, 16)
                pool.wait_ge(n_ulo, 2 * KD)
                pool.dma_start(vbs[:, 1, 0:WB], A["cache_diff_v"][0, l].rearrange("t h d -> t (h d)")).then_inc(kv_in, 16)
                pool.memset(vbs[:, :, WB:288], 0.0).then_inc(pool_c, 1)
                pool.wait_ge(ev_ok, PROJ.index("vb") + 1)
                pool.dma_start(O["new_diff_v"][0, l].rearrange("t h d -> t (h d)"), vbs[:, 0, 0:WB]).then_inc(out_in, 16)
                pool.wait_ge(cq_ok, 1)
                pool.dma_start(O["new_mla_ckv"][0, l], cqkv[:, 0, Q_RANK:Q_RANK + KV_RANK]).then_inc(out_in, 16)
                pool.dma_start(O["new_mla_krope"][0, l], cqkv[:, 0, 640:672]).then_inc(out_in, 16)
                pool.wait_ge(bk_ev, 2)
                pool.dma_start(O["new_diff_k"][0, l].rearrange("t h d -> t (h d)"), ck[:, :]).then_inc(out_in, 16)
                for d in range(2):
                    dst = O["new_gla_fwd" if d == 0 else "new_gla_bwd"][0, l].rearrange("(p h) k v -> h k p v", h=2)
                    pool.wait_ge(g_fin, d + 1)
                    for hh in range(2):
                        pool.dma_start(dst[hh], S[HW * hh:HW * hh + DK, S_FIN[d], :, :]).then_inc(out_in, 16)
                    if d == 0:
                        pool.wait_ge(out_in, l * (16 * 8) + 16 * 6)
                        pool.sem_inc(fin_out, 1)
                pool.wait_ge(gn_ok, 1)
                pool.dma_start(wuq[:, :, :], A["mla_w_uq"][l].rearrange("(k p) n -> p k n", p=P)).then_inc(aw_in, 16)
                pool.dma_start(wuk[:, :, :], A["mla_w_uk"][l].rearrange("(k p) n -> p k n", p=P)).then_inc(aw_in, 16)
                pool.dma_start(wuv[:, :, :], A["mla_w_uv"][l].rearrange("(k p) n -> p k n", p=P)).then_inc(aw_in, 16)
                pool.dma_start(cc[:, :], A["cache_mla_ckv"][0, l]).then_inc(aw_in, 16)
                pool.dma_start(cck[:, :], A["cache_mla_krope"][0, l]).then_inc(aw_in, 16)
                pool.memset(vas[:, :, WA:416], 0.0).then_inc(pool_c, 1)
                pool.wait_ge(out_in, (l + 1) * (16 * 8))
                pool.wait_ge(pool_c, 2)
                pool.sem_inc(l_done, 1)
                pool.wait_ge(s_go, l + 1)

        @block.scalar
        def _(act):
            steps = [0]

            def link(ins):
                steps[0] += 1
                ins.then_inc(act_c, 1)
                act.wait_ge(act_c, steps[0])

            def hi(g, step=0):
                act.wait_ge(raw_in[g % 2], raw_need(g) + step * 16)
                if g >= 2:
                    act.wait_ge(mm_ok, g - 1 + step)
                act.activation(w_hi[:, g % 2, :], raw[:, g % 2, :], ACT.Copy).then_inc(hi_ok, 1)

            def norm(n, last_norm=False):
                for m in range(KD):
                    if n > 0:
                        act.wait_ge(x_upd, (0, 24, 32)[n] - KD + m + 1)
                    if m >= 2:
                        act.wait_ge(n_sqd, n * KD + m - 1)
                    act.activation(sq[:, m % 2, :], xT[:, m, :], ACT.Square).then_inc(n_sq, 1)
                act.wait_ge(n_ss, n + 1)
                act.activation(stdv[:, :].rearrange("p (b t) -> p b t", b=2), ps[:, 0:2, 0:TH], ACT.Sqrt,
                               bias=eps, scale=1.0 / D).then_inc(n_std, 1)
                sh = 3 * n * KD
                for m in range(KD + 1):
                    if m < KD:
                        act.wait_ge(n_xn, n * KD + m + 1)
                        if m >= 2:
                            act.wait_ge(n_ulo, n * KD + m - 1)
                        for c, t0, t1 in ((0, 0, TC), (1, TC, T)):
                            act.activation(u32[:, m % 2, t0:t1], xn[:, m % 2, t0:t1], ACT.Identity,
                                           bias=modT[:, sh + m, c:c + 1], scale=gains[:, n, m, c:c + 1]).then_inc(n_u32, 1)
                    if m >= 1:
                        act.wait_ge(n_u32, 2 * (n * KD + m))
                        act.activation(u_hi[:, m - 1, :], u32[:, (m - 1) % 2, :], ACT.Copy).then_inc(n_uhi, 1)

            def ffn(g, up0, last=False):
                for q, n in enumerate(PARTS):
                    with act.Fori(0, n // 2) as i:
                        for j in range(2):
                            k = up0 + j
                            act.wait_ge(mm_ok, g + j + 1 + i * 2)
                            if k >= 2:
                                act.wait_ge(h32_ok, k - 1 + i * 2)
                            act.activation(silu_a[:, j, :].rearrange("p (b t) -> p b t", b=2),
                                           ps[:, 4 * ((g + j) % 2):4 * ((g + j) % 2) + 2, 0:TH], ACT.Silu).then_inc(sil_ok, 1)
                            act.wait_ge(h32_ok, k + 1 + i * 2)
                            act.activation(h_hi[:, bass.ds(i * 2 + j, 1), :].rearrange("p a t -> p (a t)"), h32[:, j, :],
                                           ACT.Copy).then_inc(hhi_ok, 1)
                            hi(g + j + 2, i * 2)
                    g += n
                    up0 += n
                    stop = last and q == len(PARTS) - 1
                    if stop:
                        for j in range(2):
                            act.wait_ge(mm_ok, g + j + 1)
                            hi(g + j + 2)
                    else:
                        with act.Fori(0, NW2 // 2) as i:
                            for j in range(2):
                                act.wait_ge(mm_ok, g + j + 1 + i * 2)
                                hi(g + j + 2, i * 2)
                    g += NW2

            act.wait_ge(s_ctp, 1)
            act.activation(csp[:, :, 0:2].rearrange("p k c -> p c k"), ps[:, 0, 0:2 * KD].rearrange("p (c k) -> p c k", c=2),
                           ACT.Silu).then_inc(s_csil, 1)
            for m in range(KD):
                if m % 2:
                    continue
                act.wait_ge(s_xtp, m + 1)
                b = 2 * (m % 4)
                act.activation(xT[:, m, :], psf[:, b * 512:b * 512 + T], ACT.Copy).then_inc(s_xa, 1)

            with act.Fori(0, DEPTH) as l:
                steps[0] = 0
                act.wait_ge(lam_s, 1)
                act.activation(lexp, lam2, ACT.Exp).then_inc(lam_e, 1)
                for c in range(NMC):
                    act.wait_ge(m_mm, c + 1)
                    act.activation(mrows[:, c, :], ps[:, c, :], ACT.Copy).then_inc(m_row, 1)
                hi(0)
                hi(1)
                act.wait_ge(mod_ok, 1)
                norm(0)
                ffn(G_FFN1, 0)
                act.wait_ge(mod_ok, 2)
                norm(1)
                def gate_logs(d):
                    act.wait_ge(g_min, d + 1)
                    link(act.activation(gab[d][:, :, :], gb[d][:, :, :], ACT.Abs))
                    link(act.activation(gab[d][:, :, :], gab[d][:, :, :], ACT.Exp, scale=-1.0))
                    act.activation(gab[d][:, :, :], gab[d][:, :, :], ACT.Ln, bias=1.0).then_inc(g_ln, 1)

                def gate_exps(d):
                    act.wait_ge(g_cum, d + 1)
                    act.activation(gqe[d][:, :, :], gcum[d][:, :, :], ACT.Exp, scale=1.0 / GATE_NORM).then_inc(g_e1, 1)
                    tot = gcum[d][:, :, :].rearrange("p a (c t) -> p a c t", t=CH)[:, :, :, (CH - 1, 0)[d]]
                    link(act.activation(gtot[d][:, :, :], tot, ACT.Exp, scale=1.0 / GATE_NORM))
                    act.wait_ge(g_bl, d + 1)
                    act.activation(gkd[d][:, :, :], gb[d][:, :, :], ACT.Exp, scale=1.0 / GATE_NORM).then_inc(g_e3, 1)
                    link(act.activation(gke[d][:, :, :], gcum[d][:, :, :], ACT.Exp, scale=-1.0 / GATE_NORM))
                    act.sem_inc(g_e2, 1)

                for n, name in enumerate(PROJ):
                    g = G_PROJ + n
                    b = 4 * (g % 2)
                    act.wait_ge(mm_ok, g + 1)
                    four = ps[:, b:b + 4, 0:TH]
                    tm = psf[:, b * 512:b * 512 + NT * CW].rearrange("p (t n) -> p t n", n=CW)
                    if name == "gl":
                        act.activation(glT[:, :].rearrange("p (b t) -> p b t", b=2), ps[0:2 * GR, b:b + 2, 0:TH], ACT.Copy).then_inc(ev_ok, 1)
                    elif name in ("qc", "kc", "qb"):
                        dst = {"qc": qcT, "kc": kcT, "qb": qbT}[name]
                        act.activation(dst[:, :, :].rearrange("p m (b t) -> p (m b) t", b=2), four, ACT.Copy).then_inc(ev_ok, 1)
                    elif name == "kb":
                        f2 = ps[:, b:b + 4, :].rearrange("p (m b) t -> p m b t", b=2)
                        act.activation(kbT[:, :, 0:TC], f2[:, :, 0, 0:TC], ACT.Copy)
                        act.activation(kbT[:, :, TC + PAST:PAST + TH], f2[:, :, 0, TC:TH], ACT.Copy)
                        act.activation(kbT[:, :, PAST + TH:NKEY], f2[:, :, 1, 0:TH], ACT.Copy).then_inc(ev_ok, 1)
                    elif name == "vr0":
                        act.wait_ge(cq_ss, 1)
                        act.activation(vcs[:, :, 0:CW], tm, ACT.Copy).then_inc(ev_ok, 1)
                    elif name == "vr1":
                        act.activation(vcs[:, :, CW:WC], tm[:, :, 0:P], ACT.Copy)
                        act.activation(rcs[:, :, 0:P], tm[:, :, P:CW], ACT.Silu).then_inc(ev_ok, 1)
                    elif name == "vr2":
                        act.activation(rcs[:, :, P:WC], tm, ACT.Silu).then_inc(ev_ok, 1)
                    elif name == "vb":
                        act.activation(vbs[:, 0, 0:WB], tm[:, 0, :], ACT.Copy)
                        act.activation(vbs[:, 2:NKT, 0:WB], tm[:, 1:NT, :], ACT.Copy).then_inc(ev_ok, 1)
                    else:
                        c0 = int(name[1]) * CW
                        w = min(CW, 672 - c0)
                        act.activation(cqkv[:, :, c0:c0 + w], tm[:, :, 0:w], ACT.Copy).then_inc(ev_ok, 1)
                    hi(g + 2)
                    if n == Z_AT:
                        gate_logs(0)
                    elif name == "kc":
                        gate_exps(0)
                    elif name == "c2":
                        act.wait_ge(ev_ok, n + 1)
                        for t in range(NT):
                            act.activation(vcs[:, t, 0:Q_RANK], cqkv[:, t, 0:Q_RANK], ACT.Square, accum_out=ss10[:, t:t + 1])
                            last = act.activation(rcs[:, t, 0:KV_RANK], cqkv[:, t, Q_RANK:640], ACT.Square, accum_out=ss10[:, NT + t:NT + t + 1])
                        last.then_inc(cq_ss, 1)
                        act.wait_ge(cq_ss, 1)
                        act.activation(rs10[:, 0:NT], ss10[:, 0:NT], ACT.Sqrt, bias=eps, scale=1.0 / Q_RANK)
                        act.activation(rs10[:, NT:2 * NT], ss10[:, NT:2 * NT], ACT.Sqrt, bias=eps, scale=1.0 / KV_RANK).then_inc(cq_ss, 1)
                def turned_keys(d):
                    for t in range(NT):
                        act.wait_ge(g_tp, d * NT + t + 1)
                        act.activation(kdt[:, t, :, :], ps[:, 4 + t % 2, 0:256].rearrange("p (a k) -> p a k", a=2), ACT.Copy).then_inc(g_tev, 1)

                turned_keys(0)
                act.wait_ge(bk_tp, 1)
                act.activation(kbT[:, :, TC:TC + PAST], ps[:, 6, 0:256].rearrange("p (m t) -> p m t", m=2), ACT.Copy).then_inc(bk_ev, 1)
                act.wait_ge(bk_tp, 2)
                act.activation(ck[:, :], ps[:, 7, 0:256], ACT.Copy).then_inc(bk_ev, 1)
                gate_logs(1)
                gate_exps(1)
                for n, t in enumerate(O_ORDER[0]):
                    act.wait_ge(g_o, n + 1)
                    act.activation(heads_out(t), heads_ps(), ACT.Copy).then_inc(g_oev, 1)
                turned_keys(1)
                act.wait_ge(gn_v, 1)
                act.activation(crs, css, ACT.Sqrt, bias=eps, scale=1.0 / DV_C).then_inc(gn_s, 1)
                NB = H_B * NT

                def scores_view(s, qi):
                    if qi == 0:
                        return ps[:, s, 0:P], lambda tile: tile[:, 0:P]
                    return ps[:, s:s + 2, 0:TH], lambda tile: tile[:, :].rearrange("p (b t) -> p b t", b=2)

                def turn_copy(n, s_tp, s_pv, s_pt):
                    nk = 1 if n % NT == 0 else NT
                    act.wait_ge(s_tp, n + 1)
                    if n >= 2:
                        act.wait_ge(s_pv, n - 1)
                    act.activation(pt[n % 2][:, 0:nk, :].rearrange("p a t -> p (a t)"), psf[:, 4 * 512:4 * 512 + nk * P], ACT.Copy).then_inc(s_pt, 1)

                act.wait_ge(out_in, (l + 1) * (16 * 8))
                for n in range(NB + 2):
                    if n < NB:
                        for j in range(2):
                            act.wait_ge(b_neg, 2 * n + j + 1)
                            if n >= 3 and j == 0:
                                act.wait_ge(b_tp, n - 2)
                            if n >= 2:
                                act.wait_ge(b_a, n - 1)
                            src, view = scores_view(2 * j, n % NT)
                            c = 2 * (n % 2) + j
                            act.activation(view(p1[n % 2] if j else p0[n % 3]), src, ACT.Exp, bias=aneg[:, c:c + 1],
                                           accum_out=asum[:, c:c + 1]).then_inc(b_exp, 1)
                    if n >= 2:
                        turn_copy(n - 2, b_tp, b_pv, b_pt)
                for s in range(6):
                    act.wait_ge(ap_tp, s + 1)
                    b = 2 * (s % 4) * 512
                    if s < 3:
                        ins = act.activation(cqT[:, s, :], psf[:, b:b + T], ACT.Copy, scale=parT[:, R_QN + s:R_QN + s + 1])
                    elif s < 5:
                        ins = act.activation(ckvT[:, s - 3, :], psf[:, b:b + NKEY], ACT.Copy)
                    else:
                        ins = act.activation(krT[:, :], psf[0:DR, b:b + NKEY], ACT.Copy)
                    ins.then_inc(ap_ev, 1)
                for t in range(NKT):
                    act.wait_ge(ap_tp, 6 + t + 1)
                    act.activation(vas[:, t, 0:WA], ps[:, t, 0:WA], ACT.Copy).then_inc(ap_ev, 1)
                SA = DQ ** -0.5
                NA = H_A * NT

                def head_piece(r):
                    h, k = r // 4, r % 4
                    if h >= 2:
                        act.wait_ge(a_sc, (h - 1) * NT)
                    act.wait_ge(x_mm, r + 1)
                    if k < 2:
                        ins = act.activation(qA[h % 2][0:DQ, k * TH:(k + 1) * TH], ps[0:DQ, 7, 0:TH], ACT.Copy, scale=SA)
                    else:
                        c0 = (k - 2) * (NKEY // 2)
                        ins = act.activation(kA[h % 2][0:DN, c0:c0 + NKEY // 2], ps[0:DN, 7, 0:NKEY // 2], ACT.Copy)
                    ins.then_inc(x_ev, 1)

                for r in range(4):
                    head_piece(r)
                for n in range(NA + 2):
                    h, qi = n // NT, n % NT
                    if n < NA:
                        act.wait_ge(a_neg, n + 1)
                        if n >= 3:
                            act.wait_ge(a_tp, n - 2)
                        src, view = scores_view(2 * (n % 2), qi)
                        act.activation(view(pa[n % 3]), src, ACT.Exp, bias=aneg[:, n % 2:n % 2 + 1],
                                       accum_out=asum[:, n % 2:n % 2 + 1]).then_inc(a_exp, 1)
                    if n >= 2:
                        turn_copy(n - 2, a_tp, a_pv, a_pt)
                    if qi < 4 and h < H_A - 1:
                        head_piece(4 * (h + 1) + qi)
                act.wait_ge(on_v, 1)
                act.activation(rs10[:, 0:NT], ss10[:, 0:NT], ACT.Sqrt, bias=eps, scale=1.0 / WA)
                act.activation(crs, css, ACT.Sqrt, bias=eps, scale=1.0 / DV_B).then_inc(on_s, 1)
                for k in range(KD):
                    act.wait_ge(ot_tp, k + 1)
                    b = 2 * (k % 4) * 512
                    act.activation(u_hi[:, k, :], psf[:, b:b + T], ACT.Copy, scale=parT[:, R_OG + k:R_OG + k + 1]).then_inc(ot_hi, 1)
                for n in range(NW2):
                    g = G_WOUT + n
                    act.wait_ge(mm_ok, g + 1)
                    hi(g + 2)
                norm(2)
                ffn(G_FFN2, NF, last=True)
                act.drain().then_inc(l_done, 1)
                act.wait_ge(s_go, l + 1)
            for m in range(KD):
                if m >= 2:
                    act.wait_ge(f_sqd, m - 1)
                act.activation(sq[:, m % 2, :], xT[:, m, :], ACT.Square).then_inc(f_sq, 1)
            act.wait_ge(f_ss, 1)
            act.activation(stdv[:, :].rearrange("p (b t) -> p b t", b=2), ps[:, 0:2, 0:TH], ACT.Sqrt, bias=eps, scale=1.0 / D).then_inc(f_std, 1)
            for m in range(KD):
                act.wait_ge(f_xn, m + 1)
                act.activation(yT[:, m, :], xn[:, m % 2, :], ACT.Copy, scale=parT[:, R_FIN + m:R_FIN + m + 1]).then_inc(s_yt, 1)
            for t in range(NT):
                act.wait_ge(s_ytp, t + 1)
                if t >= 2:
                    act.wait_ge(s_yout[t % 2], 16 * (t // 2))
                b = 2 * (t % 4) * 512
                act.activation(ytm[:, t % 2, :], psf[:, b:b + D], ACT.Copy).then_inc(s_ytm, 1)

        @block.vector
        def _(dve):
            steps = [0]

            def link(ins):
                steps[0] += 1
                ins.then_inc(dve_c, 1)
                dve.wait_ge(dve_c, steps[0])

            def lo(g, step=0):
                dve.wait_ge(hi_ok, g + 1 + step)
                dve.tensor_tensor(w_lo[:, g % 2, :], raw[:, g % 2, :], cv(w_hi[:, g % 2, :]), ALU.subtract).then_inc(lo_ok, 1)

            def norm(n):
                for m in range(KD):
                    dve.wait_ge(n_sq, n * KD + m + 1)
                    if m == 0:
                        dve.tensor_copy(sqsum[:, :], sq[:, 0, :]).then_inc(n_sqd, 1)
                    else:
                        dve.wait_ge(n_sqd, n * KD + m)
                        dve.tensor_tensor(sqsum[:, :], sqsum[:, :], sq[:, m % 2, :], ALU.add).then_inc(n_sqd, 1)
                dve.wait_ge(n_std, n + 1)
                link(dve.reciprocal(rstd[:, :], stdv[:, :]))
                for m in range(KD + 1):
                    if m < KD:
                        if m >= 2:
                            dve.wait_ge(n_u32, 2 * (n * KD + m - 1))
                        dve.tensor_tensor(xn[:, m % 2, :], xT[:, m, :], rstd[:, :], ALU.mult).then_inc(n_xn, 1)
                    if m >= 1:
                        dve.wait_ge(n_uhi, n * KD + m)
                        dve.tensor_tensor(u_lo[:, m - 1, :], u32[:, (m - 1) % 2, :], cv(u_hi[:, m - 1, :]), ALU.subtract).then_inc(n_ulo, 1)

            def update_x(kind, bank, m, dyn):
                for n, (c, b, o, t0, w) in enumerate(RANGES):
                    xa = xT[:, bass.ds(m, 1), t0:t0 + w].rearrange("p a t -> p (a t)") if dyn else xT[:, m, t0:t0 + w]
                    ga = gates[:, kind, bass.ds(m, 1), c:c + 1].rearrange("p a c -> p (a c)") if dyn else gates[:, kind, m, c:c + 1]
                    last = dve.scalar_tensor_tensor(out=xa, in0=ps[:, bank + b, o:o + w], scalar=ga, in1=xa, op0=ALU.mult, op1=ALU.add)
                return last

            def mod_under(g, i=0):
                c = g - G_MOD
                if 0 <= c < N_UNDER:
                    dve.tensor_copy(urows[:, g % 2, :].rearrange("p (b n) -> p b n", b=2),
                                    ps[:, 4 * (g % 2) + 2:4 * (g % 2) + 4, TH:TH + P]).then_inc(v_row, 1)
                if 2 <= c < N_UNDER + 2:
                    r0 = i * 4 + (2 * KD + 2 * (c - 2))
                    dve.tensor_tensor(modT[:, bass.ds(r0, 2), :], ps[:, 4 * (g % 2) + 2, TH + P:TH + P + 4].rearrange("p (r c) -> p r c", c=2),
                                      parT[:, bass.ds(r0, 2)].unsqueeze(2).broadcast_to([P, 2, 2]), ALU.add).then_inc(v_ev, 1)

            def ffn(g, up0, kind, x0, last=False):
                first = kind == 0
                for q, n in enumerate(PARTS):
                    def up_step(j, k, i):
                        b = 4 * ((g + j) % 2)
                        dve.wait_ge(sil_ok, k + 1 + i * 2)
                        if k >= 2:
                            dve.wait_ge(hlo_ok, k - 1 + i * 2)
                        if first:
                            mod_under(g + j, i)
                        dve.tensor_tensor(h32[:, j % 2, :].rearrange("p (b t) -> p b t", b=2), ps[:, b + 2:b + 4, 0:TH],
                                          silu_a[:, j % 2, :].rearrange("p (b t) -> p b t", b=2), ALU.mult).then_inc(h32_ok, 1)
                        dve.wait_ge(hhi_ok, k + 1 + i * 2)
                        tile = bass.ds(i * 2 + j, 1)
                        dve.tensor_tensor(h_lo[:, tile, :].rearrange("p a t -> p (a t)"), h32[:, j % 2, :],
                                          cv(h_hi[:, tile, :]).rearrange("p a t -> p (a t)"), ALU.subtract).then_inc(hlo_ok, 1)
                        lo(g + j + 2, i * 2)

                    start = 0
                    if q == 0:
                        for j in range(4):
                            up_step(j, up0 + j, 0)
                        start = 4
                    with dve.Fori(0, (n - start) // 2) as i:
                        for j in range(start, start + 2):
                            up_step(j, up0 + j, i)
                    g += n
                    up0 += n
                    if q == 0 and first:
                        dve.wait_ge(v_ev, KD // 2)
                        link(dve.tensor_scalar(gates[:, 0], modT[:, 2 * KD:3 * KD, :], 0.5, None, ALU.mult))
                    if x0 > 0 or q > 0:
                        dve.wait_ge(x_upd, x0)
                    with dve.Fori(0, NW2 // 2 - (1 if q == len(PARTS) - 1 else 0)) as i:
                        for j in range(2):
                            dve.wait_ge(mm_ok, g + j + 1 + i * 2)
                            if first:
                                mod_under(g + j, i)
                            for m2 in range(2):
                                update_x(kind, 4 * ((g + j) % 2) + 2 * m2, i * 4 + (2 * j + m2), True).then_inc(x_upd, 1)
                            lo(g + j + 2, i * 2)
                    if q == len(PARTS) - 1:
                        for j in range(2):
                            dve.wait_ge(mm_ok, g + j + 3)
                            for m2 in range(2):
                                update_x(kind, 4 * ((g + j) % 2) + 2 * m2, 4 + 2 * j + m2, False).then_inc(x_upd, 1)
                            if not last:
                                lo(g + j + 4)
                    g += NW2
                    x0 += KD

            def rope(x, rot, cos, sin, lk):
                swap = [i + 8 if i % 16 < 8 else i - 8 for i in range(32)]
                lk(dve.stream_shuffle(rot, x, swap))
                dve.tensor_tensor(x, x, cos, ALU.mult)
                lk(dve.tensor_tensor(rot, rot, sin, ALU.mult))
                return dve.tensor_tensor(x, x, rot, ALU.add)

            dve.wait_ge(s_const, 1)
            for m in range(KD):
                if m % 2 == 0:
                    continue
                dve.wait_ge(s_xtp, m + 1)
                b = 2 * (m % 4)
                dve.tensor_copy(xT[:, m, :], psf[:, b * 512:b * 512 + T]).then_inc(s_xv, 1)

            with dve.Fori(0, DEPTH) as l:
                steps[0] = 0
                dve.wait_ge(par_in, (l + 1) * (16 * names["n_par"]))
                for n in range(2):
                    last = dve.tensor_tensor_reduce(out=lqk[:, 2 * n, :], in0=lqk[:, 2 * n, :], in1=lqk[:, 2 * n + 1, :], scale=1.0,
                                                    scalar=0.0, op0=ALU.mult, op1=ALU.add, accum_out=lam2[:, n:n + 1])
                last.then_inc(lam_s, 1)
                dve.wait_ge(par_tp, 1)
                dve.tensor_copy(parT[:, 0:P], ps[:, 7, 0:P]).then_inc(par_ok, 1)
                dve.wait_ge(par_ok, 1)
                dve.wait_ge(lam_e, 1)
                link(dve.tensor_tensor(ldif, lexp[:, 1:2], lexp[:, 0:1], ALU.subtract))
                dve.tensor_tensor(nlam, ldif, lcon[:, 0:1], ALU.subtract)
                link(dve.tensor_scalar(parT[:, R_OG + 3:R_OG + 5], parT[:, R_OG + 3:R_OG + 5], lcon[:, 1:2], None, ALU.mult))

                for c in range(NMC):
                    n = MW // P
                    dve.wait_ge(m_tp, c + 1)
                    dve.tensor_tensor(modT[:, c * n:(c + 1) * n, :], ps[:, 4 + c, 0:2 * n].rearrange("p (r c) -> p r c", c=2),
                                      parT[:, c * n:(c + 1) * n].unsqueeze(2).broadcast_to([P, n, 2]), ALU.add).then_inc(m_ev, 1)
                dve.wait_ge(m_ev, NMC)

                def gain(n, r):
                    w = parT[:, r:r + KD].unsqueeze(2).broadcast_to([P, KD, 2])
                    return dve.scalar_tensor_tensor(out=gains[:, n], in0=modT[:, (3 * n + 1) * KD:(3 * n + 2) * KD, :], scalar=1.0, in1=w,
                                                    op0=ALU.add, op1=ALU.mult)

                gain(0, R_N1).then_inc(mod_ok, 1)
                lo(0)
                lo(1)
                norm(0)
                ffn(G_FFN1, 0, 0, 0)
                dve.wait_ge(v_ev, N_UNDER)
                gain(1, R_NM)
                gain(2, R_N2)
                for n in (1, 2):
                    last = dve.tensor_scalar(gates[:, n], modT[:, (3 * n + 2) * KD:(3 * n + 3) * KD, :], (1.0, 0.5)[n - 1], None, ALU.mult)
                link(last)
                dve.sem_inc(mod_ok, 1)
                norm(1)
                cos2 = cosT[:, :].unsqueeze(1).broadcast_to([P, 2, TL])
                sin2 = sinT[:, :].unsqueeze(1).broadcast_to([P, 2, TL])

                def gate_bias(d):
                    dve.wait_ge(g_z, d + 1)
                    for p in range(2):
                        last = dve.tensor_scalar(gb[d][:, p, :].rearrange("p (b t) -> p b t", b=2), ps[:, (4, 0)[d] + 2 * p:(4, 0)[d] + 2 * p + 2, 0:TH],
                                                 parT[:, R_BG + 2 * d + p:R_BG + 2 * d + p + 1], None, ALU.add)
                    last.then_inc(g_min, 1)

                def gate_sums(d):
                    rev = slice(None, None, -1) if d else slice(None)
                    dve.wait_ge(g_ln, d + 1)
                    link(dve.scalar_tensor_tensor(out=gb[d][:, :, :], in0=gb[d][:, :, :], scalar=0.0, in1=gab[d][:, :, :], op0=ALU.min, op1=ALU.subtract))
                    for p in range(2):
                        last = dve.tensor_tensor_scan(gcum[d][:, p, rev], keep[:, d, rev], gb[d][:, p, rev], 0.0, ALU.mult, ALU.add)
                    last.then_inc(g_cum, 1)
                    dve.wait_ge(g_cum, d + 1)
                    c4 = gcum[d][:, :, :].rearrange("p a (c t) -> p (a c) t", t=CH)
                    e = (CH - 1, 0)[d]
                    dve.tensor_tensor(gb[d][:, :, :].rearrange("p a (c t) -> p (a c) t", t=CH),
                                      c4[:, :, e:e + 1].broadcast_to([P, 2 * NCH, CH]), c4, ALU.subtract).then_inc(g_bl, 1)

                def decay(d, step):
                    if step == 0:
                        dve.wait_ge(g_e1, d + 1)
                        dve.scalar_tensor_tensor(out=gqe[d][:, :, :], in0=qcT[:, :, :], scalar=DK ** -0.5, in1=gqe[d][:, :, :],
                                                 op0=ALU.mult, op1=ALU.mult).then_inc(g_qe, 1)
                    elif step == 1:
                        dve.wait_ge(g_e3, d + 1)
                        dve.tensor_tensor(gkd[d][:, :, :], kcT[:, :, :], gkd[d][:, :, :], ALU.mult).then_inc(g_kd, 1)
                    else:
                        dve.wait_ge(g_e2, d + 1)
                        dve.tensor_tensor(gke[d][:, :, :], kcT[:, :, :], gke[d][:, :, :], ALU.mult).then_inc(g_ke, 1)

                for n, name in enumerate(PROJ):
                    if n == Z_AT:
                        gate_bias(0)
                    lo(G_PROJ + n + 2)
                    if name in ("kb", "qb"):
                        dve.wait_ge(ev_ok, n + 1)
                        link(rope({"kb": kbT[:, :, TC + PAST:NKEY], "qb": qbT[:, :, TC:T]}[name], rotb[:, :, :], cos2, sin2, link))
                    elif name == "qc":
                        gate_sums(0)
                    elif name == "kc":
                        dve.wait_ge(ev_ok, n + 1)
                        for step in range(3):
                            decay(0, step)
                    elif name == "c2":
                        dve.wait_ge(cq_ss, 2)
                        link(dve.reciprocal(ss10, rs10))
                        for t in range(NT):
                            dve.tensor_scalar(cqkv[:, t, 0:Q_RANK], cqkv[:, t, 0:Q_RANK], ss10[:, t:t + 1], None, ALU.mult)
                            last = dve.tensor_scalar(cqkv[:, t, Q_RANK:640], cqkv[:, t, Q_RANK:640], ss10[:, NT + t:NT + t + 1], None, ALU.mult)
                        link(last)
                        kv = cqkv[:, :, Q_RANK:640]
                        dve.tensor_tensor(kv, kv, kvw[:, :].unsqueeze(1).broadcast_to([P, NT, KV_RANK]), ALU.mult).then_inc(cq_ok, 1)

                def states(d):
                    for n, c in enumerate(U_ORDER[d]):
                        dve.wait_ge(g_u, d * N_STATE + n + 1)
                        upd = ps[:, 6 + n % 2, 0:2 * DV_C].rearrange("p (a v) -> p a v", a=2)
                        nxt = S_FIN[d] if n == 1 else c + (1, -1)[d]
                        if d == 1 and n >= 2 and nxt == S_FIN[0]:
                            dve.wait_ge(fin_out, 1)
                        if n == 0:
                            dve.tensor_copy(S[:, nxt], upd).then_inc(g_s, 1)
                            continue
                        dve.wait_ge(g_s, d * N_STATE + n)
                        src = entering(d, c)
                        for a in range(2):
                            last = dve.scalar_tensor_tensor(out=S[:, nxt, a, :], in0=src[:, a, :], scalar=gtot[d][:, a, c:c + 1], in1=upd[:, a, :],
                                                            op0=ALU.mult, op1=ALU.add)
                        last.then_inc(g_s, 1)
                        if n == 1:
                            dve.wait_ge(g_s, d * N_STATE + 2)
                            dve.sem_inc(g_fin, 1)

                def masked(d, n):
                    dve.wait_ge(g_at, d * NT + n + 1)
                    if d * NT + n >= 2:
                        dve.wait_ge(g_o, d * NT + n - 1)
                    b = 2 * (n % 2)
                    dve.tensor_tensor(am[:, n % 2, :].rearrange("p (b a t) -> p b a t", b=2, a=2),
                                      ps[:, b:b + 2, 0:2 * P].rearrange("p b (a t) -> p b a t", a=2),
                                      mask[:, d, :].unsqueeze(1).unsqueeze(1).broadcast_to([P, 2, 2, P]), ALU.mult).then_inc(g_am, 1)

                def add_back(n):
                    t = O_ORDER[1][n]
                    dve.wait_ge(g_o, NT + n + 1)
                    dve.tensor_tensor(heads_out(t), heads_ps(), heads_out(t), ALU.add).then_inc(g_oev, 1)

                gate_bias(1)
                states(0)
                gate_sums(1)
                for n in range(NT):
                    masked(0, n)
                    if 1 <= n <= 3:
                        decay(1, n - 1)
                states(1)
                for n in range(NT):
                    masked(1, n)
                    if n >= 1:
                        add_back(n - 1)
                add_back(NT - 1)
                dve.wait_ge(g_oev, 2 * NT)
                link(dve.tensor_tensor(osq[:, :, :], oc[:, :, :], oc[:, :, :], ALU.mult))
                dve.tensor_reduce(css.rearrange("p (t h) -> p t h", h=H_C), osq[:, :, :].rearrange("p t (h v) -> p t h v", h=H_C), AX.X, ALU.add).then_inc(gn_v, 1)
                dve.wait_ge(gn_s, 1)
                link(dve.reciprocal(css, crs))
                och = oc[:, :, :].rearrange("p t (h v) -> p t h v", h=H_C)
                link(dve.tensor_tensor(och, och, css.rearrange("p (t h) -> p t h", h=H_C).unsqueeze(3).broadcast_to([P, NT, H_C, DV_C]), ALU.mult))
                dve.tensor_tensor(omix[:, :, WA + WB:D], oc[:, :, :], rcs[:, :, :], ALU.mult).then_inc(gn_ok, 1)
                NB = H_B * NT

                def scores(s, qi):
                    return ps[:, s, 0:P] if qi == 0 else ps[:, s:s + 2, 0:TH]

                def top(s, qi, c):
                    return dve.tensor_reduce(aneg[:, c:c + 1], scores(s, qi), AX.X if qi == 0 else AX.XY, ALU.max, negate=True)

                for n in range(NB + 4):
                    h, qi = n // NT, n % NT
                    if n >= 4:
                        m = n - 4
                        dve.wait_ge(b_pv, m + 1)
                        c0 = WA + (m // NT) * DV_B
                        dve.tensor_scalar(omix[:, m % NT, c0:c0 + DV_B], ps[:, 6, 0:DV_B],
                                          arec[:, 2 * (m % 4):2 * (m % 4) + 1], None, ALU.mult).then_inc(b_o, 1)
                    if n < NB:
                        if qi == 0:
                            if h >= 2:
                                dve.wait_ge(b_sc, 2 * NT * (h - 1))
                            for j in range(2):
                                r = 2 * h + j
                                last = dve.tensor_scalar(qm[h % 2][j][:, :], qbT[:, r // 4, :], grp[:, r % 4:r % 4 + 1], DH_B ** -0.5, ALU.mult, ALU.mult)
                            last.then_inc(b_qm, 1)
                        for j in range(2):
                            dve.wait_ge(b_sc, 2 * n + j + 1)
                            top(2 * j, qi, 2 * (n % 2) + j).then_inc(b_neg, 1)
                    if 1 <= n <= NB:
                        m = n - 1
                        w = P if m % NT == 0 else T
                        c, r = 2 * (m % 2), 2 * (m % 4)
                        dve.wait_ge(b_exp, 2 * m + 2)
                        link(dve.reciprocal(arec[:, r:r + 2], asum[:, c:c + 2]))
                        link(dve.scalar_tensor_tensor(out=ratio[:, m % 2:m % 2 + 1], in0=asum[:, c:c + 1], scalar=arec[:, r + 1:r + 2], in1=nlam,
                                                      op0=ALU.mult, op1=ALU.mult))
                        dve.scalar_tensor_tensor(out=p0[m % 3][:, 0:w], in0=p1[m % 2][:, 0:w], scalar=ratio[:, m % 2:m % 2 + 1], in1=p0[m % 3][:, 0:w],
                                                 op0=ALU.mult, op1=ALU.add).then_inc(b_a, 1)
                dve.wait_ge(ap_ev, 6)
                rope(krT[:, TC + PAST:NKEY], rota[0:DR, :], cosT[0:DR, :], sinT[0:DR, :], link).then_inc(ap_kr, 1)
                dve.wait_ge(ap_kr, 1)

                def head_ready(h):
                    dve.wait_ge(x_ev, 4 * h + 4)
                    dve.tensor_copy(kA[h % 2][DN:DQ, :], krT[:, :])
                    rope(qA[h % 2][DN:DQ, TC:T], rota[DN:DQ, :], cosT[DN:DQ, :], sinT[DN:DQ, :], link).then_inc(a_qk, 1)

                head_ready(0)
                NA = H_A * NT
                for n in range(NA + 4):
                    h, qi = n // NT, n % NT
                    if n >= 4:
                        m = n - 4
                        dve.wait_ge(a_pv, m + 1)
                        dve.tensor_scalar(omix[:, m % NT, (m // NT) * DV_A:(m // NT + 1) * DV_A], ps[:, 6, 0:DV_A],
                                          arec[:, m % 4:m % 4 + 1], None, ALU.mult).then_inc(a_o, 1)
                    if n < NA:
                        dve.wait_ge(a_sc, n + 1)
                        top(2 * (n % 2), qi, n % 2).then_inc(a_neg, 1)
                    if 1 <= n <= NA:
                        m = n - 1
                        dve.wait_ge(a_exp, m + 1)
                        link(dve.reciprocal(arec[:, m % 4:m % 4 + 1], asum[:, m % 2:m % 2 + 1]))
                    if qi == 4 and h < H_A - 1:
                        head_ready(h + 1)
                dve.wait_ge(a_o, NA)
                oa, ob = omix[:, :, 0:WA], omix[:, :, WA:WA + WB]
                link(dve.tensor_tensor(asq[:, :, :], oa, oa, ALU.mult))
                link(dve.tensor_reduce(ss10[:, 0:NT], asq[:, :, :], AX.X, ALU.add))
                link(dve.tensor_tensor(asq[:, :, 0:WB], ob, ob, ALU.mult))
                dve.tensor_reduce(css.rearrange("p (t h) -> p t h", h=H_B), asq[:, :, 0:WB].rearrange("p t (h v) -> p t h v", h=H_B), AX.X, ALU.add).then_inc(on_v, 1)
                dve.wait_ge(on_s, 1)
                dve.reciprocal(ss10[:, 0:NT], rs10[:, 0:NT])
                link(dve.reciprocal(css, crs))
                dve.tensor_tensor(oa, oa, ss10[:, 0:NT].unsqueeze(2).broadcast_to([P, NT, WA]), ALU.mult)
                obh = ob.rearrange("p t (h v) -> p t h v", h=H_B)
                dve.tensor_tensor(obh, obh, css.rearrange("p (t h) -> p t h", h=H_B).unsqueeze(3).broadcast_to([P, NT, H_B, DV_B]), ALU.mult).then_inc(on_ok, 1)
                for k in range(KD):
                    dve.wait_ge(ot_hi, k + 1)
                    b = 2 * (k % 4) * 512
                    dve.scalar_tensor_tensor(out=u_lo[:, k, :], in0=psf[:, b:b + T], scalar=parT[:, R_OG + k:R_OG + k + 1], in1=cv(u_hi[:, k, :]),
                                             op0=ALU.mult, op1=ALU.subtract).then_inc(ot_lo, 1)
                for n in range(NW2):
                    g = G_WOUT + n
                    dve.wait_ge(mm_ok, g + 1)
                    for m2 in range(2):
                        update_x(1, 4 * (g % 2) + 2 * m2, 2 * n + m2, False).then_inc(x_upd, 1)
                    lo(g + 2)
                norm(2)
                ffn(G_FFN2, NF, 2, (len(PARTS) + 1) * KD, last=True)
                dve.drain().then_inc(l_done, 1)
                dve.wait_ge(s_go, l + 1)
            for m in range(KD):
                dve.wait_ge(f_sq, m + 1)
                if m == 0:
                    dve.tensor_copy(sqsum[:, :], sq[:, 0, :]).then_inc(f_sqd, 1)
                else:
                    dve.wait_ge(f_sqd, m)
                    dve.tensor_tensor(sqsum[:, :], sqsum[:, :], sq[:, m % 2, :], ALU.add).then_inc(f_sqd, 1)
            dve.wait_ge(f_std, 1)
            dve.reciprocal(rstd[:, :], stdv[:, :]).then_inc(f_sum, 1)
            dve.wait_ge(f_sum, 1)
            for m in range(KD):
                if m >= 2:
                    dve.wait_ge(s_yt, m - 1)
                dve.tensor_tensor(xn[:, m % 2, :], xT[:, m, :], rstd[:, :], ALU.mult).then_inc(f_xn, 1)

        @block.tensor
        def _(pe):
            def up_banks(g):
                return 4 * (g % 2)

            def fm(g, step, src, nk, per_k, n_out=2, width=P, tail=None):
                b = up_banks(g)
                wh = w_hi[:, g % 2, :].rearrange("p (k n) -> p k n", k=KD)
                wl = w_lo[:, g % 2, :].rearrange("p (k n) -> p k n", k=KD)
                xh, xl = src
                pe.wait_ge(lo_ok, g + 1 + step)
                for o in range(n_out):
                    for k in range(nk):
                        if o == 0 and per_k is not None:
                            per_k(k)
                        for half in range(2):
                            t = slice(half * TH, (half + 1) * TH)
                            out = ps[0:width, b + 2 * o + half, 0:TH]
                            c = slice(o * P, o * P + width)
                            pe.matmul(out, wh[:, k, c], xh[:, k, t], start=k == 0, stop=False)
                            pe.matmul(out, wh[:, k, c], xl[:, k, t], start=False, stop=False)
                            last = pe.matmul(out, wl[:, k, c], xh[:, k, t], start=False, stop=k == nk - 1)
                last.then_inc(mm_ok, 1)

            def fm_pair(g, src, per_k, shapes):
                xh, xl = src
                pe.wait_ge(lo_ok, g + 2)
                last = [None, None]
                for k in range(KD):
                    per_k(k)
                    for c in range(2):
                        n_out, width = shapes[c]
                        wh = w_hi[:, (g + c) % 2, :].rearrange("p (k n) -> p k n", k=KD)
                        wl = w_lo[:, (g + c) % 2, :].rearrange("p (k n) -> p k n", k=KD)
                        for o in range(n_out):
                            for half in range(2):
                                t = slice(half * TH, (half + 1) * TH)
                                out = ps[0:width, up_banks(g + c) + 2 * o + half, 0:TH]
                                w = slice(o * P, o * P + width)
                                pe.matmul(out, wh[:, k, w], xh[:, k, t], start=k == 0, stop=False)
                                pe.matmul(out, wh[:, k, w], xl[:, k, t], start=False, stop=False)
                                last[c] = pe.matmul(out, wl[:, k, w], xh[:, k, t], start=False, stop=k == KD - 1)
                        if k == KD - 1:
                            last[c].then_inc(mm_ok, 1)

            def tmaj(g):
                b = up_banks(g)
                wh = w_hi[:, g % 2, :].rearrange("p (k n) -> p k n", k=KD)
                wl = w_lo[:, g % 2, :].rearrange("p (k n) -> p k n", k=KD)
                pe.wait_ge(lo_ok, g + 1)
                for t in range(NT):
                    out = psf[:, b * 512 + t * CW:b * 512 + (t + 1) * CW]
                    c = slice(t * P, (t + 1) * P)
                    for k in range(KD):
                        pe.matmul(out, u_hi[:, k, c], wh[:, k, :], start=k == 0, stop=False)
                        pe.matmul(out, u_lo[:, k, c], wh[:, k, :], start=False, stop=False)
                        last = pe.matmul(out, u_hi[:, k, c], wl[:, k, :], start=False, stop=k == KD - 1)
                last.then_inc(mm_ok, 1)

            def sums(s_in, v_in, s_out):
                pe.wait_ge(s_in, v_in)
                for half in range(2):
                    last = pe.matmul(ps[:, half, 0:TH], ones[:, :], sqsum[:, half * TH:(half + 1) * TH], start=True, stop=True)
                last.then_inc(s_out, 1)

            def u_tile(n):
                return lambda k: pe.wait_ge(n_ulo, n * KD + k + 1)

            def mod_under(g, i=0):
                c = g - G_MOD
                s = g % 2
                b = up_banks(g) + 2
                if 0 <= c < N_UNDER:
                    pe.wait_ge(v_in[s], i * 16 + 16 * (c // 2 + 1))
                    for half in range(2):
                        for kk in range(2):
                            for j in range(4):
                                k = j + 4 * kk
                                last = pe.matmul(ps[32 * j:32 * j + 32, b + half, TH:TH + P], csp[:, k, :], uraw[:, s, k, half * P:(half + 1) * P],
                                                 start=kk == 0, stop=kk == 1)
                    last.then_inc(v_mm, 1)
                if 2 <= c < N_UNDER + 2:
                    pe.wait_ge(v_row, i * 2 + (c - 1))
                    for r in range(2):
                        pe.matmul(ps[:, b, TH + P + 2 * r:TH + P + 2 * r + 2], urows[:, s, r * P:(r + 1) * P], comb[:, :], start=True, stop=True)

            def ffn(g, up0, x0, n):
                first = n == 0
                for q, cnt in enumerate(PARTS):
                    def up_step(j, i):
                        if first:
                            mod_under(g + j, i)
                        fm(g + j, i * 2, (u_hi, u_lo), KD, None)

                    start = 0
                    if q == 0:
                        fm_pair(g, (u_hi, u_lo), u_tile(n), [(2, P), (2, P)])
                        for j in range(2, 4):
                            pe.wait_ge(h32_ok, up0 + j - 1)
                            up_step(j, 0)
                        start = 4
                    else:
                        pe.wait_ge(x_upd, x0 + q * KD)
                    with pe.Fori(0, (cnt - start) // 2) as i:
                        for j in range(start, start + 2):
                            pe.wait_ge(h32_ok, up0 + j - 1 + i * 2)
                            up_step(j, i)
                    g += cnt
                    up0 += cnt
                    pe.wait_ge(h32_ok, up0)
                    for j in range(2):
                        if first:
                            mod_under(g + j)
                        fm(g + j, 0, (h_hi, h_lo), cnt, None if j else lambda k: pe.wait_ge(hlo_ok, up0 - cnt + k + 1))
                    with pe.Fori(0, NW2 // 2 - 1) as i:
                        for j in range(2):
                            pe.wait_ge(x_upd, i * 4 + (x0 + q * KD + 2 * j + 2))
                            if first:
                                mod_under(g + j + 2, i)
                            fm(g + j + 2, i * 2, (h_hi, h_lo), cnt, None)
                    g += NW2

            pe.wait_ge(s_const, 26)
            pe.wait_ge(s_tab, 64)
            pe.transpose(ps[:, 0, 0:2 * KD], par[0:2 * KD, :], ident[0:2 * KD, 0:2 * KD]).then_inc(s_ctp, 1)
            pe.wait_ge(s_csil, 1)
            pe.wait_ge(s_xs, 32)
            for m in range(KD):
                if m >= 4:
                    pe.wait_ge((s_xa, s_xv)[m % 2], (m - 4) // 2 + 1)
                b = 2 * (m % 4) * 512
                for t in range(NT):
                    last = pe.transpose(psf[:, b + t * P:b + (t + 1) * P], xs[:, t, m * P:(m + 1) * P], ident[:, :])
                last.then_inc(s_xtp, 1)
            pe.wait_ge(s_const, 27)
            pe.wait_ge(s_xa, KD // 2)
            pe.wait_ge(s_xv, KD // 2)

            with pe.Fori(0, DEPTH) as l:
                pe.wait_ge(par_in, (l + 1) * (16 * names["n_par"]))
                pe.transpose(ps[:, 7, 0:P], par[:, :], ident[:, :]).then_inc(par_tp, 1)
                for c in range(NMC):
                    pe.wait_ge(m_raw[c], 16)
                    for kk in range(2):
                        for j in range(4):
                            k = j + 4 * kk
                            last = pe.matmul(ps[32 * j:32 * j + 32, c, :], csp[:, k, :], mraw[:, c, k, :], start=kk == 0, stop=kk == 1)
                    last.then_inc(m_mm, 1)
                    pe.wait_ge(m_row, c + 1)
                    if c == NMC - 1:
                        pe.wait_ge(par_ok, 1)
                    for r in range(MW // P):
                        last = pe.matmul(ps[:, 4 + c, 2 * r:2 * r + 2], mrows[:, c, r * P:(r + 1) * P], comb[:, :], start=True, stop=True)
                    last.then_inc(m_tp, 1)
                sums(n_sqd, KD, n_ss)
                ffn(G_FFN1, 0, 0, 0)
                sums(n_sqd, 2 * KD, n_ss)
                def gate_products(d, b):
                    for p in range(2):
                        for half in range(2):
                            last = pe.matmul(ps[:, b + 2 * p + half, 0:TH], wgp[:, d, p * P:(p + 1) * P], glT[:, half * TH:(half + 1) * TH], start=True, stop=True)
                    last.then_inc(g_z, 1)

                for n, name in enumerate(PROJ):
                    g = G_PROJ + n
                    if n >= 2:
                        pe.wait_ge(ev_ok, n - 1)
                    if n == Z_AT + 1:
                        gate_products(0, up_banks(g))
                        pe.wait_ge(g_min, 1)
                    if n == 0:
                        fm_pair(g, (u_hi, u_lo), u_tile(1), [(1, 2 * GR), (2, P)])
                    elif n == 1:
                        continue
                    elif name in ("qc", "kc", "qb"):
                        fm(g, 0, (u_hi, u_lo), KD, None)
                    else:
                        tmaj(g)
                pe.wait_ge(ev_ok, len(PROJ) - 1)
                gate_products(1, 0)
                pe.wait_ge(ev_ok, len(PROJ))
                for d in range(2):
                    pe.wait_ge(g_kd, d + 1)
                    if d == 1:
                        pe.wait_ge(g_oev, NT)
                    for t in range(NT):
                        if d * NT + t >= 2:
                            pe.wait_ge(g_tev, d * NT + t - 1)
                        for a in range(2):
                            last = pe.transpose(ps[:, 4 + t % 2, a * P:(a + 1) * P], gkd[d][:, a, t * P:(t + 1) * P], ident[:, :])
                        last.then_inc(g_tp, 1)
                    if d == 0:
                        pe.wait_ge(kv_in, (l + 1) * 32)
                        for m in range(2):
                            last = pe.transpose(ps[:, 6, m * P:(m + 1) * P], ck[:, m * P:(m + 1) * P], ident[:, :])
                        last.then_inc(bk_tp, 1)
                        for m in range(2):
                            last = pe.transpose(ps[:, 7, m * P:(m + 1) * P], kbT[:, m, 0:TC], ident[:, :])
                        last.then_inc(bk_tp, 1)
                        pe.wait_ge(bk_ev, 2)
                    for n, c in enumerate(U_ORDER[d]):
                        pe.wait_ge(g_tev, d * NT + c // 2 + 1)
                        if d * N_STATE + n >= 2:
                            pe.wait_ge(g_s, d * N_STATE + n - 1)
                        r = slice(CH * (c % 2), CH * (c % 2) + CH)
                        for h in range(H_C):
                            hh, a = h % 2, h // 2
                            last = pe.matmul(ps[HW * hh:HW * hh + HW, 6 + n % 2, a * DV_C:(a + 1) * DV_C],
                                             kdt[r, c // 2, a, HW * hh:HW * hh + HW], vcs[r, c // 2, h * DV_C:(h + 1) * DV_C], start=True, stop=True)
                        last.then_inc(g_u, 1)
                    if d == 0:
                        pe.wait_ge(g_min, 2)
                    pe.wait_ge(g_ke, d + 1)

                    def intra_scores(n):
                        t = O_ORDER[d][n]
                        if d * NT + n >= 2:
                            pe.wait_ge(g_am, d * NT + n - 1)
                        ts = slice(t * P, (t + 1) * P)
                        for h in range(H_C):
                            rows = slice(HW * (h % 2), HW * (h % 2) + DK)
                            last = pe.matmul(ps[:, 2 * (n % 2) + h % 2, (h // 2) * P:(h // 2 + 1) * P], gke[d][rows, h // 2, ts], gqe[d][rows, h // 2, ts], start=True, stop=True)
                        last.then_inc(g_at, 1)

                    intra_scores(0)
                    for n, t in enumerate(O_ORDER[d]):
                        if n + 1 < NT:
                            intra_scores(n + 1)
                        pe.wait_ge(g_am, d * NT + n + 1)
                        if n >= 1:
                            pe.wait_ge(g_oev, d * NT + n)
                        for c in (2 * t, 2 * t + 1):
                            if state_count(d, c):
                                pe.wait_ge(g_s, d * N_STATE + state_count(d, c))
                        for h in range(H_C):
                            rows = slice(HW * (h % 2), HW * (h % 2) + DK)
                            bank, cols = 4 + h % 2, slice((h // 2) * DV_C, (h // 2 + 1) * DV_C)
                            ha = 2 * (h % 2) + h // 2
                            last = pe.matmul(ps[:, bank, cols], am[:, n % 2, ha * P:(ha + 1) * P], vcs[:, t, h * DV_C:(h + 1) * DV_C], start=True, stop=False, skip_group_check=True)
                            for c in (2 * t, 2 * t + 1):
                                if has_state(d, c):
                                    q0 = CH * (c % 2)
                                    last = pe.matmul(ps[q0:q0 + CH, bank, cols], gqe[d][rows, h // 2, c * CH:(c + 1) * CH],
                                                     entering(d, c)[rows, h // 2, :], start=False, stop=True, skip_group_check=True)
                        last.then_inc(g_o, 1)
                NB = H_B * NT
                pe.wait_ge(g_oev, 2 * NT)
                pe.wait_ge(g_s, 2 * N_STATE)

                def score(s, q, kt, qi, s_sc):
                    if qi == 0:
                        last = pe.matmul(ps[:, s, 0:P], q, kt[:, 0:TC], start=True, stop=True)
                    else:
                        for half in range(2):
                            k0 = TC + half * TH
                            last = pe.matmul(ps[:, s + half, 0:TH], q, kt[:, k0:k0 + TH], start=True, stop=True)
                    last.then_inc(s_sc, 1)

                def turn(m, prob, s_tp, s_pt):
                    nk = 1 if m % NT == 0 else NT
                    if m >= 1:
                        pe.wait_ge(s_pt, m)
                    for k in range(nk):
                        last = pe.transpose(psf[:, 4 * 512 + k * P:4 * 512 + (k + 1) * P], prob[:, k * P:(k + 1) * P], ident[:, :])
                    last.then_inc(s_tp, 1)

                def values(m, s_pt, s_pv, s_o, v, c0):
                    nk = 1 if m % NT == 0 else NT
                    pe.wait_ge(s_pt, m + 1)
                    if m >= 1:
                        pe.wait_ge(s_o, m)
                    v0 = keys_of(m % NT)[0]
                    for k in range(nk):
                        last = pe.matmul(ps[:, 6, 0:96], pt[m % 2][:, k, :], v[:, v0 + k, c0:c0 + 96], start=k == 0, stop=k == nk - 1)
                    last.then_inc(s_pv, 1)

                pe.wait_ge(pool_c, 1)
                for n in range(NB + 3):
                    h, qi = n // NT, n % NT

                    def softmax_scores(j):
                        r = 2 * h + j
                        if n >= 1:
                            pe.wait_ge(b_exp, 2 * (n - 1) + j + 1)
                        score(2 * j, qm[h % 2][j][:, qi * P:(qi + 1) * P], kbT[:, r // 4, :], qi, b_sc)

                    if n < NB:
                        if qi == 0:
                            pe.wait_ge(b_qm, h + 1)
                        softmax_scores(0)
                    if n >= 3:
                        values(n - 3, b_pt, b_pv, b_o, vbs, ((n - 3) // NT) * DV_B)
                    if n < NB:
                        softmax_scores(1)
                    if 2 <= n <= NB + 1:
                        pe.wait_ge(b_a, n - 1)
                        turn(n - 2, p0[(n - 2) % 3], b_tp, b_pt)
                pe.wait_ge(aw_in, (l + 1) * (16 * 5))
                pe.wait_ge(b_o, NB)
                pe.wait_ge(cq_ok, 1)
                for s in range(6):
                    if s >= 4:
                        pe.wait_ge(ap_ev, s - 3)
                    b = 2 * (s % 4) * 512
                    w = (DR if s == 5 else P)
                    c0 = (s * P if s < 3 else Q_RANK + (s - 3) * P if s < 5 else 640)
                    tiles = [cqkv[:, t, c0:c0 + w] for t in range(NT)]
                    if s in (3, 4):
                        tiles.insert(1, cc[:, (s - 3) * P:(s - 2) * P])
                    if s == 5:
                        tiles.insert(1, cck[:, :])
                    for t, src in enumerate(tiles):
                        last = pe.transpose(psf[0:w, b + t * P:b + (t + 1) * P], src, ident[:, :])
                    last.then_inc(ap_tp, 1)
                pe.wait_ge(ap_ev, 6)
                for t in range(NKT):
                    for k in range(2):
                        last = pe.matmul(ps[:, t, 0:WA], ckvT[:, k, t * P:(t + 1) * P], wuv[:, k, :], start=k == 0, stop=k == 1)
                    last.then_inc(ap_tp, 1)

                def head_piece(r):
                    h, k = r // 4, r % 4
                    if r >= 1:
                        pe.wait_ge(x_ev, r)
                    if k < 2:
                        for c in range(3):
                            last = pe.matmul(ps[0:DQ, 7, 0:TH], wuq[:, c, h * DQ:(h + 1) * DQ], cqT[:, c, k * TH:(k + 1) * TH], start=c == 0, stop=c == 2)
                    else:
                        c0 = (k - 2) * (NKEY // 2)
                        for c in range(2):
                            last = pe.matmul(ps[0:DN, 7, 0:NKEY // 2], wuk[:, c, h * DN:(h + 1) * DN], ckvT[:, c, c0:c0 + NKEY // 2], start=c == 0, stop=c == 1)
                    last.then_inc(x_mm, 1)

                for r in range(4):
                    head_piece(r)
                NA = H_A * NT
                pe.wait_ge(ap_ev, 6 + NKT)
                pe.wait_ge(pool_c, 2)
                for n in range(NA + 3):
                    h, qi = n // NT, n % NT
                    if n < NA:
                        if qi == 0:
                            pe.wait_ge(a_qk, h + 1)
                        if n >= 2:
                            pe.wait_ge(a_exp, n - 1)
                        score(2 * (n % 2), qA[h % 2][0:DQ, qi * P:(qi + 1) * P], kA[h % 2][0:DQ, :], qi, a_sc)
                    if n >= 3:
                        values(n - 3, a_pt, a_pv, a_o, vas, ((n - 3) // NT) * DV_A)
                    if 2 <= n <= NA + 1:
                        pe.wait_ge(a_exp, n - 1)
                        turn(n - 2, pa[(n - 2) % 3], a_tp, a_pt)
                    if qi < 4 and h < H_A - 1:
                        head_piece(4 * (h + 1) + qi)
                pe.wait_ge(on_ok, 1)
                for k in range(KD):
                    if k >= 4:
                        pe.wait_ge(ot_lo, k - 3)
                    b = 2 * (k % 4) * 512
                    for t in range(NT):
                        last = pe.transpose(psf[:, b + t * P:b + (t + 1) * P], omix[:, t, k * P:(k + 1) * P], ident[:, :])
                    last.then_inc(ot_tp, 1)
                pe.wait_ge(ot_lo, KD)
                for n in range(NW2):
                    g = G_WOUT + n
                    if n >= 2:
                        pe.wait_ge(x_upd, 3 * KD + 2 * (n - 1))
                    fm(g, 0, (u_hi, u_lo), KD, None)
                sums(n_sqd, 3 * KD, n_ss)
                ffn(G_FFN2, NF, 4 * KD, 2)
                pe.drain().then_inc(l_done, 1)
                pe.wait_ge(s_go, l + 1)
            sums(f_sqd, KD, f_ss)
            pe.wait_ge(s_yt, KD)
            for t in range(NT):
                if t >= 4:
                    pe.wait_ge(s_ytm, t - 3)
                b = 2 * (t % 4) * 512
                for k in range(KD):
                    last = pe.transpose(psf[:, b + k * P:b + (k + 1) * P], yT[:, k, t * P:(t + 1) * P], ident[:, :])
                last.then_inc(s_ytp, 1)


def rope_tables():
    inv = (10000.0 ** (-np.arange(0, 16, 2, dtype=np.float32) / np.float32(16))).astype(np.float32)
    tok = np.arange(TL)
    cos, sin = np.zeros((32, TL), np.float32), np.zeros((32, TL), np.float32)
    for i in range(32):
        pos = (tok // GRID_W if i < 16 else tok % GRID_W).astype(np.float32)
        ang = pos * inv[i % 8]
        cos[i] = np.cos(ang)
        sin[i] = np.sin(ang) * (-1.0 if i % 16 < 8 else 1.0)
    return np.tile(cos, (4, 1)), np.tile(sin, (4, 1))


def layer_constants():
    lam = [0.8 - 0.6 * math.exp(-0.3 * l) for l in range(DEPTH)]
    return np.ascontiguousarray(np.broadcast_to(np.array([[x, 1.0 - x] for x in lam], np.float32)[:, None, :], (DEPTH, P, 2)))


OUTS = {
    "y_prompt": (1, TC, D), "y_sample": (1, TL, D),
    "new_mla_ckv": (1, DEPTH, TC, KV_RANK), "new_mla_krope": (1, DEPTH, TC, DR),
    "new_diff_k": (1, DEPTH, TC, H_B, 2 * DH_B), "new_diff_v": (1, DEPTH, TC, H_B, DV_B),
    "new_gla_fwd": (1, DEPTH, H_C, DK, DV_C), "new_gla_bwd": (1, DEPTH, H_C, DK, DV_C),
}


def kernel(**inputs):
    import concourse.bacc as bacc
    from concourse.bass_utils import run_bass_kernel_spmd

    nc = bacc.Bacc("TRN2", target_bir_lowering=False, num_devices=1)
    arrays = {name: np.ascontiguousarray(a) for name, a in inputs.items()}
    arrays["rope_cos"], arrays["rope_sin"] = rope_tables()
    arrays["layer_consts"] = layer_constants()
    A = {n: nc.dram_tensor(f"in_{n}", a.shape, mybir.dt.from_np(a.dtype), kind="ExternalInput").ap() for n, a in arrays.items()}
    O = {n: nc.dram_tensor(f"out_{n}", s, F32, kind="ExternalOutput").ap() for n, s in OUTS.items()}
    build(nc, A, O)
    r = run_bass_kernel_spmd(nc, [{f"in_{n}": a for n, a in arrays.items()}], core_ids=[0])
    return tuple(r.results[0][f"out_{n}"] for n in OUTS)
```

```python
import math
from contextlib import ExitStack

import concourse.bass as bass
import numpy as np
from concourse import mybir

F32 = mybir.dt.float32
F32R = mybir.dt.float32r
ACT = mybir.ActivationFunctionType
ALU = mybir.AluOpType
AX = mybir.AxisListType

P = 128
D = 1024
KD = D // P
DEPTH = 2
TC, TL, PAST = 128, 512, 128
T = TC + TL
NT = T // P
TH = T // 2
NKEY = TC + PAST + TL
NKT = NKEY // P
GRID_W = 64
EPS = 1e-6
H_A, DN, DR, DV_A = 6, 64, 32, 64
DQ = DN + DR
Q_RANK, KV_RANK = 384, 256
H_B, DH_B, DV_B = 4, 32, 64
H_C, DK, DV_C = 4, 48, 96
GR = 16
GATE_NORM = 16.0
CH = 64
NCH = T // CH
HW = 64
WA, WB, WC = H_A * DV_A, H_B * DV_B, H_C * DV_C
F = 2816
NF = F // P
PARTS = [8, 8, 6]
NMOD = 9
NMT = NMOD * KD
CW = 256
MW = 512
NMC = 2 * D // MW
G_MOD = 2
N_UNDER = ((NMOD - 2) * D // CW, 2 * D // CW)
V0 = (0, N_UNDER[0])
NW2 = D // CW
O_CQ, O_QB, O_KB, O_VB = 0, 672, 928, 1184
O_QC, O_KC, O_VR, O_GL = 1440, 1632, 1824, 2592
PROJ = ["gl", "kb", "qb", "qc", "kc", "c0", "c1", "c2", "vb", "vr0", "vr1", "vr2"]
Z_AT = 2
G_FFN1 = 0
N_FFN = sum(PARTS) + NW2 * len(PARTS)
G_PROJ = G_FFN1 + N_FFN
G_WOUT = G_PROJ + len(PROJ)
G_FFN2 = G_WOUT + NW2
N_CHUNK = G_FFN2 + N_FFN
R_BMOD, R_N1, R_NM, R_N2, R_FIN, R_QN, R_OG, R_BG, NPAR = 0, 72, 80, 88, 96, 104, 107, 115, 119


def chunk_dmas(g):
    if G_PROJ <= g < G_WOUT and PROJ[g - G_PROJ] in ("qc", "kc"):
        return H_C
    return 2


def raw_need(g):
    return 16 * sum(chunk_dmas(x) for x in range(g % 2, g + 1, 2))


def build(nc, A, O):
    ctx = ExitStack()
    with ctx:
        names = {}

        def sb(name, shape, offset, dtype=F32):
            return nc.alloc_sbuf_tensor_at(name, shape, dtype, offset=offset)

        def sem(name):
            return ctx.enter_context(nc.semaphore(name))

        XB = 16512
        UB = XB + KD * T * 4
        RB = UB + 2 * KD * T * 4
        DG = RB + 6 * KD * CW * 4
        CB = DG + 81920
        xT = sb("xT", [P, KD, T], XB)
        u_hi = sb("u_hi", [P, KD, T], UB, F32R)
        u_lo = sb("u_lo", [P, KD, T], UB + KD * T * 4, F32R)
        raw = sb("raw", [P, 2, KD * CW], RB)
        w_hi = sb("w_hi", [P, 2, KD * CW], RB + 2 * KD * CW * 4, F32R)
        w_lo = sb("w_lo", [P, 2, KD * CW], RB + 4 * KD * CW * 4, F32R)
        h_hi = sb("h_hi", [P, 8, T], DG, F32R)
        h_lo = sb("h_lo", [P, 8, T], DG + 20480, F32R)
        G0 = DG + 40960
        silu_a = sb("silu_a", [P, 2, T], G0)
        h32 = sb("h32", [P, 2, T], G0 + 5120)
        sq = sb("sq", [P, 2, T], G0 + 10240)
        sqsum = sb("sqsum", [P, T], G0 + 15360)
        rstd = sb("rstd", [P, T], G0 + 17920)
        xn = sb("xn", [P, 2, T], G0 + 20480)
        u32 = sb("u32", [P, 2, T], G0 + 25600)
        dg = sb("dg", [P, NT, P], G0 + 30720)
        mraw = [sb(f"mraw{c}", [P, KD, MW], o) for c, o in enumerate((RB + 16384, RB + 32768, DG, DG + 16384))]
        mrows = sb("mrows", [P, NMC, MW], DG + 32768)
        uraw = sb("uraw", [P, 2, KD, CW], G0 + 10240)
        urows = sb("urows", [P, 2, CW], G0 + 26624)
        xs = sb("xs", [P, NT, D], UB)
        yT = sb("yT", [P, KD, T], UB)
        ytm = sb("ytm", [P, 2, D], DG)
        omix = sb("omix", [P, NT, D], DG)
        qcT = sb("qcT", [P, 2, T], DG + 20480)
        kcT = sb("kcT", [P, 2, T], DG + 25600)
        glT = sb("glT", [2 * GR, T], DG + 30720)
        vcs = sb("vcs", [P, NT, WC], DG + 33280)
        rcs = sb("rcs", [P, NT, WC], DG + 40960)
        cqkv = sb("cqkv", [P, NT, 672], DG + 48640)
        qbT = sb("qbT", [P, 2, T], DG + 62080)
        kbT = sb("kbT", [P, 2, NKEY], DG + 67200)
        vbs = sb("vbs", [P, NKT, 288], DG + 73344)
        ck = sb("ck", [P, 256], DG + 80256)
        rotb = sb("rotb", [P, 2, TL], DG + 15360)
        GB = (DG, UB)
        gab = [sb(f"gab{d}", [P, 2, T], GB[d]) for d in range(2)]
        gb = [sb(f"gb{d}", [P, 2, T], GB[d] + 5120) for d in range(2)]
        gcum = [sb(f"gcum{d}", [P, 2, T], GB[d] + 10240) for d in range(2)]
        gqe = [sb(f"gqe{d}", [P, 2, T], GB[d] + 15360) for d in range(2)]
        gke, gkd = gcum, gab
        am = sb("am", [P, 2, 512], DG + 5120)
        kdt = sb("kdt", [P, NT, 2, P], UB + 20480)
        S = sb("S", [P, NCH, 2, DV_C], UB + 25600)
        S_FIN = (2, 1)
        oc = sb("oc", [P, NT, WC], UB + 33280)
        osq = sb("osq", [P, NT, WC], DG + 10240)
        qm = [[sb(f"qm{s}{j}", [P, T], UB + o) for j, o in enumerate(os)] for s, os in enumerate([(13824, 16384), (20480, 23040)])]
        p0 = [sb(f"p0_{s}", [P, T], UB + o) for s, o in enumerate((25600, 28160, 0))]
        pa = [sb(f"pa_{s}", [P, T], UB + o) for s, o in enumerate((25600, 28160, 33280))]
        p1 = [sb(f"p1_{s}", [P, T], UB + 30720 + 2560 * s) for s in range(2)]
        pt = [sb(f"pt_{s}", [P, NT, P], UB + 35840 + 2560 * s) for s in range(2)]
        cqT = sb("cqT", [P, 3, T], UB)
        ckvT = sb("ckvT", [P, 2, NKEY], UB + 7680)
        kA = [sb(f"kA{s}", [P, NKEY], UB + 13824 + 3072 * s) for s in range(2)]
        qA = [sb(f"qA{s}", [P, T], UB + 20480 + 2560 * s) for s in range(2)]
        rota = sb("rota", [P, TL], UB + 30720)
        wuq = sb("wuq", [P, 3, H_A * DQ], DG + 20480)
        wuk = sb("wuk", [P, 2, H_A * DN], DG + 27392)
        wuv = sb("wuv", [P, 2, WA], DG + 30464)
        vas = sb("vas", [P, NKT, 416], DG + 33536)
        krT = sb("krT", [DR, NKEY], DG + 43520)
        cc = sb("cc", [P, KV_RANK], DG + 46592)
        cck = sb("cck", [P, DR], DG + 47616)
        asq = sb("asq", [P, NT, WA], DG + 48640)
        bsq = sb("bsq", [P, NT, WB], DG + 56320)
        off = [CB]

        def small(name, shape, dtype=F32):
            n = 4
            for s in shape[1:]:
                n *= s
            t = sb(name, shape, off[0], dtype)
            off[0] += (n + 31) // 32 * 32
            return t

        cosT, sinT = small("cosT", [P, TL]), small("sinT", [P, TL])
        ident, ones = small("ident", [P, P]), small("ones", [P, P])
        mask = small("mask", [P, 2, P])
        keep = small("keep", [P, 2, T])
        csp = small("csp", [P, KD, 32])
        comb = small("comb", [P, 2])
        modT = small("modT", [P, NMT, 2])
        gains = small("gains", [P, 3, KD, 2])
        gates = small("gates", [P, 3, KD, 2])
        par = small("par", [P, P])
        parT = small("parT", [P, P])
        grp = small("grp", [P, 4])
        lqk = small("lqk", [P, 4, DH_B])
        wgp = small("wgp", [2 * GR, 2, H_C * HW])
        Sini = small("Sini", [P, 2, 2, DV_C])
        kvw = small("kvw", [P, KV_RANK])
        st = small("st", [P, 96])
        sd5, rs5 = small("sd5", [P, NT]), small("rs5", [P, NT])
        gtot = [small(f"gtot{d}", [P, 2, NCH]) for d in range(2)]
        assert off[0] <= 229368, off[0]
        eps = st[:, 0:1]
        lam2, lexp, nlam = st[:, 1:3], st[:, 3:5], st[:, 5:6]
        lcon = st[:, 6:8]
        ldif = st[:, 8:9]
        css, crs = st[:, 10:30], st[:, 30:50]
        ss10, rs10 = st[:, 50:60], st[:, 60:70]
        ratio, aneg, asum, arec = st[:, 70:72], st[:, 74:78], st[:, 78:82], st[:, 82:90]
        ps = ctx.enter_context(nc.psum_tensor("ps", [P, 8, 512], F32))
        psf = ps[:, :, :].rearrange("p b n -> p (b n)")

        s_const = sem("s_const")
        s_tab = sem("s_tab")
        s_xs = sem("s_xs")
        s_ctp = sem("s_ctp")
        s_csil = sem("s_csil")
        s_xtp = sem("s_xtp")
        s_xa = sem("s_xa")
        s_xv = sem("s_xv")
        s_go = sem("s_go")
        s_yt = sem("s_yt")
        s_ytp = sem("s_ytp")
        s_ytm = sem("s_ytm")
        s_yout = [sem("s_yout0"), sem("s_yout1")]
        s_sq, s_sqd = sem("s_sq"), sem("s_sqd")
        f_ss, f_std, f_dg, f_bc, f_xn = (sem("f_" + n) for n in ("ss", "std", "dg", "bc", "xn"))
        m_raw = [sem(f"m_raw{i}") for i in range(NMC)]
        m_mm, m_row, m_tp, m_ev = sem("m_mm"), sem("m_row"), sem("m_tp"), sem("m_ev")
        s_ptp, s_par = sem("s_ptp"), sem("s_par")
        s_gain = sem("s_gain")
        par_in = sem("par_in")
        kv_in = sem("kv_in")
        aw_in = sem("aw_in")
        out_in = sem("out_in")
        layer_sems = []

        def lsem(name):
            s = sem(name)
            layer_sems.append(s)
            return s

        l_done = lsem("l_done")
        par_ok = lsem("par_ok")
        lam_s = lsem("lam_s")
        lam_e = lsem("lam_e")
        mod_ok = lsem("mod_ok")
        v_in = [lsem("v_in0"), lsem("v_in1")]
        v_mm, v_row, v_ev = lsem("v_mm"), lsem("v_row"), lsem("v_ev")
        raw_in = [lsem("raw_in0"), lsem("raw_in1")]
        hi_ok, lo_ok = lsem("hi_ok"), lsem("lo_ok")
        mm_ok = lsem("mm_ok")
        ev_ok = lsem("ev_ok")
        sil_ok, h32_ok, hhi_ok, hlo_ok = lsem("sil_ok"), lsem("h32_ok"), lsem("hhi_ok"), lsem("hlo_ok")
        x_upd = lsem("x_upd")
        n_sq, n_sqd, n_ss, n_std, n_dg, n_bc = (lsem("n_" + n) for n in ("sq", "sqd", "ss", "std", "dg", "bc"))
        n_xn, n_u32, n_uhi, n_ulo = (lsem("n_" + n) for n in ("xn", "u32", "uhi", "ulo"))
        dve_c = lsem("dve_c")
        act_c = lsem("act_c")
        pool_c = lsem("pool_c")
        bk_tp, bk_ev = lsem("bk_tp"), lsem("bk_ev")
        cq_ss, cq_sd, cq_ok = lsem("cq_ss"), lsem("cq_sd"), lsem("cq_ok")
        g_z, g_abs, g_min, g_ln, g_cum = (lsem("g_" + n) for n in ("z", "abs", "min", "ln", "cum"))
        g_e1, g_e2, g_bl, g_e3, g_qe, g_ke, g_kd = (lsem("g_" + n) for n in ("e1", "e2", "bl", "e3", "qe", "ke", "kd"))
        g_tp, g_tev, g_u, g_s = (lsem("g_" + n) for n in ("tp", "tev", "u", "s"))
        g_at, g_am, g_o, g_oev = (lsem("g_" + n) for n in ("at", "am", "o", "oev"))
        g_fin = lsem("g_fin")
        fin_out = lsem("fin_out")
        gn_v, gn_s, gn_ok = lsem("gn_v"), lsem("gn_s"), lsem("gn_ok")
        b_qm, b_sc, b_neg, b_exp, b_a, b_tp, b_pt, b_pv, b_o = (lsem("b_" + n) for n in ("qm", "sc", "neg", "exp", "a", "tp", "pt", "pv", "o"))
        ap_tp, ap_ev, ap_kr = lsem("ap_tp"), lsem("ap_ev"), lsem("ap_kr")
        x_mm, x_ev, a_qk = lsem("x_mm"), lsem("x_ev"), lsem("a_qk")
        a_sc, a_neg, a_exp, a_tp, a_pt, a_pv, a_o = (lsem("a_" + n) for n in ("sc", "neg", "exp", "tp", "pt", "pv", "o"))
        on_v, on_s, on_ok = lsem("on_v"), lsem("on_s"), lsem("on_ok")
        ot_tp, ot_hi, ot_lo = lsem("ot_tp"), lsem("ot_hi"), lsem("ot_lo")
        lo_n, hi_n = min(s.num for s in layer_sems), max(s.num for s in layer_sems)
        assert hi_n - lo_n + 1 == len(layer_sems)

        RANGES = [(0, 0, 0, 0, TC), (1, 0, TC, TC, TH - TC), (1, 1, 0, TH, TH)]
        U_ORDER = [[0, 1, 2, 3, 4, 5, 6, 7, 8], [1, 0, 9, 8, 7, 6, 5, 4, 3]]
        O_ORDER = [[0, 1, 2, 3, 4], [0, 4, 3, 2, 1]]
        N_STATE = len(U_ORDER[0])

        def state_count(d, c):
            if d == 0:
                return {0: 0, 2: 0}.get(c, c)
            return {1: 0, 9: 0, 0: 1}.get(c, 11 - c)

        def has_state(d, c):
            return c != (0, 1)[d]

        def entering(d, c):
            return Sini[:, d] if c == (2, 9)[d] else S[:, c]

        def heads_out(t):
            return oc[:, t, :].rearrange("p (a b v) -> p b a v", b=2, v=DV_C)

        def heads_ps():
            return ps[:, 4:6, 0:2 * DV_C].rearrange("p b (a v) -> p b a v", a=2)

        def keys_of(qi):
            return (0, 1) if qi == 0 else (1, NKT)

        def token_sums():
            return ps[:, 0, 0:2 * NT].rearrange("p (t c) -> p t c", c=2)[:, :, 0]

        LAG = 2
        K_ORDER = [3, 4, 5, 6, 7, 0, 1, 2]

        cv = lambda ap: ap.bitcast(F32)

        block = ctx.enter_context(nc.Block())

        @block.sync
        def _(sp):
            sp.dma_start(cosT[:, :], A["rope_cos"]).then_inc(s_tab, 16)
            sp.dma_start(sinT[:, :], A["rope_sin"]).then_inc(s_tab, 16)
            sp.dma_start(par[0:KD, :], A["c_ctx"].rearrange("(k p) -> k p", p=P)).then_inc(s_tab, 16)
            sp.dma_start(par[KD:2 * KD, :], A["c"].rearrange("b (k p) -> (b k) p", p=P)).then_inc(s_tab, 16)
            sp.dma_start(xs[:, 0, :], A["x_prompt"][0]).then_inc(s_xs, 16)
            sp.dma_start(xs[:, 1:NT, :], A["x_sample"][0].rearrange("(t p) d -> p t d", p=P)).then_inc(s_xs, 16)
            sp.wait_ge(s_xa, KD // 2)
            sp.wait_ge(s_xv, KD // 2)

            for c in range(NMC):
                src = A["w_mod"][0][:, c * MW:(c + 1) * MW].rearrange("(k p) n -> p k n", p=P)
                sp.dma_start(mraw[c][:, :, :], src).then_inc(m_raw[c], 16)

            with sp.Fori(0, DEPTH) as l:
                def slot(g):
                    return raw[:, g % 2, :].rearrange("p (k n) -> p k n", k=KD)

                def halves(dst, src, g):
                    n = dst.shape[1] // 2
                    for k in range(2):
                        sp.dma_start(dst[:, k * n:(k + 1) * n, :], src[:, k * n:(k + 1) * n, :]).then_inc(raw_in[g % 2], 16)

                def free(g, step=0):
                    if g >= 2:
                        sp.wait_ge(lo_ok, g - 1 + step)

                def load_up(w13, g, i, j, f0):
                    src = w13[l].rearrange("(k p) n -> p k n", p=P)
                    for s in range(2):
                        sp.dma_start(slot(g)[:, :, s * P:(s + 1) * P], src[:, :, bass.ds(i * 256 + (j * P + f0 + s * F), P)]).then_inc(raw_in[g % 2], 16)

                def load_down(w2, g, j, r0, n):
                    halves(slot(g)[:, 0:n, :], w2[l][r0:r0 + n * P, j * CW:(j + 1) * CW].rearrange("(k p) n -> p k n", p=P), g)

                def load_under(f, g, i=0):
                    c = (g - (G_FFN1, G_FFN2)[f]) - G_MOD
                    if not 0 <= c < N_UNDER[f]:
                        return
                    if c + V0[f] >= 2:
                        sp.wait_ge(v_mm, i * 2 + (c + V0[f] - 1))
                    w = A["w_mod"][l if f == 0 else (l + 1) % DEPTH]
                    src = w[:, bass.ds(i * (2 * CW) + ((2 * D, 0)[f] + c * CW), CW)].rearrange("(k p) n -> p k n", p=P)
                    sp.dma_start(uraw[:, g % 2], src).then_inc(v_in[g % 2], 16)

                def load_ffn(w13, w2, g, f):
                    for q, n in enumerate(PARTS):
                        f0 = sum(PARTS[:q]) * P
                        start = 0
                        if q == 0:
                            for j in range(4):
                                free(g + j)
                                load_up(w13, g + j, 0, j, f0)
                            sp.wait_ge(n_ulo, (1, 3)[f] * KD)
                            for j in range(2):
                                load_under(f, g + G_MOD + j)
                            start = 2
                        with sp.Fori(0, n // 2 - start) as i:
                            for j in range(2):
                                free(g + 2 * start + j, i * 2)
                                load_up(w13, g + j, i, 2 * start + j, f0)
                                load_under(f, g + 2 * start + j, i)
                        g += n
                        for j in range(NW2):
                            free(g + j)
                            load_down(w2, g + j, j, f0, n)
                            load_under(f, g + j)
                        g += NW2

                load_ffn(A["ffn1_w13"], A["ffn1_w2"], G_FFN1, 0)
                win = A["w_in"][l].rearrange("(k p) n -> p k n", p=P)
                COL = {"vr0": O_VR, "vr1": O_VR + CW, "vr2": O_VR + 2 * CW, "vb": O_VB, "c0": 0, "c1": CW, "c2": 2 * CW,
                       "qb": O_QB, "kb": O_KB}
                for n, name in enumerate(PROJ):
                    g = G_PROJ + n
                    free(g)
                    if name == "gl":
                        halves(slot(g)[:, :, 0:2 * GR], win[:, :, O_GL:O_GL + 2 * GR], g)
                    elif name in ("qc", "kc"):
                        for h in range(H_C):
                            c0 = {"qc": O_QC, "kc": O_KC}[name] + h * DK
                            sp.dma_start(slot(g)[:, :, h * HW:(h + 1) * HW], win[:, :, c0:c0 + HW]).then_inc(raw_in[g % 2], 16)
                    else:
                        halves(slot(g), win[:, :, COL[name]:COL[name] + CW], g)
                wo = A["w_out"][l].rearrange("(k p) n -> p k n", p=P)
                for n in range(NW2):
                    g = G_WOUT + n
                    free(g)
                    halves(slot(g), wo[:, :, n * CW:(n + 1) * CW], g)
                load_ffn(A["ffn2_w13"], A["ffn2_w2"], G_FFN2, 1)
                sp.wait_ge(l_done, 4)
                sp.sem_clear(range(lo_n, hi_n + 1))
                sp.sem_inc(s_go, 1)
            for t in range(NT):
                sp.wait_ge(s_ytm, t + 1)
                dst = O["y_prompt"][0] if t == 0 else O["y_sample"][0, (t - 1) * P:t * P, :]
                sp.dma_start(dst, ytm[:, t % 2, :]).then_inc(s_yout[t % 2], 16)
            sp.wait_ge(s_yout[0], 16 * 3)
            sp.wait_ge(s_yout[1], 16 * 2)

        @block.gpsimd
        def _(pool):
            n_const = [0]

            def made(ins):
                n_const[0] += 1
                ins.then_inc(s_const, 1)
                pool.wait_ge(s_const, n_const[0])

            made(pool.memset(ident[:, :], 0.0))
            made(pool.affine_select(out=ident[:, :], in_=ident[:, :], compare_op=ALU.not_equal, fill=1.0, base=0,
                                    pattern=[[-1, P]], channel_multiplier=1))
            made(pool.memset(ones[:, :], 1.0))
            made(pool.memset(mask[:, :, :], 1.0))
            made(pool.affine_select(out=mask[:, 0, :], in_=mask[:, 0, :], compare_op=ALU.is_ge, fill=0.0, base=0,
                                    pattern=[[1, P]], channel_multiplier=-1))
            made(pool.memset(mask[0:CH, 0, CH:P], 0.0))
            made(pool.affine_select(out=mask[:, 1, :], in_=mask[:, 1, :], compare_op=ALU.is_ge, fill=0.0, base=0,
                                    pattern=[[-1, P]], channel_multiplier=1))
            made(pool.memset(mask[CH:P, 1, 0:CH], 0.0))
            made(pool.memset(keep[:, :, :], 1.0))
            kc = keep[:, :, :].rearrange("p d (c t) -> p d c t", t=CH)
            made(pool.memset(kc[:, 0, :, 0:1], 0.0))
            made(pool.memset(kc[:, 1, :, CH - 1:CH], 0.0))
            made(pool.memset(comb[:, :], 0.0))
            for j in range(4):
                made(pool.affine_select(out=comb[:, :], in_=comb[:, :], compare_op=ALU.not_equal, fill=1.0, base=-32 * j,
                                        pattern=[[-1, 2]], channel_multiplier=1))
            made(pool.memset(grp[:, :], 0.0))
            for j in range(4):
                made(pool.memset(grp[32 * j:32 * j + 32, j:j + 1], 1.0))
            made(pool.memset(csp[:, :, :], 0.0))
            made(pool.memset(wgp[:, :, :], 0.0))
            made(pool.memset(Sini[:, :, :, :], 0.0))
            made(pool.memset(st[:, :], 0.0))
            made(pool.memset(eps, EPS))
            pool.wait_ge(s_ctp, 1)
            made(pool.memset(par[:, :], 0.0))

            def load_params(l):
                n_par = [0]

                def pin(dst, src):
                    n_par[0] += 1
                    pool.dma_start(dst, src).then_inc(par_in, 16)

                pin(par[R_BMOD:R_BMOD + NMT, :], A["b_mod"][l].rearrange("(r p) -> r p", p=P))
                pin(par[R_N1:R_N1 + KD, :], A["norm_ffn1"][l].rearrange("(r p) -> r p", p=P))
                pin(par[R_NM:R_NM + KD, :], A["norm_mix"][l].rearrange("(r p) -> r p", p=P))
                pin(par[R_N2:R_N2 + KD, :], A["norm_ffn2"][l].rearrange("(r p) -> r p", p=P))
                pin(par[R_FIN:R_FIN + KD, :], A["final_norm"].rearrange("(r p) -> r p", p=P))
                pin(par[R_QN:R_QN + 3, :], A["mla_q_norm"][l].rearrange("(r p) -> r p", p=P))
                pin(par[R_OG:R_OG + 3, :], A["mla_out_norm"][l].rearrange("(r p) -> r p", p=P))
                dn = A["diff_norm"][l].rearrange("(a n) -> a n", a=1)
                for r in range(2):
                    for c in range(2):
                        pin(par[R_OG + 3 + r:R_OG + 4 + r, c * DV_B:(c + 1) * DV_B], dn)
                gn = A["gla_norm"][l].rearrange("(a n) -> a n", a=1)
                at = 0
                while at < WC:
                    src0 = at % DV_C
                    n = min(DV_C - src0, P - at % P)
                    r = R_OG + 5 + at // P
                    pin(par[r:r + 1, at % P:at % P + n], gn[:, src0:src0 + n])
                    at += n
                for d, name in enumerate(("f", "b")):
                    bg = A["gla_bg_" + name][l].rearrange("(a n) -> a n", a=1)
                    wg = A["gla_wg_" + name][l]
                    for h in range(H_C):
                        n = min(HW, H_C * DK - h * DK)
                        r = R_BG + 2 * d + h // 2
                        pin(par[r:r + 1, (h % 2) * HW:(h % 2) * HW + n], bg[:, h * DK:h * DK + n])
                        pin(wgp[GR * d:GR * d + GR, d, h * HW:h * HW + n], wg[:, h * DK:h * DK + n])
                    s0 = A["state_gla_fwd" if d == 0 else "state_gla_bwd"][0, l].rearrange("(p h) k v -> h k p v", h=2)
                    for hh in range(2):
                        pin(Sini[HW * hh:HW * hh + DK, d, :, :], s0[hh])
                for n, name in enumerate(("diff_lq1", "diff_lk1", "diff_lq2", "diff_lk2")):
                    pin(lqk[:, n, :], A[name][l].rearrange("(a n) -> a n", a=1).broadcast_to([P, DH_B]))
                pin(kvw[:, :], A["mla_kv_norm"][l].rearrange("(a n) -> a n", a=1).broadcast_to([P, KV_RANK]))
                pin(lcon, A["layer_consts"][l])
                names["n_par"] = n_par[0]

            load_params(0)
            with pool.Fori(0, DEPTH) as l:
                pool.dma_start(ck[:, :], A["cache_diff_k"][0, l].rearrange("t h d -> t (h d)")).then_inc(kv_in, 16)
                pool.wait_ge(n_ulo, 2 * KD)
                pool.dma_start(vbs[:, 1, 0:WB], A["cache_diff_v"][0, l].rearrange("t h d -> t (h d)")).then_inc(kv_in, 16)
                pool.memset(vbs[:, :, WB:288], 0.0).then_inc(pool_c, 1)
                pool.wait_ge(ev_ok, PROJ.index("vb") + 1)
                pool.dma_start(O["new_diff_v"][0, l].rearrange("t h d -> t (h d)"), vbs[:, 0, 0:WB]).then_inc(out_in, 16)
                pool.wait_ge(cq_ok, 1)
                pool.dma_start(O["new_mla_ckv"][0, l], cqkv[:, 0, Q_RANK:Q_RANK + KV_RANK]).then_inc(out_in, 16)
                pool.dma_start(O["new_mla_krope"][0, l], cqkv[:, 0, 640:672]).then_inc(out_in, 16)
                pool.wait_ge(bk_ev, 2)
                pool.dma_start(O["new_diff_k"][0, l].rearrange("t h d -> t (h d)"), ck[:, :]).then_inc(out_in, 16)
                for d in range(2):
                    dst = O["new_gla_fwd" if d == 0 else "new_gla_bwd"][0, l].rearrange("(p h) k v -> h k p v", h=2)
                    pool.wait_ge(g_fin, d + 1)
                    for hh in range(2):
                        pool.dma_start(dst[hh], S[HW * hh:HW * hh + DK, S_FIN[d], :, :]).then_inc(out_in, 16)
                    if d == 0:
                        pool.wait_ge(out_in, l * (16 * 8) + 16 * 6)
                        pool.sem_inc(fin_out, 1)
                pool.wait_ge(gn_ok, 1)
                pool.dma_start(wuq[:, :, :], A["mla_w_uq"][l].rearrange("(k p) n -> p k n", p=P)).then_inc(aw_in, 16)
                pool.dma_start(wuk[:, :, :], A["mla_w_uk"][l].rearrange("(k p) n -> p k n", p=P)).then_inc(aw_in, 16)
                pool.dma_start(wuv[:, :, :], A["mla_w_uv"][l].rearrange("(k p) n -> p k n", p=P)).then_inc(aw_in, 16)
                pool.dma_start(cc[:, :], A["cache_mla_ckv"][0, l]).then_inc(aw_in, 16)
                pool.dma_start(cck[:, :], A["cache_mla_krope"][0, l]).then_inc(aw_in, 16)
                pool.memset(vas[:, :, WA:416], 0.0).then_inc(pool_c, 1)
                pool.wait_ge(ot_lo, KD)
                load_params((l + 1) % DEPTH)
                pool.wait_ge(out_in, (l + 1) * (16 * 8))
                pool.wait_ge(pool_c, 2)
                pool.sem_inc(l_done, 1)
                pool.wait_ge(s_go, l + 1)

        @block.scalar
        def _(act):
            steps = [0]

            def link(ins):
                steps[0] += 1
                ins.then_inc(act_c, 1)
                act.wait_ge(act_c, steps[0])

            def hi(g, step=0):
                act.wait_ge(raw_in[g % 2], raw_need(g) + step * 16)
                if g >= 2:
                    act.wait_ge(mm_ok, g - 1 + step)
                act.activation(w_hi[:, g % 2, :], raw[:, g % 2, :], ACT.Copy).then_inc(hi_ok, 1)

            X_DONE = (0, 3 * KD, 4 * KD, 7 * KD)

            def squares(n, m):
                k = (n - 1) * KD + m
                act.wait_ge(x_upd, X_DONE[n] - KD + m + 1)
                if k >= 2:
                    act.wait_ge(n_sqd, k - 1)
                act.activation(sq[:, m % 2, :], xT[:, m, :], ACT.Square).then_inc(n_sq, 1)

            def norm(n, between=None):
                act.wait_ge(n_ss, n + 1)
                act.activation(sd5[:, :], token_sums(), ACT.Sqrt, bias=eps, scale=1.0 / D).then_inc(n_std, 1)
                if between:
                    between()
                sh = 3 * n * KD
                for m in range(KD):
                    act.wait_ge(n_xn, n * KD + m + 1)
                    if m >= 2:
                        act.wait_ge(n_ulo, n * KD + m - 1)
                    for c, t0, t1 in ((0, 0, TC), (1, TC, T)):
                        act.activation(u32[:, m % 2, t0:t1], xn[:, m % 2, t0:t1], ACT.Identity,
                                       bias=modT[:, sh + m, c:c + 1], scale=gains[:, n, m, c:c + 1]).then_inc(n_u32, 1)
                    act.wait_ge(n_u32, 2 * (n * KD + m + 1))
                    act.activation(u_hi[:, m, :], u32[:, m % 2, :], ACT.Copy).then_inc(n_uhi, 1)

            def ffn(g, up0, norm_after):
                for q, n in enumerate(PARTS):
                    with act.Fori(0, n // 2) as i:
                        for j in range(2):
                            k = up0 + j
                            act.wait_ge(mm_ok, g + j + 1 + i * 2)
                            if k >= 2:
                                act.wait_ge(h32_ok, k - 1 + i * 2)
                            act.activation(silu_a[:, j, :].rearrange("p (b t) -> p b t", b=2),
                                           ps[:, 4 * ((g + j) % 2):4 * ((g + j) % 2) + 2, 0:TH], ACT.Silu).then_inc(sil_ok, 1)
                            act.wait_ge(h32_ok, k + 1 + i * 2)
                            act.activation(h_hi[:, bass.ds(i * 2 + j, 1), :].rearrange("p a t -> p (a t)"), h32[:, j, :],
                                           ACT.Copy).then_inc(hhi_ok, 1)
                            hi(g + j + 2, i * 2)
                    g += n
                    up0 += n
                    for j in range(NW2):
                        act.wait_ge(mm_ok, g + j + 1)
                        if g + j + 2 < N_CHUNK:
                            hi(g + j + 2)
                        if q == len(PARTS) - 1:
                            for m in (2 * j, 2 * j + 1):
                                squares(norm_after, m)
                    g += NW2

            act.wait_ge(s_ctp, 1)
            act.activation(csp[:, :, 0:2].rearrange("p k c -> p c k"), ps[:, 0, 0:2 * KD].rearrange("p (c k) -> p c k", c=2),
                           ACT.Silu).then_inc(s_csil, 1)
            for m in range(KD):
                if m % 2:
                    continue
                act.wait_ge(s_xtp, m + 1)
                b = 2 * (m % 4)
                act.activation(xT[:, m, :], psf[:, b * 512:b * 512 + T], ACT.Copy).then_inc(s_xa, 1)

            act.wait_ge(s_xa, KD // 2)
            for m in range(KD):
                if m % 2:
                    act.wait_ge(s_xv, m // 2 + 1)
                if m >= 2:
                    act.wait_ge(s_sqd, m - 1)
                act.activation(sq[:, m % 2, :], xT[:, m, :], ACT.Square).then_inc(s_sq, 1)
            for c in range(NMC):
                act.wait_ge(m_mm, c + 1)
                act.activation(mrows[:, c, :], ps[:, c, :], ACT.Copy).then_inc(m_row, 1)
            act.wait_ge(s_gain, 1)

            with act.Fori(0, DEPTH) as l:
                steps[0] = 0
                norm(0, lambda: (hi(0), hi(1)))
                act.wait_ge(lam_s, 1)
                act.activation(lexp, lam2, ACT.Exp).then_inc(lam_e, 1)
                ffn(G_FFN1, 0, 1)
                act.wait_ge(mod_ok, 1)
                norm(1)
                def gate_logs(d):
                    act.wait_ge(g_min, d + 1)
                    link(act.activation(gab[d][:, :, :], gb[d][:, :, :], ACT.Abs))
                    link(act.activation(gab[d][:, :, :], gab[d][:, :, :], ACT.Exp, scale=-1.0))
                    act.activation(gab[d][:, :, :], gab[d][:, :, :], ACT.Ln, bias=1.0).then_inc(g_ln, 1)

                def gate_exps(d):
                    act.wait_ge(g_cum, d + 1)
                    act.activation(gqe[d][:, :, :], gcum[d][:, :, :], ACT.Exp, scale=1.0 / GATE_NORM).then_inc(g_e1, 1)
                    tot = gcum[d][:, :, :].rearrange("p a (c t) -> p a c t", t=CH)[:, :, :, (CH - 1, 0)[d]]
                    link(act.activation(gtot[d][:, :, :], tot, ACT.Exp, scale=1.0 / GATE_NORM))
                    act.wait_ge(g_bl, d + 1)
                    act.activation(gkd[d][:, :, :], gb[d][:, :, :], ACT.Exp, scale=1.0 / GATE_NORM).then_inc(g_e3, 1)
                    link(act.activation(gke[d][:, :, :], gcum[d][:, :, :], ACT.Exp, scale=-1.0 / GATE_NORM))
                    act.sem_inc(g_e2, 1)

                for n, name in enumerate(PROJ):
                    g = G_PROJ + n
                    b = 4 * (g % 2)
                    act.wait_ge(mm_ok, g + 1)
                    four = ps[:, b:b + 4, 0:TH]
                    tm = psf[:, b * 512:b * 512 + NT * CW].rearrange("p (t n) -> p t n", n=CW)
                    if name == "gl":
                        act.activation(glT[:, :].rearrange("p (b t) -> p b t", b=2), ps[0:2 * GR, b:b + 2, 0:TH], ACT.Copy).then_inc(ev_ok, 1)
                    elif name in ("qc", "kc", "qb"):
                        dst = {"qc": qcT, "kc": kcT, "qb": qbT}[name]
                        act.activation(dst[:, :, :].rearrange("p m (b t) -> p (m b) t", b=2), four, ACT.Copy).then_inc(ev_ok, 1)
                    elif name == "kb":
                        f2 = ps[:, b:b + 4, :].rearrange("p (m b) t -> p m b t", b=2)
                        act.activation(kbT[:, :, 0:TC], f2[:, :, 0, 0:TC], ACT.Copy)
                        act.activation(kbT[:, :, TC + PAST:PAST + TH], f2[:, :, 0, TC:TH], ACT.Copy)
                        act.activation(kbT[:, :, PAST + TH:NKEY], f2[:, :, 1, 0:TH], ACT.Copy).then_inc(ev_ok, 1)
                    elif name == "vr0":
                        act.wait_ge(cq_ss, 1)
                        act.activation(vcs[:, :, 0:CW], tm, ACT.Copy).then_inc(ev_ok, 1)
                    elif name == "vr1":
                        act.activation(vcs[:, :, CW:WC], tm[:, :, 0:P], ACT.Copy)
                        act.activation(rcs[:, :, 0:P], tm[:, :, P:CW], ACT.Silu).then_inc(ev_ok, 1)
                    elif name == "vr2":
                        act.activation(rcs[:, :, P:WC], tm, ACT.Silu).then_inc(ev_ok, 1)
                    elif name == "vb":
                        act.activation(vbs[:, 0, 0:WB], tm[:, 0, :], ACT.Copy)
                        act.activation(vbs[:, 2:NKT, 0:WB], tm[:, 1:NT, :], ACT.Copy).then_inc(ev_ok, 1)
                    else:
                        c0 = int(name[1]) * CW
                        w = min(CW, 672 - c0)
                        act.activation(cqkv[:, :, c0:c0 + w], tm[:, :, 0:w], ACT.Copy).then_inc(ev_ok, 1)
                    hi(g + 2)
                    if n == Z_AT:
                        gate_logs(0)
                    elif name == "kc":
                        gate_exps(0)
                    elif name == "c2":
                        act.wait_ge(ev_ok, n + 1)
                        for t in range(NT):
                            act.activation(vcs[:, t, 0:Q_RANK], cqkv[:, t, 0:Q_RANK], ACT.Square, accum_out=ss10[:, t:t + 1])
                            last = act.activation(rcs[:, t, 0:KV_RANK], cqkv[:, t, Q_RANK:640], ACT.Square, accum_out=ss10[:, NT + t:NT + t + 1])
                        last.then_inc(cq_ss, 1)
                        act.wait_ge(cq_ss, 1)
                        act.activation(rs10[:, 0:NT], ss10[:, 0:NT], ACT.Sqrt, bias=eps, scale=1.0 / Q_RANK)
                        act.activation(rs10[:, NT:2 * NT], ss10[:, NT:2 * NT], ACT.Sqrt, bias=eps, scale=1.0 / KV_RANK).then_inc(cq_ss, 1)
                def turned_keys(d):
                    for t in range(NT):
                        act.wait_ge(g_tp, d * NT + t + 1)
                        act.activation(kdt[:, t, :, :], ps[:, 4 + t % 2, 0:256].rearrange("p (a k) -> p a k", a=2), ACT.Copy).then_inc(g_tev, 1)

                turned_keys(0)
                act.wait_ge(bk_tp, 1)
                act.activation(kbT[:, :, TC:TC + PAST], ps[:, 6, 0:256].rearrange("p (m t) -> p m t", m=2), ACT.Copy).then_inc(bk_ev, 1)
                act.wait_ge(bk_tp, 2)
                act.activation(ck[:, :], ps[:, 7, 0:256], ACT.Copy).then_inc(bk_ev, 1)
                gate_logs(1)
                gate_exps(1)
                for n, t in enumerate(O_ORDER[0]):
                    act.wait_ge(g_o, n + 1)
                    act.activation(heads_out(t), heads_ps(), ACT.Copy).then_inc(g_oev, 1)
                turned_keys(1)
                act.wait_ge(gn_v, NT)
                act.activation(crs, css, ACT.Sqrt, bias=eps, scale=1.0 / DV_C).then_inc(gn_s, 1)
                NB = H_B * NT

                def scores_view(s, qi):
                    if qi == 0:
                        return ps[:, s, 0:P], lambda tile: tile[:, 0:P]
                    return ps[:, s:s + 2, 0:TH], lambda tile: tile[:, :].rearrange("p (b t) -> p b t", b=2)

                def turn_copy(n, s_tp, s_pv, s_pt):
                    nk = 1 if n % NT == 0 else NT
                    act.wait_ge(s_tp, n + 1)
                    if n >= 2:
                        act.wait_ge(s_pv, n - 1)
                    act.activation(pt[n % 2][:, 0:nk, :].rearrange("p a t -> p (a t)"), psf[:, 4 * 512:4 * 512 + nk * P], ACT.Copy).then_inc(s_pt, 1)

                act.wait_ge(out_in, (l + 1) * (16 * 8))
                for n in range(NB + 2):
                    if n < NB:
                        for j in range(2):
                            act.wait_ge(b_neg, 2 * n + j + 1)
                            if n >= 3 and j == 0:
                                act.wait_ge(b_tp, n - 2)
                            if n >= 2:
                                act.wait_ge(b_a, n - 1)
                            src, view = scores_view(2 * j, n % NT)
                            c = 2 * (n % 2) + j
                            act.activation(view(p1[n % 2] if j else p0[n % 3]), src, ACT.Exp, bias=aneg[:, c:c + 1],
                                           accum_out=asum[:, c:c + 1]).then_inc(b_exp, 1)
                    if n >= 2:
                        turn_copy(n - 2, b_tp, b_pv, b_pt)
                for s in range(6):
                    act.wait_ge(ap_tp, s + 1)
                    b = 2 * (s % 4) * 512
                    if s < 3:
                        ins = act.activation(cqT[:, s, :], psf[:, b:b + T], ACT.Copy, scale=parT[:, R_QN + s:R_QN + s + 1])
                    elif s < 5:
                        ins = act.activation(ckvT[:, s - 3, :], psf[:, b:b + NKEY], ACT.Copy)
                    else:
                        ins = act.activation(krT[:, :], psf[0:DR, b:b + NKEY], ACT.Copy)
                    ins.then_inc(ap_ev, 1)
                for t in range(NKT):
                    act.wait_ge(ap_tp, 6 + t + 1)
                    act.activation(vas[:, t, 0:WA], ps[:, t, 0:WA], ACT.Copy).then_inc(ap_ev, 1)
                SA = DQ ** -0.5
                NA = H_A * NT

                def head_piece(r):
                    h, k = r // 4, r % 4
                    if h >= 2:
                        act.wait_ge(a_sc, (h - 1) * NT)
                    act.wait_ge(x_mm, r + 1)
                    if k < 2:
                        ins = act.activation(qA[h % 2][0:DQ, k * TH:(k + 1) * TH], ps[0:DQ, 7, 0:TH], ACT.Copy, scale=SA)
                    else:
                        c0 = (k - 2) * (NKEY // 2)
                        ins = act.activation(kA[h % 2][0:DN, c0:c0 + NKEY // 2], ps[0:DN, 7, 0:NKEY // 2], ACT.Copy)
                    ins.then_inc(x_ev, 1)

                for r in range(4):
                    head_piece(r)
                for n in range(NA + 2):
                    h, qi = n // NT, n % NT
                    if n < NA:
                        act.wait_ge(a_neg, n + 1)
                        if n >= 3:
                            act.wait_ge(a_tp, n - 2)
                        src, view = scores_view(2 * (n % 2), qi)
                        act.activation(view(pa[n % 3]), src, ACT.Exp, bias=aneg[:, n % 2:n % 2 + 1],
                                       accum_out=asum[:, n % 2:n % 2 + 1]).then_inc(a_exp, 1)
                    if n >= 2:
                        turn_copy(n - 2, a_tp, a_pv, a_pt)
                    if qi < 4 and h < H_A - 1:
                        head_piece(4 * (h + 1) + qi)
                    if n == NT + 1:
                        act.wait_ge(on_v, 1)
                        act.activation(crs, css, ACT.Sqrt, bias=eps, scale=1.0 / DV_B).then_inc(on_s, 1)
                act.wait_ge(on_v, 2)
                act.activation(rs10[:, 0:NT], ss10[:, 0:NT], ACT.Sqrt, bias=eps, scale=1.0 / WA).then_inc(on_s, 1)
                for n, k in enumerate(K_ORDER):
                    act.wait_ge(ot_tp, n + 1)
                    b = 2 * (n % 4) * 512
                    act.activation(u_hi[:, k, :], psf[:, b:b + T], ACT.Copy, scale=parT[:, R_OG + k:R_OG + k + 1]).then_inc(ot_hi, 1)
                for n in range(NW2):
                    g = G_WOUT + n
                    act.wait_ge(mm_ok, g + 1)
                    hi(g + 2)
                    for m in (2 * n, 2 * n + 1):
                        squares(2, m)
                norm(2)
                ffn(G_FFN2, NF, 3)
                act.drain().then_inc(l_done, 1)
                act.wait_ge(s_go, l + 1)
            act.wait_ge(f_ss, 1)
            act.activation(sd5[:, :], token_sums(), ACT.Sqrt, bias=eps, scale=1.0 / D).then_inc(f_std, 1)
            for m in range(KD):
                act.wait_ge(f_xn, m + 1)
                act.activation(yT[:, m, :], xn[:, m % 2, :], ACT.Copy, scale=parT[:, R_FIN + m:R_FIN + m + 1]).then_inc(s_yt, 1)
            for t in range(NT):
                act.wait_ge(s_ytp, t + 1)
                if t >= 2:
                    act.wait_ge(s_yout[t % 2], 16 * (t // 2))
                b = 2 * (t % 4) * 512
                act.activation(ytm[:, t % 2, :], psf[:, b:b + D], ACT.Copy).then_inc(s_ytm, 1)

        @block.vector
        def _(dve):
            steps = [0]

            def link(ins):
                steps[0] += 1
                ins.then_inc(dve_c, 1)
                dve.wait_ge(dve_c, steps[0])

            def lo(g, step=0):
                dve.wait_ge(hi_ok, g + 1 + step)
                dve.tensor_tensor(w_lo[:, g % 2, :], raw[:, g % 2, :], cv(w_hi[:, g % 2, :]), ALU.subtract).then_inc(lo_ok, 1)

            def add_square(m, made, added, k):
                dve.wait_ge(made, k + 1)
                if m == 0:
                    dve.tensor_copy(sqsum[:, :], sq[:, 0, :]).then_inc(added, 1)
                else:
                    dve.wait_ge(added, k)
                    dve.tensor_tensor(sqsum[:, :], sqsum[:, :], sq[:, m % 2, :], ALU.add).then_inc(added, 1)

            def inverse_rms(rooted, diagonal, spread, v):
                dve.wait_ge(rooted, v)
                link(dve.reciprocal(rs5[:, :], sd5[:, :]))
                dve.tensor_tensor(dg[:, :, :], ident[:, :].unsqueeze(1).broadcast_to([P, NT, P]), rs5[:, :].unsqueeze(2).broadcast_to([P, NT, P]),
                                  ALU.mult).then_inc(diagonal, 1)
                dve.wait_ge(spread, v)
                link(dve.tensor_copy(rstd[:, :].rearrange("p (b t) -> p b t", b=2), ps[:, 0:2, 0:TH]))

            def norm(n, between=None):
                inverse_rms(n_std, n_dg, n_bc, n + 1)
                if between:
                    between()
                for m in range(KD + 1):
                    if m < KD:
                        if m >= 2:
                            dve.wait_ge(n_u32, 2 * (n * KD + m - 1))
                        dve.tensor_tensor(xn[:, m % 2, :], xT[:, m, :], rstd[:, :], ALU.mult).then_inc(n_xn, 1)
                    if m >= 1:
                        dve.wait_ge(n_uhi, n * KD + m)
                        dve.tensor_tensor(u_lo[:, m - 1, :], u32[:, (m - 1) % 2, :], cv(u_hi[:, m - 1, :]), ALU.subtract).then_inc(n_ulo, 1)

            def update_x(kind, bank, m):
                for n, (c, b, o, t0, w) in enumerate(RANGES):
                    last = dve.scalar_tensor_tensor(out=xT[:, m, t0:t0 + w], in0=ps[:, bank + b, o:o + w], scalar=gates[:, kind, m, c:c + 1],
                                                    in1=xT[:, m, t0:t0 + w], op0=ALU.mult, op1=ALU.add)
                return last

            def gain(n, r):
                w = parT[:, r:r + KD].unsqueeze(2).broadcast_to([P, KD, 2])
                return dve.scalar_tensor_tensor(out=gains[:, n], in0=modT[:, (3 * n + 1) * KD:(3 * n + 2) * KD, :], scalar=1.0, in1=w,
                                                op0=ALU.add, op1=ALU.mult)

            def mod_under(f, g, i=0):
                c = (g - (G_FFN1, G_FFN2)[f]) - G_MOD
                if 0 <= c < N_UNDER[f]:
                    dve.tensor_copy(urows[:, g % 2, :].rearrange("p (b n) -> p b n", b=2),
                                    ps[:, 4 * (g % 2) + 2:4 * (g % 2) + 4, TH:TH + P]).then_inc(v_row, 1)
                if 2 <= c < N_UNDER[f] + 2:
                    r0 = i * 4 + ((2 * KD, 0)[f] + 2 * (c - 2))
                    dve.tensor_tensor(modT[:, bass.ds(r0, 2), :], ps[:, 4 * (g % 2) + 2, TH + P:TH + P + 4].rearrange("p (r c) -> p r c", c=2),
                                      parT[:, bass.ds(r0, 2)].unsqueeze(2).broadcast_to([P, 2, 2]), ALU.add).then_inc(v_ev, 1)

            def ffn(f, g, up0, kind, x0):
                for q, n in enumerate(PARTS):
                    def up_step(j, k, i):
                        b = 4 * ((g + j) % 2)
                        dve.wait_ge(sil_ok, k + 1 + i * 2)
                        if k >= 2:
                            dve.wait_ge(hlo_ok, k - 1 + i * 2)
                        if f == 1 and q == 0 and j == 1:
                            dve.tensor_copy(parT[:, 0:P], ps[:, 7, TH:TH + P]).then_inc(par_ok, 1)
                        mod_under(f, g + j, i)
                        dve.tensor_tensor(h32[:, j % 2, :].rearrange("p (b t) -> p b t", b=2), ps[:, b + 2:b + 4, 0:TH],
                                          silu_a[:, j % 2, :].rearrange("p (b t) -> p b t", b=2), ALU.mult).then_inc(h32_ok, 1)
                        dve.wait_ge(hhi_ok, k + 1 + i * 2)
                        tile = bass.ds(i * 2 + j, 1)
                        dve.tensor_tensor(h_lo[:, tile, :].rearrange("p a t -> p (a t)"), h32[:, j % 2, :],
                                          cv(h_hi[:, tile, :]).rearrange("p a t -> p (a t)"), ALU.subtract).then_inc(hlo_ok, 1)
                        lo(g + j + 2, i * 2)

                    start = 0
                    if q == 0:
                        for j in range(4):
                            up_step(j, up0 + j, 0)
                        if f == 1:
                            dve.wait_ge(par_ok, 1)
                        start = 4
                    with dve.Fori(0, (n - start) // 2) as i:
                        for j in range(start, start + 2):
                            up_step(j, up0 + j, i)
                    g += n
                    up0 += n
                    if q == 0 and f == 0:
                        dve.wait_ge(v_ev, KD // 2)
                        link(dve.tensor_scalar(gates[:, 0], modT[:, 2 * KD:3 * KD, :], 0.5, None, ALU.mult))
                    if x0 > 0 or q > 0:
                        dve.wait_ge(x_upd, x0)
                    for j in range(NW2):
                        dve.wait_ge(mm_ok, g + j + 1)
                        mod_under(f, g + j)
                        for m2 in range(2):
                            update_x(kind, 4 * ((g + j) % 2) + 2 * m2, 2 * j + m2).then_inc(x_upd, 1)
                        if q == len(PARTS) - 1:
                            for m in (2 * j, 2 * j + 1):
                                add_square(m, n_sq, n_sqd, 2 * f * KD + m)
                        if g + j + 2 < N_CHUNK:
                            lo(g + j + 2)
                    g += NW2
                    x0 += KD
                    if q == 0 and f == 1:
                        dve.wait_ge(v_ev, V0[1] + N_UNDER[1])
                        gain(0, R_N1)

            def rope(x, rot, cos, sin, lk):
                swap = [i + 8 if i % 16 < 8 else i - 8 for i in range(32)]
                lk(dve.stream_shuffle(rot, x, swap))
                dve.tensor_tensor(x, x, cos, ALU.mult)
                lk(dve.tensor_tensor(rot, rot, sin, ALU.mult))
                return dve.tensor_tensor(x, x, rot, ALU.add)

            dve.wait_ge(s_const, 1)
            for m in range(KD):
                if m % 2 == 0:
                    continue
                dve.wait_ge(s_xtp, m + 1)
                b = 2 * (m % 4)
                dve.tensor_copy(xT[:, m, :], psf[:, b * 512:b * 512 + T]).then_inc(s_xv, 1)

            for m in range(KD):
                add_square(m, s_sq, s_sqd, m)
            dve.wait_ge(s_ptp, 1)
            dve.tensor_copy(parT[:, 0:P], ps[:, 4 + NMC - 1, P:2 * P]).then_inc(s_par, 1)
            dve.wait_ge(s_par, 1)
            for c in range(NMC):
                n = MW // P
                dve.wait_ge(m_tp, c + 1)
                dve.tensor_tensor(modT[:, c * n:(c + 1) * n, :], ps[:, 4 + c, 0:2 * n].rearrange("p (r c) -> p r c", c=2),
                                  parT[:, c * n:(c + 1) * n].unsqueeze(2).broadcast_to([P, n, 2]), ALU.add).then_inc(m_ev, 1)
            dve.wait_ge(m_ev, NMC)
            gain(0, R_N1).then_inc(s_gain, 1)

            with dve.Fori(0, DEPTH) as l:
                steps[0] = 0
                norm(0, lambda: (lo(0), lo(1)))
                dve.wait_ge(par_in, (l + 1) * (16 * names["n_par"]))
                for n in range(2):
                    last = dve.tensor_tensor_reduce(out=lqk[:, 2 * n, :], in0=lqk[:, 2 * n, :], in1=lqk[:, 2 * n + 1, :], scale=1.0,
                                                    scalar=0.0, op0=ALU.mult, op1=ALU.add, accum_out=lam2[:, n:n + 1])
                last.then_inc(lam_s, 1)
                dve.wait_ge(lam_e, 1)
                link(dve.tensor_tensor(ldif, lexp[:, 1:2], lexp[:, 0:1], ALU.subtract))
                dve.tensor_tensor(nlam, ldif, lcon[:, 0:1], ALU.subtract)
                link(dve.tensor_scalar(parT[:, R_OG + 3:R_OG + 5], parT[:, R_OG + 3:R_OG + 5], lcon[:, 1:2], None, ALU.mult))
                ffn(0, G_FFN1, 0, 0, 0)
                dve.wait_ge(v_ev, N_UNDER[0])
                gain(1, R_NM)
                gain(2, R_N2)
                for n in (1, 2):
                    last = dve.tensor_scalar(gates[:, n], modT[:, (3 * n + 2) * KD:(3 * n + 3) * KD, :], (1.0, 0.5)[n - 1], None, ALU.mult)
                link(last)
                dve.sem_inc(mod_ok, 1)
                norm(1)
                cos2 = cosT[:, :].unsqueeze(1).broadcast_to([P, 2, TL])
                sin2 = sinT[:, :].unsqueeze(1).broadcast_to([P, 2, TL])

                def gate_bias(d):
                    dve.wait_ge(g_z, d + 1)
                    for p in range(2):
                        last = dve.tensor_scalar(gb[d][:, p, :].rearrange("p (b t) -> p b t", b=2), ps[:, (4, 0)[d] + 2 * p:(4, 0)[d] + 2 * p + 2, 0:TH],
                                                 parT[:, R_BG + 2 * d + p:R_BG + 2 * d + p + 1], None, ALU.add)
                    last.then_inc(g_min, 1)

                def gate_sums(d):
                    rev = slice(None, None, -1) if d else slice(None)
                    dve.wait_ge(g_ln, d + 1)
                    link(dve.scalar_tensor_tensor(out=gb[d][:, :, :], in0=gb[d][:, :, :], scalar=0.0, in1=gab[d][:, :, :], op0=ALU.min, op1=ALU.subtract))
                    for p in range(2):
                        last = dve.tensor_tensor_scan(gcum[d][:, p, rev], keep[:, d, rev], gb[d][:, p, rev], 0.0, ALU.mult, ALU.add)
                    last.then_inc(g_cum, 1)
                    dve.wait_ge(g_cum, d + 1)
                    c4 = gcum[d][:, :, :].rearrange("p a (c t) -> p (a c) t", t=CH)
                    e = (CH - 1, 0)[d]
                    dve.tensor_tensor(gb[d][:, :, :].rearrange("p a (c t) -> p (a c) t", t=CH),
                                      c4[:, :, e:e + 1].broadcast_to([P, 2 * NCH, CH]), c4, ALU.subtract).then_inc(g_bl, 1)

                def decay(d, step):
                    if step == 0:
                        dve.wait_ge(g_e1, d + 1)
                        dve.scalar_tensor_tensor(out=gqe[d][:, :, :], in0=qcT[:, :, :], scalar=DK ** -0.5, in1=gqe[d][:, :, :],
                                                 op0=ALU.mult, op1=ALU.mult).then_inc(g_qe, 1)
                    elif step == 1:
                        dve.wait_ge(g_e3, d + 1)
                        dve.tensor_tensor(gkd[d][:, :, :], kcT[:, :, :], gkd[d][:, :, :], ALU.mult).then_inc(g_kd, 1)
                    else:
                        dve.wait_ge(g_e2, d + 1)
                        dve.tensor_tensor(gke[d][:, :, :], kcT[:, :, :], gke[d][:, :, :], ALU.mult).then_inc(g_ke, 1)

                for n, name in enumerate(PROJ):
                    if n == Z_AT:
                        gate_bias(0)
                    lo(G_PROJ + n + 2)
                    if name in ("kb", "qb"):
                        dve.wait_ge(ev_ok, n + 1)
                        link(rope({"kb": kbT[:, :, TC + PAST:NKEY], "qb": qbT[:, :, TC:T]}[name], rotb[:, :, :], cos2, sin2, link))
                    elif name == "qc":
                        gate_sums(0)
                    elif name == "kc":
                        dve.wait_ge(ev_ok, n + 1)
                        for step in range(3):
                            decay(0, step)
                    elif name == "c2":
                        dve.wait_ge(cq_ss, 2)
                        link(dve.reciprocal(ss10, rs10))
                        for t in range(NT):
                            dve.tensor_scalar(cqkv[:, t, 0:Q_RANK], cqkv[:, t, 0:Q_RANK], ss10[:, t:t + 1], None, ALU.mult)
                            last = dve.tensor_scalar(cqkv[:, t, Q_RANK:640], cqkv[:, t, Q_RANK:640], ss10[:, NT + t:NT + t + 1], None, ALU.mult)
                        link(last)
                        kv = cqkv[:, :, Q_RANK:640]
                        dve.tensor_tensor(kv, kv, kvw[:, :].unsqueeze(1).broadcast_to([P, NT, KV_RANK]), ALU.mult).then_inc(cq_ok, 1)

                def states(d):
                    for n, c in enumerate(U_ORDER[d]):
                        dve.wait_ge(g_u, d * N_STATE + n + 1)
                        upd = ps[:, 6 + n % 2, 0:2 * DV_C].rearrange("p (a v) -> p a v", a=2)
                        nxt = S_FIN[d] if n == 1 else c + (1, -1)[d]
                        if d == 1 and n >= 2 and nxt == S_FIN[0]:
                            dve.wait_ge(fin_out, 1)
                        if n == 0:
                            dve.tensor_copy(S[:, nxt], upd).then_inc(g_s, 1)
                            continue
                        dve.wait_ge(g_s, d * N_STATE + n)
                        src = entering(d, c)
                        for a in range(2):
                            last = dve.scalar_tensor_tensor(out=S[:, nxt, a, :], in0=src[:, a, :], scalar=gtot[d][:, a, c:c + 1], in1=upd[:, a, :],
                                                            op0=ALU.mult, op1=ALU.add)
                        last.then_inc(g_s, 1)
                        if n == 1:
                            dve.wait_ge(g_s, d * N_STATE + 2)
                            dve.sem_inc(g_fin, 1)

                def masked(d, n):
                    dve.wait_ge(g_at, d * NT + n + 1)
                    if d * NT + n >= 2:
                        dve.wait_ge(g_o, d * NT + n - 1)
                    b = 2 * (n % 2)
                    dve.tensor_tensor(am[:, n % 2, :].rearrange("p (b a t) -> p b a t", b=2, a=2),
                                      ps[:, b:b + 2, 0:2 * P].rearrange("p b (a t) -> p b a t", a=2),
                                      mask[:, d, :].unsqueeze(1).unsqueeze(1).broadcast_to([P, 2, 2, P]), ALU.mult).then_inc(g_am, 1)

                def add_back(n):
                    t = O_ORDER[1][n]
                    dve.wait_ge(g_o, NT + n + 1)
                    dve.tensor_tensor(heads_out(t), heads_ps(), heads_out(t), ALU.add).then_inc(g_oev, 1)

                def head_squares(n):
                    t = O_ORDER[1][n]
                    dve.wait_ge(g_oev, NT + n + 1)
                    link(dve.tensor_tensor(osq[:, t, :], oc[:, t, :], oc[:, t, :], ALU.mult))
                    dve.tensor_reduce(css[:, t * H_C:(t + 1) * H_C], osq[:, t, :].rearrange("p (h v) -> p h v", h=H_C), AX.X, ALU.add).then_inc(gn_v, 1)

                gate_bias(1)
                states(0)
                gate_sums(1)
                for n in range(NT):
                    masked(0, n)
                    if 1 <= n <= 3:
                        decay(1, n - 1)
                states(1)
                for n in range(NT):
                    masked(1, n)
                    if n >= 1:
                        add_back(n - 1)
                    if n >= 2:
                        head_squares(n - 2)
                add_back(NT - 1)
                head_squares(NT - 2)
                head_squares(NT - 1)

                def gla_gate():
                    dve.wait_ge(gn_s, 1)
                    link(dve.reciprocal(css, crs))
                    och = oc[:, :, :].rearrange("p t (h v) -> p t h v", h=H_C)
                    link(dve.tensor_tensor(och, och, css.rearrange("p (t h) -> p t h", h=H_C).unsqueeze(3).broadcast_to([P, NT, H_C, DV_C]), ALU.mult))
                    dve.tensor_tensor(omix[:, :, WA + WB:D], oc[:, :, :], rcs[:, :, :], ALU.mult).then_inc(gn_ok, 1)

                NB = H_B * NT

                def scores(s, qi):
                    return ps[:, s, 0:P] if qi == 0 else ps[:, s:s + 2, 0:TH]

                def top(s, qi, c):
                    return dve.tensor_reduce(aneg[:, c:c + 1], scores(s, qi), AX.X if qi == 0 else AX.XY, ALU.max, negate=True)

                def mask_queries(h):
                    if h >= 2:
                        dve.wait_ge(b_sc, 2 * NT * (h - 1))
                    for j in range(2):
                        r = 2 * h + j
                        last = dve.tensor_scalar(qm[h % 2][j][:, :], qbT[:, r // 4, :], grp[:, r % 4:r % 4 + 1], DH_B ** -0.5, ALU.mult, ALU.mult)
                    last.then_inc(b_qm, 1)

                mask_queries(0)
                for n in range(NB + 4):
                    h, qi = n // NT, n % NT
                    if n >= 4:
                        m = n - 4
                        dve.wait_ge(b_pv, m + 1)
                        c0 = WA + (m // NT) * DV_B
                        dve.tensor_scalar(omix[:, m % NT, c0:c0 + DV_B], ps[:, 6, 0:DV_B],
                                          arec[:, 2 * (m % 4):2 * (m % 4) + 1], None, ALU.mult).then_inc(b_o, 1)
                    if n < NB:
                        for j in range(2):
                            dve.wait_ge(b_sc, 2 * n + j + 1)
                            top(2 * j, qi, 2 * (n % 2) + j).then_inc(b_neg, 1)
                    if n == 0:
                        gla_gate()
                    if qi == 2 and h < H_B - 1:
                        mask_queries(h + 1)
                    if 1 <= n <= NB:
                        m = n - 1
                        w = P if m % NT == 0 else T
                        c, r = 2 * (m % 2), 2 * (m % 4)
                        dve.wait_ge(b_exp, 2 * m + 2)
                        link(dve.reciprocal(arec[:, r:r + 2], asum[:, c:c + 2]))
                        link(dve.scalar_tensor_tensor(out=ratio[:, m % 2:m % 2 + 1], in0=asum[:, c:c + 1], scalar=arec[:, r + 1:r + 2], in1=nlam,
                                                      op0=ALU.mult, op1=ALU.mult))
                        dve.scalar_tensor_tensor(out=p0[m % 3][:, 0:w], in0=p1[m % 2][:, 0:w], scalar=ratio[:, m % 2:m % 2 + 1], in1=p0[m % 3][:, 0:w],
                                                 op0=ALU.mult, op1=ALU.add).then_inc(b_a, 1)
                dve.wait_ge(ap_ev, 6)
                rope(krT[:, TC + PAST:NKEY], rota[0:DR, :], cosT[0:DR, :], sinT[0:DR, :], link).then_inc(ap_kr, 1)
                dve.wait_ge(ap_kr, 1)

                for kt in kA:
                    dve.tensor_copy(kt[DN:DQ, :], krT[:, :])

                def head_ready(h):
                    dve.wait_ge(x_ev, 4 * h + 2)
                    rope(qA[h % 2][DN:DQ, TC:T], rota[DN:DQ, :], cosT[DN:DQ, :], sinT[DN:DQ, :], link).then_inc(a_qk, 1)

                head_ready(0)
                NA = H_A * NT
                oa, ob = omix[:, :, 0:WA], omix[:, :, WA:WA + WB]
                for n in range(NA + 4):
                    h, qi = n // NT, n % NT
                    if n >= 4:
                        m = n - 4
                        dve.wait_ge(a_pv, m + 1)
                        dve.tensor_scalar(omix[:, m % NT, (m // NT) * DV_A:(m // NT + 1) * DV_A], ps[:, 6, 0:DV_A],
                                          arec[:, m % 4:m % 4 + 1], None, ALU.mult).then_inc(a_o, 1)
                    if n < NA:
                        dve.wait_ge(a_sc, n + 1)
                        top(2 * (n % 2), qi, n % 2).then_inc(a_neg, 1)
                    if 1 <= n <= NA:
                        m = n - 1
                        dve.wait_ge(a_exp, m + 1)
                        link(dve.reciprocal(arec[:, m % 4:m % 4 + 1], asum[:, m % 2:m % 2 + 1]))
                    if qi == 2 and h < H_A - 1:
                        head_ready(h + 1)
                    if n == NT:
                        link(dve.tensor_tensor(bsq[:, :, :], ob, ob, ALU.mult))
                        dve.tensor_reduce(css.rearrange("p (t h) -> p t h", h=H_B), bsq[:, :, :].rearrange("p t (h v) -> p t h v", h=H_B), AX.X, ALU.add).then_inc(on_v, 1)
                    if n == NT + 3:
                        dve.wait_ge(on_s, 1)
                        link(dve.reciprocal(css, crs))
                        obh = ob.rearrange("p t (h v) -> p t h v", h=H_B)
                        dve.tensor_tensor(obh, obh, css.rearrange("p (t h) -> p t h", h=H_B).unsqueeze(3).broadcast_to([P, NT, H_B, DV_B]), ALU.mult).then_inc(on_ok, 1)
                    if n == NA - 1:
                        w = WA - DV_A
                        dve.wait_ge(a_o, NA - NT)
                        link(dve.tensor_tensor(asq[:, :, 0:w], oa[:, :, 0:w], oa[:, :, 0:w], ALU.mult))
                        link(dve.tensor_reduce(ss10[:, 0:NT], asq[:, :, 0:w], AX.X, ALU.add))
                dve.wait_ge(a_o, NA)
                w = slice(WA - DV_A, WA)
                link(dve.tensor_tensor(asq[:, :, w], oa[:, :, w], oa[:, :, w], ALU.mult))
                link(dve.tensor_reduce(ss10[:, NT:2 * NT], asq[:, :, w], AX.X, ALU.add))
                dve.tensor_tensor(ss10[:, 0:NT], ss10[:, 0:NT], ss10[:, NT:2 * NT], ALU.add).then_inc(on_v, 1)
                dve.wait_ge(on_s, 2)
                link(dve.reciprocal(ss10[:, 0:NT], rs10[:, 0:NT]))
                for k in range(WA // P):
                    o = omix[:, :, k * P:(k + 1) * P]
                    dve.tensor_tensor(o, o, ss10[:, 0:NT].unsqueeze(2).broadcast_to([P, NT, P]), ALU.mult).then_inc(on_ok, 1)
                for n, k in enumerate(K_ORDER):
                    dve.wait_ge(ot_hi, n + 1)
                    b = 2 * (n % 4) * 512
                    dve.scalar_tensor_tensor(out=u_lo[:, k, :], in0=psf[:, b:b + T], scalar=parT[:, R_OG + k:R_OG + k + 1], in1=cv(u_hi[:, k, :]),
                                             op0=ALU.mult, op1=ALU.subtract).then_inc(ot_lo, 1)
                for n in range(NW2):
                    g = G_WOUT + n
                    dve.wait_ge(mm_ok, g + 1)
                    for m2 in range(2):
                        update_x(1, 4 * (g % 2) + 2 * m2, 2 * n + m2).then_inc(x_upd, 1)
                    for m in (2 * n, 2 * n + 1):
                        add_square(m, n_sq, n_sqd, KD + m)
                    lo(g + 2)
                norm(2)
                ffn(1, G_FFN2, NF, 2, (len(PARTS) + 1) * KD)
                dve.drain().then_inc(l_done, 1)
                dve.wait_ge(s_go, l + 1)
            steps[0] = 0
            inverse_rms(f_std, f_dg, f_bc, 1)
            for m in range(KD):
                if m >= 2:
                    dve.wait_ge(s_yt, m - 1)
                dve.tensor_tensor(xn[:, m % 2, :], xT[:, m, :], rstd[:, :], ALU.mult).then_inc(f_xn, 1)

        @block.tensor
        def _(pe):
            def up_banks(g):
                return 4 * (g % 2)

            def fm(g, step, src, nk, per_k, n_out=2, width=P, ks=None):
                b = up_banks(g)
                wh = w_hi[:, g % 2, :].rearrange("p (k n) -> p k n", k=KD)
                wl = w_lo[:, g % 2, :].rearrange("p (k n) -> p k n", k=KD)
                xh, xl = src
                pe.wait_ge(lo_ok, g + 1 + step)
                ks = ks or list(range(nk))
                for o in range(n_out):
                    for k in ks:
                        if o == 0 and per_k is not None:
                            per_k(k)
                        for half in range(2):
                            t = slice(half * TH, (half + 1) * TH)
                            out = ps[0:width, b + 2 * o + half, 0:TH]
                            c = slice(o * P, o * P + width)
                            pe.matmul(out, wh[:, k, c], xh[:, k, t], start=k == ks[0], stop=False)
                            pe.matmul(out, wh[:, k, c], xl[:, k, t], start=False, stop=False)
                            last = pe.matmul(out, wl[:, k, c], xh[:, k, t], start=False, stop=k == ks[-1])
                last.then_inc(mm_ok, 1)

            def fm_pair(g, src, per_k, shapes):
                xh, xl = src
                pe.wait_ge(lo_ok, g + 2)
                for step in range(KD + LAG):
                    for c in range(2):
                        k = step - LAG * c
                        if not 0 <= k < KD:
                            continue
                        if c == 0:
                            per_k(k)
                        n_out, width = shapes[c]
                        wh = w_hi[:, (g + c) % 2, :].rearrange("p (k n) -> p k n", k=KD)
                        wl = w_lo[:, (g + c) % 2, :].rearrange("p (k n) -> p k n", k=KD)
                        for o in range(n_out):
                            for half in range(2):
                                t = slice(half * TH, (half + 1) * TH)
                                out = ps[0:width, up_banks(g + c) + 2 * o + half, 0:TH]
                                w = slice(o * P, o * P + width)
                                pe.matmul(out, wh[:, k, w], xh[:, k, t], start=k == 0, stop=False)
                                pe.matmul(out, wh[:, k, w], xl[:, k, t], start=False, stop=False)
                                last = pe.matmul(out, wl[:, k, w], xh[:, k, t], start=False, stop=k == KD - 1)
                        if k == KD - 1:
                            last.then_inc(mm_ok, 1)

            def tmaj(g):
                b = up_banks(g)
                wh = w_hi[:, g % 2, :].rearrange("p (k n) -> p k n", k=KD)
                wl = w_lo[:, g % 2, :].rearrange("p (k n) -> p k n", k=KD)
                pe.wait_ge(lo_ok, g + 1)
                for t in range(NT):
                    out = psf[:, b * 512 + t * CW:b * 512 + (t + 1) * CW]
                    c = slice(t * P, (t + 1) * P)
                    for k in range(KD):
                        pe.matmul(out, u_hi[:, k, c], wh[:, k, :], start=k == 0, stop=False)
                        pe.matmul(out, u_lo[:, k, c], wh[:, k, :], start=False, stop=False)
                        last = pe.matmul(out, u_hi[:, k, c], wl[:, k, :], start=False, stop=k == KD - 1)
                last.then_inc(mm_ok, 1)

            def sums(summed, diagonal, spread, v):
                for t in range(NT):
                    last = pe.matmul(ps[:, 0, 2 * t:2 * t + 2], sqsum[:, t * P:(t + 1) * P], ones[:, 0:2], start=True, stop=True)
                last.then_inc(summed, 1)
                pe.wait_ge(diagonal, v)
                dgf = dg[:, :, :].rearrange("p t n -> p (t n)")
                for half in range(2):
                    last = pe.matmul(ps[:, half, 0:TH], ones[:, :], dgf[:, half * TH:(half + 1) * TH], start=True, stop=True)
                last.then_inc(spread, 1)

            def u_tile(n):
                return lambda k: pe.wait_ge(n_ulo, n * KD + k + 1)

            def mod_under(f, g, i=0):
                c = (g - (G_FFN1, G_FFN2)[f]) - G_MOD
                v = c + V0[f]
                s = g % 2
                b = up_banks(g) + 2
                if 0 <= c < N_UNDER[f]:
                    pe.wait_ge(v_in[s], i * 16 + 16 * (v // 2 + 1))
                    for half in range(2):
                        for kk in range(2):
                            for j in range(4):
                                k = j + 4 * kk
                                last = pe.matmul(ps[32 * j:32 * j + 32, b + half, TH:TH + P], csp[:, k, :], uraw[:, s, k, half * P:(half + 1) * P],
                                                 start=kk == 0, stop=kk == 1)
                    last.then_inc(v_mm, 1)
                if 2 <= c < N_UNDER[f] + 2:
                    pe.wait_ge(v_row, i * 2 + (v - 1))
                    for r in range(2):
                        pe.matmul(ps[:, b, TH + P + 2 * r:TH + P + 2 * r + 2], urows[:, s, r * P:(r + 1) * P], comb[:, :], start=True, stop=True)

            def ffn(f, g, up0, x0, n):
                for q, cnt in enumerate(PARTS):
                    def up_step(j, i):
                        mod_under(f, g + j, i)
                        fm(g + j, i * 2, (u_hi, u_lo), KD, None)

                    start = 0
                    if q == 0:
                        fm_pair(g, (u_hi, u_lo), u_tile(n), [(2, P), (2, P)])
                        for j in range(2, 4):
                            pe.wait_ge(h32_ok, up0 + j - 1)
                            up_step(j, 0)
                        start = 4
                    with pe.Fori(0, (cnt - start) // 2) as i:
                        for j in range(start, start + 2):
                            if q > 0:
                                pe.wait_ge(x_upd, x0 + q * KD - 2 * (1 - j))
                            pe.wait_ge(h32_ok, up0 + j - 1 + i * 2)
                            up_step(j, i)
                    g += cnt
                    up0 += cnt
                    for j in range(NW2):
                        if j < 2:
                            pe.wait_ge(h32_ok, up0 - 1 + j)
                        else:
                            pe.wait_ge(x_upd, x0 + q * KD + 2 * j - 2)
                        mod_under(f, g + j)
                        fm(g + j, 0, (h_hi, h_lo), cnt, None if j else lambda k: pe.wait_ge(hlo_ok, up0 - cnt + k + 1))
                    g += NW2

            pe.wait_ge(s_const, 26)
            pe.wait_ge(s_tab, 64)
            pe.transpose(ps[:, 0, 0:2 * KD], par[0:2 * KD, :], ident[0:2 * KD, 0:2 * KD]).then_inc(s_ctp, 1)
            pe.wait_ge(s_csil, 1)
            pe.wait_ge(s_xs, 32)
            for m in range(KD):
                if m >= 4:
                    pe.wait_ge((s_xa, s_xv)[m % 2], (m - 4) // 2 + 1)
                b = 2 * (m % 4) * 512
                for t in range(NT):
                    last = pe.transpose(psf[:, b + t * P:b + (t + 1) * P], xs[:, t, m * P:(m + 1) * P], ident[:, :])
                last.then_inc(s_xtp, 1)
            pe.wait_ge(s_const, 27)
            pe.wait_ge(s_xa, KD // 2)
            pe.wait_ge(s_xv, KD // 2)

            for c in range(NMC):
                if c == NMC - 1:
                    pe.wait_ge(par_in, 16 * names["n_par"])
                    pe.transpose(ps[:, 4 + c, P:2 * P], par[:, :], ident[:, :]).then_inc(s_ptp, 1)
                pe.wait_ge(m_raw[c], 16)
                for kk in range(2):
                    for j in range(4):
                        k = j + 4 * kk
                        last = pe.matmul(ps[32 * j:32 * j + 32, c, :], csp[:, k, :], mraw[c][:, k, :], start=kk == 0, stop=kk == 1)
                last.then_inc(m_mm, 1)
                pe.wait_ge(m_row, c + 1)
                if c == NMC - 1:
                    pe.wait_ge(s_par, 1)
                for r in range(MW // P):
                    last = pe.matmul(ps[:, 4 + c, 2 * r:2 * r + 2], mrows[:, c, r * P:(r + 1) * P], comb[:, :], start=True, stop=True)
                last.then_inc(m_tp, 1)
            pe.wait_ge(s_gain, 1)

            with pe.Fori(0, DEPTH) as l:
                sums(n_ss, n_dg, n_bc, 1)
                ffn(0, G_FFN1, 0, 0, 0)
                pe.wait_ge(n_sqd, KD)
                sums(n_ss, n_dg, n_bc, 2)
                def gate_products(d, b):
                    for p in range(2):
                        for half in range(2):
                            last = pe.matmul(ps[:, b + 2 * p + half, 0:TH], wgp[:, d, p * P:(p + 1) * P], glT[:, half * TH:(half + 1) * TH], start=True, stop=True)
                    last.then_inc(g_z, 1)

                for n, name in enumerate(PROJ):
                    g = G_PROJ + n
                    if n >= 2:
                        pe.wait_ge(ev_ok, n - 1)
                    if n == Z_AT + 1:
                        gate_products(0, up_banks(g))
                        pe.wait_ge(g_min, 1)
                    if n == 0:
                        fm_pair(g, (u_hi, u_lo), u_tile(1), [(1, 2 * GR), (2, P)])
                    elif n == 1:
                        continue
                    elif name in ("qc", "kc", "qb"):
                        fm(g, 0, (u_hi, u_lo), KD, None)
                    else:
                        tmaj(g)
                pe.wait_ge(ev_ok, len(PROJ) - 1)
                gate_products(1, 0)
                pe.wait_ge(ev_ok, len(PROJ))
                for d in range(2):
                    pe.wait_ge(g_kd, d + 1)
                    if d == 1:
                        pe.wait_ge(g_oev, NT)
                    for t in range(NT):
                        if d * NT + t >= 2:
                            pe.wait_ge(g_tev, d * NT + t - 1)
                        for a in range(2):
                            last = pe.transpose(ps[:, 4 + t % 2, a * P:(a + 1) * P], gkd[d][:, a, t * P:(t + 1) * P], ident[:, :])
                        last.then_inc(g_tp, 1)
                    if d == 0:
                        pe.wait_ge(kv_in, (l + 1) * 32)
                        for m in range(2):
                            last = pe.transpose(ps[:, 6, m * P:(m + 1) * P], ck[:, m * P:(m + 1) * P], ident[:, :])
                        last.then_inc(bk_tp, 1)
                        for m in range(2):
                            last = pe.transpose(ps[:, 7, m * P:(m + 1) * P], kbT[:, m, 0:TC], ident[:, :])
                        last.then_inc(bk_tp, 1)
                        pe.wait_ge(bk_ev, 2)
                    for n, c in enumerate(U_ORDER[d]):
                        pe.wait_ge(g_tev, d * NT + c // 2 + 1)
                        if d * N_STATE + n >= 2:
                            pe.wait_ge(g_s, d * N_STATE + n - 1)
                        r = slice(CH * (c % 2), CH * (c % 2) + CH)
                        for h in range(H_C):
                            hh, a = h % 2, h // 2
                            last = pe.matmul(ps[HW * hh:HW * hh + HW, 6 + n % 2, a * DV_C:(a + 1) * DV_C],
                                             kdt[r, c // 2, a, HW * hh:HW * hh + HW], vcs[r, c // 2, h * DV_C:(h + 1) * DV_C], start=True, stop=True)
                        last.then_inc(g_u, 1)
                    if d == 0:
                        pe.wait_ge(g_min, 2)
                    pe.wait_ge(g_ke, d + 1)

                    def intra_scores(n):
                        t = O_ORDER[d][n]
                        if d * NT + n >= 2:
                            pe.wait_ge(g_am, d * NT + n - 1)
                        ts = slice(t * P, (t + 1) * P)
                        for h in range(H_C):
                            rows = slice(HW * (h % 2), HW * (h % 2) + DK)
                            last = pe.matmul(ps[:, 2 * (n % 2) + h % 2, (h // 2) * P:(h // 2 + 1) * P], gke[d][rows, h // 2, ts], gqe[d][rows, h // 2, ts], start=True, stop=True)
                        last.then_inc(g_at, 1)

                    intra_scores(0)
                    for n, t in enumerate(O_ORDER[d]):
                        if n + 1 < NT:
                            intra_scores(n + 1)
                        pe.wait_ge(g_am, d * NT + n + 1)
                        if n >= 1:
                            pe.wait_ge(g_oev, d * NT + n)
                        for c in (2 * t, 2 * t + 1):
                            if state_count(d, c):
                                pe.wait_ge(g_s, d * N_STATE + state_count(d, c))
                        for h in range(H_C):
                            rows = slice(HW * (h % 2), HW * (h % 2) + DK)
                            bank, cols = 4 + h % 2, slice((h // 2) * DV_C, (h // 2 + 1) * DV_C)
                            ha = 2 * (h % 2) + h // 2
                            last = pe.matmul(ps[:, bank, cols], am[:, n % 2, ha * P:(ha + 1) * P], vcs[:, t, h * DV_C:(h + 1) * DV_C], start=True, stop=False, skip_group_check=True)
                            for c in (2 * t, 2 * t + 1):
                                if has_state(d, c):
                                    q0 = CH * (c % 2)
                                    last = pe.matmul(ps[q0:q0 + CH, bank, cols], gqe[d][rows, h // 2, c * CH:(c + 1) * CH],
                                                     entering(d, c)[rows, h // 2, :], start=False, stop=True, skip_group_check=True)
                        last.then_inc(g_o, 1)
                NB = H_B * NT
                pe.wait_ge(g_oev, 2 * NT)
                pe.wait_ge(g_s, 2 * N_STATE)

                def score(s, q, kt, qi, s_sc):
                    if qi == 0:
                        last = pe.matmul(ps[:, s, 0:P], q, kt[:, 0:TC], start=True, stop=True)
                    else:
                        for half in range(2):
                            k0 = TC + half * TH
                            last = pe.matmul(ps[:, s + half, 0:TH], q, kt[:, k0:k0 + TH], start=True, stop=True)
                    last.then_inc(s_sc, 1)

                def turn(m, prob, s_tp, s_pt):
                    nk = 1 if m % NT == 0 else NT
                    if m >= 1:
                        pe.wait_ge(s_pt, m)
                    for k in range(nk):
                        last = pe.transpose(psf[:, 4 * 512 + k * P:4 * 512 + (k + 1) * P], prob[:, k * P:(k + 1) * P], ident[:, :])
                    last.then_inc(s_tp, 1)

                def values(m, s_pt, s_pv, s_o, v, c0):
                    nk = 1 if m % NT == 0 else NT
                    pe.wait_ge(s_pt, m + 1)
                    if m >= 1:
                        pe.wait_ge(s_o, m)
                    v0 = keys_of(m % NT)[0]
                    for k in range(nk):
                        last = pe.matmul(ps[:, 6, 0:96], pt[m % 2][:, k, :], v[:, v0 + k, c0:c0 + 96], start=k == 0, stop=k == nk - 1)
                    last.then_inc(s_pv, 1)

                pe.wait_ge(pool_c, 1)
                for n in range(NB + 3):
                    h, qi = n // NT, n % NT

                    def softmax_scores(j):
                        r = 2 * h + j
                        if n >= 1:
                            pe.wait_ge(b_exp, 2 * (n - 1) + j + 1)
                        score(2 * j, qm[h % 2][j][:, qi * P:(qi + 1) * P], kbT[:, r // 4, :], qi, b_sc)

                    if n < NB:
                        if qi == 0:
                            pe.wait_ge(b_qm, h + 1)
                        softmax_scores(0)
                        softmax_scores(1)
                    if n >= 3:
                        values(n - 3, b_pt, b_pv, b_o, vbs, ((n - 3) // NT) * DV_B)
                    if 2 <= n <= NB + 1:
                        pe.wait_ge(b_a, n - 1)
                        turn(n - 2, p0[(n - 2) % 3], b_tp, b_pt)
                pe.wait_ge(aw_in, (l + 1) * (16 * 5))
                pe.wait_ge(b_o, NB)
                pe.wait_ge(cq_ok, 1)
                for s in range(6):
                    if s >= 4:
                        pe.wait_ge(ap_ev, s - 3)
                    b = 2 * (s % 4) * 512
                    w = (DR if s == 5 else P)
                    c0 = (s * P if s < 3 else Q_RANK + (s - 3) * P if s < 5 else 640)
                    tiles = [cqkv[:, t, c0:c0 + w] for t in range(NT)]
                    if s in (3, 4):
                        tiles.insert(1, cc[:, (s - 3) * P:(s - 2) * P])
                    if s == 5:
                        tiles.insert(1, cck[:, :])
                    for t, src in enumerate(tiles):
                        last = pe.transpose(psf[0:w, b + t * P:b + (t + 1) * P], src, ident[:, :])
                    last.then_inc(ap_tp, 1)
                pe.wait_ge(ap_ev, 6)
                for t in range(NKT):
                    for k in range(2):
                        last = pe.matmul(ps[:, t, 0:WA], ckvT[:, k, t * P:(t + 1) * P], wuv[:, k, :], start=k == 0, stop=k == 1)
                    last.then_inc(ap_tp, 1)

                def head_piece(r):
                    h, k = r // 4, r % 4
                    if r >= 1:
                        pe.wait_ge(x_ev, r)
                    if k < 2:
                        for c in range(3):
                            last = pe.matmul(ps[0:DQ, 7, 0:TH], wuq[:, c, h * DQ:(h + 1) * DQ], cqT[:, c, k * TH:(k + 1) * TH], start=c == 0, stop=c == 2)
                    else:
                        c0 = (k - 2) * (NKEY // 2)
                        for c in range(2):
                            last = pe.matmul(ps[0:DN, 7, 0:NKEY // 2], wuk[:, c, h * DN:(h + 1) * DN], ckvT[:, c, c0:c0 + NKEY // 2], start=c == 0, stop=c == 1)
                    last.then_inc(x_mm, 1)

                for r in range(4):
                    head_piece(r)
                NA = H_A * NT
                pe.wait_ge(ap_ev, 6 + NKT)
                pe.wait_ge(pool_c, 2)
                for n in range(NA + 3):
                    h, qi = n // NT, n % NT
                    if n < NA:
                        if qi == 0:
                            pe.wait_ge(a_qk, h + 1)
                            pe.wait_ge(x_ev, 4 * h + 4)
                        if n >= 2:
                            pe.wait_ge(a_exp, n - 1)
                        score(2 * (n % 2), qA[h % 2][0:DQ, qi * P:(qi + 1) * P], kA[h % 2][0:DQ, :], qi, a_sc)
                    if n >= 3:
                        values(n - 3, a_pt, a_pv, a_o, vas, ((n - 3) // NT) * DV_A)
                    if 2 <= n <= NA + 1:
                        pe.wait_ge(a_exp, n - 1)
                        turn(n - 2, pa[(n - 2) % 3], a_tp, a_pt)
                    if qi < 4 and h < H_A - 1:
                        head_piece(4 * (h + 1) + qi)
                for n, k in enumerate(K_ORDER):
                    pe.wait_ge(on_ok, 1 if k >= WA // P else k + 2)
                    if n == 3:
                        pe.wait_ge(a_o, NA)
                    if n >= 4:
                        pe.wait_ge(ot_lo, n - 3)
                    b = 2 * (n % 4) * 512
                    for t in range(NT):
                        last = pe.transpose(psf[:, b + t * P:b + (t + 1) * P], omix[:, t, k * P:(k + 1) * P], ident[:, :])
                    last.then_inc(ot_tp, 1)
                pe.wait_ge(ot_lo, 6)
                for n in range(NW2):
                    g = G_WOUT + n
                    if n == 1:
                        pe.wait_ge(ot_lo, KD)
                    if n >= 2:
                        pe.wait_ge(x_upd, 3 * KD + 2 * (n - 1))
                    fm(g, 0, (u_hi, u_lo), KD, None if n else lambda k: pe.wait_ge(ot_lo, K_ORDER.index(k) + 1), ks=K_ORDER)
                pe.wait_ge(n_sqd, 2 * KD)
                sums(n_ss, n_dg, n_bc, 3)
                pe.wait_ge(par_in, (l + 2) * (16 * names["n_par"]))
                pe.transpose(ps[:, 7, TH:TH + P], par[:, :], ident[:, :])
                ffn(1, G_FFN2, NF, 4 * KD, 2)
                pe.drain().then_inc(l_done, 1)
                pe.wait_ge(s_go, l + 1)
            sums(f_ss, f_dg, f_bc, 1)
            pe.wait_ge(s_yt, KD)
            for t in range(NT):
                if t >= 4:
                    pe.wait_ge(s_ytm, t - 3)
                b = 2 * (t % 4) * 512
                for k in range(KD):
                    last = pe.transpose(psf[:, b + k * P:b + (k + 1) * P], yT[:, k, t * P:(t + 1) * P], ident[:, :])
                last.then_inc(s_ytp, 1)


def rope_tables():
    inv = (10000.0 ** (-np.arange(0, 16, 2, dtype=np.float32) / np.float32(16))).astype(np.float32)
    tok = np.arange(TL)
    cos, sin = np.zeros((32, TL), np.float32), np.zeros((32, TL), np.float32)
    for i in range(32):
        pos = (tok // GRID_W if i < 16 else tok % GRID_W).astype(np.float32)
        ang = pos * inv[i % 8]
        cos[i] = np.cos(ang)
        sin[i] = np.sin(ang) * (-1.0 if i % 16 < 8 else 1.0)
    return np.tile(cos, (4, 1)), np.tile(sin, (4, 1))


def layer_constants():
    lam = [0.8 - 0.6 * math.exp(-0.3 * l) for l in range(DEPTH)]
    return np.ascontiguousarray(np.broadcast_to(np.array([[x, 1.0 - x] for x in lam], np.float32)[:, None, :], (DEPTH, P, 2)))


OUTS = {
    "y_prompt": (1, TC, D), "y_sample": (1, TL, D),
    "new_mla_ckv": (1, DEPTH, TC, KV_RANK), "new_mla_krope": (1, DEPTH, TC, DR),
    "new_diff_k": (1, DEPTH, TC, H_B, 2 * DH_B), "new_diff_v": (1, DEPTH, TC, H_B, DV_B),
    "new_gla_fwd": (1, DEPTH, H_C, DK, DV_C), "new_gla_bwd": (1, DEPTH, H_C, DK, DV_C),
}


def kernel(**inputs):
    import concourse.bacc as bacc
    from concourse.bass_utils import run_bass_kernel_spmd

    nc = bacc.Bacc("TRN2", target_bir_lowering=False, num_devices=1)
    arrays = {name: np.ascontiguousarray(a) for name, a in inputs.items()}
    arrays["rope_cos"], arrays["rope_sin"] = rope_tables()
    arrays["layer_consts"] = layer_constants()
    A = {n: nc.dram_tensor(f"in_{n}", a.shape, mybir.dt.from_np(a.dtype), kind="ExternalInput").ap() for n, a in arrays.items()}
    O = {n: nc.dram_tensor(f"out_{n}", s, F32, kind="ExternalOutput").ap() for n, s in OUTS.items()}
    build(nc, A, O)
    r = run_bass_kernel_spmd(nc, [{f"in_{n}": a for n, a in arrays.items()}], core_ids=[0])
    return tuple(r.results[0][f"out_{n}"] for n in OUTS)
```
